# Optimizing a Trainium2 kernel written in Bass

```python
import math
import jax, jax.numpy as jnp
from jax import lax
import numpy as np

D_MODEL = 1024
BATCH = 1
SEQ = 1024
DEPTH = 1

D_MIX = D_MODEL
D_SSM = D_MIX // 2
SSM_GROUP = 16
N_SSM_GROUPS = D_SSM // SSM_GROUP
SSM_STATE = 64
N_DIR = 2
DT_MIN = 1e-3
DT_MAX = 1e-1
N_HEADS = 8
QK_NOPE_DIM = 64
QK_ROPE_DIM = 32
V_HEAD_DIM = 64
D_ATTN = N_HEADS * V_HEAD_DIM
Q_LORA_RANK = 256
KV_LORA_RANK = 128
ROPE_THETA = 10000.0
Q_BLOCK = 128
D_IN = D_SSM + Q_LORA_RANK + KV_LORA_RANK + QK_ROPE_DIM
N_EXPERTS = 64
TOP_K = 6
N_EXPERT_GROUPS = 8
TOPK_GROUPS = 4
D_EXPERT = 256
N_SHARED = 1
ROUTED_SCALE = 2.5
EXPERT_BLOCK = 128
DEEPNORM_ALPHA = (2 * DEPTH) ** 0.25
DEEPNORM_BETA = (8 * DEPTH) ** -0.25
LN_EPS = 1e-5
RMS_EPS = 1e-6

kernel_name = "hybrid_s5_mla_moe_deepnorm_encoder"

def _layer_norm(x, g, b):
    xf = x.astype(jnp.float32)
    mu = jnp.mean(xf, axis=-1, keepdims=True)
    xc = xf - mu
    var = jnp.mean(xc * xc, axis=-1, keepdims=True)
    return xc * lax.rsqrt(var + LN_EPS) * g.astype(jnp.float32) + b.astype(jnp.float32)

def _rms_norm(x, g):
    xf = x.astype(jnp.float32)
    y = xf * lax.rsqrt(jnp.mean(xf * xf, axis=-1, keepdims=True) + RMS_EPS) * g.astype(jnp.float32)
    return y.astype(x.dtype)

def _rope(t, cos, sin):
    half = t.shape[-1] // 2
    t1, t2 = t[..., :half], t[..., half:]
    cos = cos.astype(t.dtype)
    sin = sin.astype(t.dtype)
    return jnp.concatenate([t1 * cos - t2 * sin, t1 * sin + t2 * cos], axis=-1)

def _ssm_combine(ei, ej):
    ai_r, ai_i, bi_r, bi_i = ei
    aj_r, aj_i, bj_r, bj_i = ej
    a_r = aj_r * ai_r - aj_i * ai_i
    a_i = aj_r * ai_i + aj_i * ai_r
    b_r = aj_r * bi_r - aj_i * bi_i + bj_r
    b_i = aj_r * bi_i + aj_i * bi_r + bj_i
    return a_r, a_i, b_r, b_i

def _s5_bidirectional(u, lam_re, lam_im, log_dt, b_re, b_im, c_re, c_im, d_skip):
    bsz, seq, _ = u.shape
    uf = u.astype(jnp.float32)
    ul = uf.reshape(bsz, seq, N_SSM_GROUPS, SSM_GROUP).transpose(1, 0, 2, 3)
    y = jnp.zeros_like(ul)
    for d in range(N_DIR):
        lr = jnp.minimum(lam_re[d].astype(jnp.float32), -1e-4)
        li = lam_im[d].astype(jnp.float32)
        dt = jnp.exp(log_dt[d].astype(jnp.float32))[:, None]
        mag = jnp.exp(lr * dt)
        ar = mag * jnp.cos(li * dt)
        ai = mag * jnp.sin(li * dt)
        den = lr * lr + li * li
        kr = ((ar - 1.0) * lr + ai * li) / den
        ki = (ai * lr - (ar - 1.0) * li) / den
        br = b_re[d].astype(jnp.float32)
        bi = b_im[d].astype(jnp.float32)
        bbr = kr[..., None] * br - ki[..., None] * bi
        bbi = kr[..., None] * bi + ki[..., None] * br
        bu_r = jnp.einsum('lbgp,gnp->lbgn', ul, bbr)
        bu_i = jnp.einsum('lbgp,gnp->lbgn', ul, bbi)
        a_r = jnp.broadcast_to(ar[None, None], (seq, 1) + ar.shape)
        a_i = jnp.broadcast_to(ai[None, None], (seq, 1) + ai.shape)
        _, _, h_r, h_i = lax.associative_scan(
            _ssm_combine, (a_r, a_i, bu_r, bu_i), reverse=(d == 1), axis=0)
        y = y + jnp.einsum('lbgn,gpn->lbgp', h_r, c_re[d].astype(jnp.float32)) \
              - jnp.einsum('lbgn,gpn->lbgp', h_i, c_im[d].astype(jnp.float32))
    y = y.transpose(1, 0, 2, 3).reshape(bsz, seq, D_SSM) + uf * d_skip.astype(jnp.float32)
    return y.astype(u.dtype)

def _mla(c_q, ckv_rope, q_norm_g, w_uq, kv_norm_g, w_ukv, cos, sin):
    bsz, seq, _ = c_q.shape
    q = (_rms_norm(c_q, q_norm_g) @ w_uq).reshape(bsz, seq, N_HEADS, QK_NOPE_DIM + QK_ROPE_DIM)
    q_nope = q[..., :QK_NOPE_DIM]
    q_rope = _rope(q[..., QK_NOPE_DIM:], cos[None, :, None, :], sin[None, :, None, :])
    ckv = _rms_norm(ckv_rope[..., :KV_LORA_RANK], kv_norm_g)
    k_rope = _rope(ckv_rope[..., KV_LORA_RANK:], cos[None], sin[None])
    kv = (ckv @ w_ukv).reshape(bsz, seq, N_HEADS, QK_NOPE_DIM + V_HEAD_DIM)
    k_nope = kv[..., :QK_NOPE_DIM]
    v = kv[..., QK_NOPE_DIM:]
    scale = (QK_NOPE_DIM + QK_ROPE_DIM) ** -0.5
    n_blk = seq // Q_BLOCK
    qn_blocks = q_nope.reshape(bsz, n_blk, Q_BLOCK, N_HEADS, QK_NOPE_DIM).transpose(1, 0, 2, 3, 4)
    qr_blocks = q_rope.reshape(bsz, n_blk, Q_BLOCK, N_HEADS, QK_ROPE_DIM).transpose(1, 0, 2, 3, 4)

    def attend(blk):
        qn, qr = blk
        s = (jnp.einsum('bqhd,bkhd->bhqk', qn, k_nope)
             + jnp.einsum('bqhr,bkr->bhqk', qr, k_rope)).astype(jnp.float32) * scale
        p = jax.nn.softmax(s, axis=-1).astype(v.dtype)
        return jnp.einsum('bhqk,bkhd->bqhd', p, v)

    o = lax.map(attend, (qn_blocks, qr_blocks))
    return o.transpose(1, 0, 2, 3, 4).reshape(bsz, seq, D_ATTN)

def _moe(x, w_router, router_bias, we_gate, we_up, we_down, ws_gate, ws_up, ws_down):
    bsz, seq, dm = x.shape
    xt = x.reshape(-1, dm)
    n_tok = xt.shape[0]
    scores = jax.nn.sigmoid((xt @ w_router).astype(jnp.float32))
    choice = scores + router_bias.astype(jnp.float32)
    grp = choice.reshape(n_tok, N_EXPERT_GROUPS, N_EXPERTS // N_EXPERT_GROUPS)
    grp_score = lax.top_k(grp, 2)[0].sum(-1)
    top_grp = lax.top_k(grp_score, TOPK_GROUPS)[1]
    grp_mask = jax.nn.one_hot(top_grp, N_EXPERT_GROUPS, dtype=jnp.float32).sum(1) > 0
    exp_mask = jnp.repeat(grp_mask, N_EXPERTS // N_EXPERT_GROUPS, axis=1)
    _, top_idx = lax.top_k(jnp.where(exp_mask, choice, -jnp.inf), TOP_K)
    top_w = jnp.take_along_axis(scores, top_idx, axis=1)
    top_w = top_w / (top_w.sum(-1, keepdims=True) + 1e-20) * ROUTED_SCALE

    n_assign = n_tok * TOP_K
    n_blocks = -(-n_assign // EXPERT_BLOCK) + N_EXPERTS
    n_rows = n_blocks * EXPERT_BLOCK
    flat_e = top_idx.reshape(-1).astype(jnp.int32)
    flat_tok = jnp.arange(n_assign, dtype=jnp.int32) // TOP_K
    flat_w = top_w.reshape(-1)
    order = jnp.argsort(flat_e)
    sorted_e = flat_e[order]
    counts = jnp.bincount(flat_e, length=N_EXPERTS).astype(jnp.int32)
    starts = jnp.cumsum(counts) - counts
    padded = (counts + EXPERT_BLOCK - 1) // EXPERT_BLOCK * EXPERT_BLOCK
    pends = jnp.cumsum(padded)
    pstarts = pends - padded
    dest = pstarts[sorted_e] + jnp.arange(n_assign, dtype=jnp.int32) - starts[sorted_e]
    row_tok = jnp.full((n_rows,), n_tok, jnp.int32).at[dest].set(flat_tok[order])
    row_w = jnp.zeros((n_rows,), jnp.float32).at[dest].set(flat_w[order])
    block_start = jnp.arange(n_blocks, dtype=jnp.int32) * EXPERT_BLOCK
    block_e = jnp.minimum(jnp.searchsorted(pends, block_start, side='right'), N_EXPERTS - 1)
    x_pad = jnp.concatenate([xt, jnp.zeros((1, dm), xt.dtype)], axis=0)

    def run_block(args):
        tok, wrow, e = args
        xb = x_pad[tok]
        hb = jax.nn.silu(xb @ we_gate[e]) * (xb @ we_up[e])
        return (hb @ we_down[e]).astype(jnp.float32) * wrow[:, None]

    y_rows = lax.map(run_block, (row_tok.reshape(n_blocks, EXPERT_BLOCK),
                                 row_w.reshape(n_blocks, EXPERT_BLOCK), block_e))
    routed = jnp.zeros((n_tok + 1, dm), jnp.float32).at[row_tok].add(
        y_rows.reshape(n_rows, dm))[:n_tok]
    shared = (jax.nn.silu(xt @ ws_gate) * (xt @ ws_up)) @ ws_down
    return (routed.astype(x.dtype) + shared).reshape(bsz, seq, dm)

def _layer(x, cos, sin, w_in, lam_re, lam_im, log_dt, b_re, b_im, c_re, c_im, d_skip,
           w_glu, b_glu, q_norm_g, w_uq, kv_norm_g, w_ukv, w_o, ln1_g, ln1_b,
           w_router, router_bias, we_gate, we_up, we_down, ws_gate, ws_up, ws_down,
           ln2_g, ln2_b):
    proj = x @ w_in
    u = proj[..., :D_SSM]
    c_q = proj[..., D_SSM:D_SSM + Q_LORA_RANK]
    ckv_rope = proj[..., D_SSM + Q_LORA_RANK:]
    s = jax.nn.gelu(_s5_bidirectional(u, lam_re, lam_im, log_dt, b_re, b_im, c_re, c_im, d_skip))
    s = s * jax.nn.sigmoid(s @ w_glu + b_glu)
    a = _mla(c_q, ckv_rope, q_norm_g, w_uq, kv_norm_g, w_ukv, cos, sin)
    mix = jnp.concatenate([s, a], axis=-1) @ w_o
    x1 = _layer_norm(DEEPNORM_ALPHA * x + mix, ln1_g, ln1_b).astype(x.dtype)
    f = _moe(x1, w_router, router_bias, we_gate, we_up, we_down, ws_gate, ws_up, ws_down)
    return _layer_norm(DEEPNORM_ALPHA * x1 + f, ln2_g, ln2_b).astype(x.dtype)

def setup_inputs(seed: int = 0) -> dict:
    key = jax.random.key(seed)
    ks = jax.random.split(key, 32)
    f32 = jnp.float32
    nrm = lambda k, shape, s: jax.random.normal(k, shape, f32) * s
    L = DEPTH
    G, N, P = N_SSM_GROUPS, SSM_STATE, SSM_GROUP
    d_sh = D_EXPERT * N_SHARED
    return {
        "x": jax.random.normal(ks[0], (BATCH, SEQ, D_MODEL), f32),
        "w_in": nrm(ks[1], (L, D_MODEL, D_IN), D_MODEL ** -0.5),
        "lam_re": -0.5 + nrm(ks[2], (L, N_DIR, G, N), 0.01),
        "lam_im": math.pi * jnp.arange(N, dtype=f32) + nrm(ks[3], (L, N_DIR, G, N), 0.01),
        "log_dt": jax.random.uniform(ks[4], (L, N_DIR, G), f32, math.log(DT_MIN), math.log(DT_MAX)),
        "b_re": nrm(ks[5], (L, N_DIR, G, N, P), (2 * P) ** -0.5),
        "b_im": nrm(ks[6], (L, N_DIR, G, N, P), (2 * P) ** -0.5),
        "c_re": nrm(ks[7], (L, N_DIR, G, P, N), N ** -0.5),
        "c_im": nrm(ks[8], (L, N_DIR, G, P, N), N ** -0.5),
        "d_skip": nrm(ks[9], (L, D_SSM), 1.0),
        "w_glu": nrm(ks[10], (L, D_SSM, D_SSM), D_SSM ** -0.5),
        "b_glu": nrm(ks[11], (L, D_SSM), 0.01),
        "q_norm_g": 1.0 + nrm(ks[12], (L, Q_LORA_RANK), 0.01),
        "w_uq": nrm(ks[13], (L, Q_LORA_RANK, N_HEADS * (QK_NOPE_DIM + QK_ROPE_DIM)), Q_LORA_RANK ** -0.5),
        "kv_norm_g": 1.0 + nrm(ks[14], (L, KV_LORA_RANK), 0.01),
        "w_ukv": nrm(ks[15], (L, KV_LORA_RANK, N_HEADS * (QK_NOPE_DIM + V_HEAD_DIM)), KV_LORA_RANK ** -0.5),
        "w_o": nrm(ks[16], (L, D_MIX, D_MODEL), D_MIX ** -0.5 * DEEPNORM_BETA),
        "ln1_g": 1.0 + nrm(ks[17], (L, D_MODEL), 0.01),
        "ln1_b": nrm(ks[18], (L, D_MODEL), 0.01),
        "w_router": nrm(ks[19], (L, D_MODEL, N_EXPERTS), D_MODEL ** -0.5),
        "router_bias": nrm(ks[20], (L, N_EXPERTS), 0.01),
        "we_gate": nrm(ks[21], (L, N_EXPERTS, D_MODEL, D_EXPERT), D_MODEL ** -0.5),
        "we_up": nrm(ks[22], (L, N_EXPERTS, D_MODEL, D_EXPERT), D_MODEL ** -0.5),
        "we_down": nrm(ks[23], (L, N_EXPERTS, D_EXPERT, D_MODEL), D_EXPERT ** -0.5 * DEEPNORM_BETA),
        "ws_gate": nrm(ks[24], (L, D_MODEL, d_sh), D_MODEL ** -0.5),
        "ws_up": nrm(ks[25], (L, D_MODEL, d_sh), D_MODEL ** -0.5),
        "ws_down": nrm(ks[26], (L, d_sh, D_MODEL), d_sh ** -0.5 * DEEPNORM_BETA),
        "ln2_g": 1.0 + nrm(ks[27], (L, D_MODEL), 0.01),
        "ln2_b": nrm(ks[28], (L, D_MODEL), 0.01),
    }

def reference(x, w_in, lam_re, lam_im, log_dt, b_re, b_im, c_re, c_im, d_skip, w_glu, b_glu,
              q_norm_g, w_uq, kv_norm_g, w_ukv, w_o, ln1_g, ln1_b, w_router, router_bias,
              we_gate, we_up, we_down, ws_gate, ws_up, ws_down, ln2_g, ln2_b):
    seq = x.shape[1]
    pos = jnp.arange(seq, dtype=jnp.float32)
    inv_freq = ROPE_THETA ** (-jnp.arange(0, QK_ROPE_DIM, 2, dtype=jnp.float32) / QK_ROPE_DIM)
    ang = pos[:, None] * inv_freq[None, :]
    cos, sin = jnp.cos(ang), jnp.sin(ang)
    h = x
    for i in range(DEPTH):
        h = _layer(h, cos, sin, w_in[i], lam_re[i], lam_im[i], log_dt[i], b_re[i], b_im[i],
                   c_re[i], c_im[i], d_skip[i], w_glu[i], b_glu[i], q_norm_g[i], w_uq[i],
                   kv_norm_g[i], w_ukv[i], w_o[i], ln1_g[i], ln1_b[i], w_router[i],
                   router_bias[i], we_gate[i], we_up[i], we_down[i], ws_gate[i], ws_up[i],
                   ws_down[i], ln2_g[i], ln2_b[i])
    return h


_drawn_inputs = setup_inputs


def setup_inputs(seed=0):
    import zlib

    import numpy as np

    out = dict(_drawn_inputs(seed))
    spreads = {}
    factors = {'lam_re': 200.0,
     'b_glu': 29.259,
     'q_norm_g': 8.0,
     'kv_norm_g': 8.0,
     'ln2_g': 200.0,
     'ln2_b': 200.0,
     'lam_im': 30.84,
     'log_dt': 24.086,
     'b_re': 30.272,
     'b_im': 27.755,
     'c_re': 30.024,
     'c_im': 35.63}
    for name, (base, spread) in spreads.items():
        noise = np.random.default_rng([zlib.crc32(name.encode()), seed]).standard_normal(out[name].shape)
        drawn = base * np.exp(spread * noise) if base else spread * noise
        out[name] = __import__('jax').numpy.asarray(drawn.astype(out[name].dtype))
    for name, factor in factors.items():
        out[name] = (out[name] * factor).astype(out[name].dtype)
    return out
```

```python
import math
from contextlib import ExitStack

import concourse.bass as bass
from concourse import mybir

f32 = mybir.dt.float32
i32 = mybir.dt.int32
u32 = mybir.dt.uint32
ALU = mybir.AluOpType
ACT = mybir.ActivationFunctionType
AX = mybir.AxisListType

P = 128
D = 1024
SEQ = 1024
T = 8
NC = SEQ // T
KD = D // P
D_SSM = 512
G = 32
CH = 16
N = 64
Q_RANK = 256
KV_RANK = 128
HEADS = 8
NOPE = 64
ROPE = 32
DQ = NOPE + ROPE
DV = 64
N_EXPERTS = 64
TOP_K = 6
EGROUPS = 8
TOP_GROUPS = 4
F = 256
KF = F // P
OVER = SEQ * TOP_K // P
SLOTS = (N_EXPERTS + OVER) * P
ROUTED_SCALE = 2.5
ALPHA = 2.0 ** 0.25
LN_EPS = 1e-5
RMS_EPS = 1e-6
BIG = 1e30
TWO_PI = 2.0 * math.pi
ROUND = 1.5 * 2.0 ** 23


def makers(nc, ctx, stage, held=None):
    def sb(name, shape, dt):
        return ctx.enter_context(nc.sbuf_tensor(f"{stage}_{name}", shape, dt))

    def ps(name, shape):
        return ctx.enter_context(nc.psum_tensor(f"{stage}_{name}", shape, f32))

    def sem(name):
        held.append(nc.alloc_semaphore(name=f"{stage}_{name}"))
        return held[-1]
    return sb, ps, sem


def hand_back(nc, held):
    nc.all_engine_barrier()
    nc.clear_and_free_semaphores(held)
    nc.all_engine_barrier()
    held.clear()


class Kit:

    def __init__(self, given):
        self.x_in = given["x"]
        self.w_in, self.lam_re, self.lam_im, self.log_dt = [given[n] for n in ("w_in", "lam_re", "lam_im", "log_dt")]
        self.b_re, self.b_im, self.c_re, self.c_im = [given[n] for n in ("b_re", "b_im", "c_re", "c_im")]
        self.d_skip, self.w_glu, self.b_glu, self.q_norm_g = [given[n] for n in ("d_skip", "w_glu", "b_glu", "q_norm_g")]
        self.w_uq, self.kv_norm_g, self.w_ukv, self.w_o = [given[n] for n in ("w_uq", "kv_norm_g", "w_ukv", "w_o")]
        self.ln1_g, self.ln1_b, self.w_router, self.router_bias = [given[n] for n in ("ln1_g", "ln1_b", "w_router", "router_bias")]
        self.we_gate, self.we_up, self.we_down, self.ws_gate = [given[n] for n in ("we_gate", "we_up", "we_down", "ws_gate")]
        self.ws_up, self.ws_down, self.ln2_g, self.ln2_b = [given[n] for n in ("ws_up", "ws_down", "ln2_g", "ln2_b")]
        self.consts, self.out = [given[n] for n in ("consts", "out")]


class Chain:

    def __init__(self, eng, sem, base=0):
        self.eng, self.sem, self.base, self.n = eng, sem, base, 0

    def link(self, ins):
        self.n += 1
        ins.then_inc(self.sem, 1)
        self.eng.wait_ge(self.sem, self.base + self.n)


C_ID, C_TRI, C_ONE, C_CHUNK, C_CHUNKR, C_COS, C_SIN, C_E, C_E128, C_TOK, C_PART, C_SGN, C_END = [
    0, 128, 256, 384, 512, 640, 768, 896, 960, 1024, 1032, 1033, 1036]


def constants():
    import numpy as np
    c = np.zeros((P, C_END), np.float32)
    p = np.arange(P)
    c[:, C_ID:C_ID + P] = np.eye(P)
    c[:, C_TRI:C_TRI + P] = p[:, None] < p[None, :]
    c[:, C_ONE:C_ONE + P] = 1.0
    c[:, C_CHUNK:C_CHUNK + P] = p[None, :]
    c[:, C_CHUNKR:C_CHUNKR + P] = P - 1 - p[None, :]
    inv = (np.float32(10000.0) ** (-np.arange(0, ROPE, 2, dtype=np.float32) / np.float32(ROPE))).astype(np.float32)
    pos = (T * p[:, None] + np.arange(T)[None, :]).astype(np.float32)
    ang = (pos[:, :, None] * inv[None, None, :]).astype(np.float32).astype(np.float64)
    c[:, C_COS:C_COS + P] = np.cos(ang).reshape(P, P)
    c[:, C_SIN:C_SIN + P] = np.sin(ang).reshape(P, P)
    c[:, C_E:C_E + N_EXPERTS] = np.arange(N_EXPERTS)[None, :]
    c[:, C_E128:C_E128 + N_EXPERTS] = P * np.arange(N_EXPERTS)[None, :]
    c[:, C_TOK:C_TOK + T] = p[:, None] + P * np.arange(T)[None, :]
    c[:, C_PART] = p
    c[:, C_SGN] = np.where(p < N, 1.0, -1.0)
    c[:, C_SGN + 2] = math.pi / 2
    c[:, C_SGN + 1] = np.float32(6.2831850) * c[:, C_SGN]
    return c


def persistent(nc, ctx, k):
    sb, _, _ = makers(nc, ctx, "all")
    const = sb("const", [P, C_END], f32)
    k.const = const
    k.ident = const[:, C_ID:C_ID + P]
    k.tri = const[:, C_TRI:C_TRI + P]
    k.ones = const[:, C_ONE:C_ONE + P]
    k.iota_e = const[:, C_E:C_E + N_EXPERTS]
    k.iota_e128 = const[:, C_E128:C_E128 + N_EXPERTS]
    k.tok = const[:, C_TOK:C_TOK + T]
    k.cos = const[:, C_COS:C_COS + P].rearrange("p (t f) -> p t f", t=T)
    k.sin = const[:, C_SIN:C_SIN + P].rearrange("p (t f) -> p t f", t=T)
    k.chunk = const[:, C_CHUNK:C_CHUNK + NC]
    k.chunkr = const[:, C_CHUNKR:C_CHUNKR + NC]
    k.sgn = const[:, C_SGN:C_SGN + 1]
    k.sgn2pi = const[:, C_SGN + 1:C_SGN + 2]
    k.half_pi = const[:, C_SGN + 2:C_SGN + 3]
    k.part = const[:, C_PART:C_PART + 1]
    k.x = sb("x_sb", [P, T, D], f32)
    k.rank = sb("rank", [P, T, N_EXPERTS], f32)
    k.counts = sb("counts", [P, N_EXPERTS], f32)
    k.picked = sb("picked", [P, T, TOP_K], f32)
    k.top_w = sb("top_w", [P, T, TOP_K], f32)
    k.dest = sb("dest_i", [P, T * TOP_K], i32)
    k.block_tok = sb("block_tok", [P, N_EXPERTS + OVER], i32)
    k.over_expert = sb("over_expert", [1, OVER], i32)
    k.n_over = sb("n_over", [1, 1], i32)
    k.x1_d = nc.dram_tensor("x1_d", (SEQ, D), f32).ap()
    k.y_d = nc.dram_tensor("y_d", (SLOTS, D), f32).ap()
    k.slot_tok_d = nc.dram_tensor("slot_tok_d", (SLOTS, 1), f32).ap()
    k.u_d = nc.dram_tensor("u_d", (D_SSM, SEQ), f32).ap()
    k.ys_d = nc.dram_tensor("ys_d", (D_SSM, SEQ), f32).ap()
    k.expert_d = nc.dram_tensor("expert_d", (P,), i32).ap()


def project(nc, k):
    NCV = Q_RANK + KV_RANK + ROPE
    with ExitStack() as ctx:
        sb, ps, sem = makers(nc, ctx, "proj", k.held)
        w = sb("w", [P, KD, D_SSM + NCV], f32)
        xT = sb("xT", [P, KD, SEQ], f32)
        uT = sb("uT", [P, 4, SEQ], f32)
        c = sb("c", [P, T, NCV], f32)
        sq = sb("sq", [P, Q_RANK], f32)
        ssq = sb("ssq", [P, 2, T], f32)
        ms = sb("ms", [P, 2, T], f32)
        rms = sb("rms", [P, 2, T], f32)
        rot = sb("rot", [P, 4, T, ROPE // 2], f32)
        gq = sb("gq", [P, 2], f32)
        gkv = sb("gkv", [P, 1], f32)
        p_x = ps("p_x", [P, 2, KD, P])
        p_c = ps("p_c", [P, 2, 512])
        p_u = ps("p_u", [P, 2, 512])
        const_in, w_in, g_in, u_out = sem("const_in"), sem("w_in"), sem("g_in"), sem("u_out")
        x_in = [sem(f"x_in{t}") for t in range(T)]
        x_turned, xT_dve, xT_act = sem("x_turned"), sem("xT_dve"), sem("xT_act")
        c_done, c_read, sq_done, ms_done, rms_done = sem("c_done"), sem("c_read"), sem("sq_done"), sem("ms_done"), sem("rms_done")
        u_done, u_read, scaled, c_turned, cT_read, own = sem("u_done"), sem("u_read"), sem("scaled"), sem("c_turned"), sem("cT_read"), sem("own")
        block = ctx.enter_context(nc.Block())

        @block.sync
        def _(sp):
            sp.dma_start(k.const[:, :], k.consts).then_inc(const_in, 16)
            xv = k.x_in[0].rearrange("(c j) d -> c j d", j=T)
            wv = k.w_in[0].rearrange("(p k) n -> p k n", k=KD)
            for t in range(T):
                sp.dma_start(k.x[:, t, :], xv[:, t, :]).then_inc(x_in[t], 16)
                if t == 1:
                    sp.dma_start(w[:, :, :], wv).then_inc(w_in, 16)
            for kk in range(2):
                sp.dma_start(gq[:, kk:kk + 1], k.q_norm_g[0, kk * P:(kk + 1) * P].rearrange("(p o) -> p o", o=1)).then_inc(g_in, 16)
            sp.dma_start(gkv[:, :], k.kv_norm_g[0].rearrange("(p o) -> p o", o=1)).then_inc(g_in, 16)
            sp.wait_ge(u_read, 8)
            sp.dma_start(k.u_d.rearrange("(m p) t -> p m t", p=P), uT[:, :, :]).then_inc(u_out, 16)
            sp.wait_ge(u_out, 16)

        @block.tensor
        def _(pe):
            def turn_x(t):
                pe.wait_ge(x_in[t], 16)
                if t >= 2:
                    pe.wait_ge(xT_dve, t - 1)
                    pe.wait_ge(xT_act, t - 1)
                for half in range(2):
                    for q in range(4):
                        kk = half * 4 + q
                        last = nc.tensor.transpose(p_x[:, t % 2, kk, :], k.x[:, t, kk::KD], k.ident)
                    last.then_inc(x_turned, 1)

            pe.wait_ge(const_in, 16)
            turn_x(0)
            for t in range(T):
                if t + 1 < T:
                    turn_x(t + 1)
                pe.wait_ge(xT_dve, t + 1)
                pe.wait_ge(xT_act, t + 1)
                if t == 0:
                    pe.wait_ge(w_in, 16)
                if t >= 2:
                    pe.wait_ge(c_read, t - 1)
                for kk in range(KD):
                    last = nc.tensor.matmul(p_c[:, t % 2, 0:NCV], xT[:, kk, t * P:(t + 1) * P], w[:, kk, D_SSM:],
                                            start=(kk == 0), stop=(kk == KD - 1))
                last.then_inc(c_done, 1)
            for n in range(8):
                m, half = n // 2, n % 2
                if n >= 2:
                    pe.wait_ge(u_read, n - 1)
                for kk in range(KD):
                    last = nc.tensor.matmul(p_u[:, n % 2, :], w[:, kk, m * P:(m + 1) * P], xT[:, kk, half * 512:(half + 1) * 512],
                                            start=(kk == 0), stop=(kk == KD - 1))
                last.then_inc(u_done, 1)
            pe.wait_ge(c_read, T)
            for t in range(T):
                pe.wait_ge(scaled, t + 1)
                if t >= 2:
                    pe.wait_ge(cT_read, t - 1)
                nc.tensor.transpose(p_c[:, t % 2, 0:P], c[:, t, 0:P], k.ident)
                nc.tensor.transpose(p_c[:, t % 2, P:2 * P], c[:, t, P:2 * P], k.ident)
                nc.tensor.transpose(p_c[:, t % 2, 2 * P:3 * P], c[:, t, 2 * P:3 * P], k.ident)
                nc.tensor.transpose(p_c[0:DQ, t % 2, 3 * P:4 * P], c[:, t, NCV - DQ:NCV], k.ident).then_inc(c_turned, 1)

        @block.scalar
        def _(act):
            for t in range(T):
                act.wait_ge(x_turned, 2 * t + 2)
                nc.scalar.activation(xT[:, 4:8, t * P:(t + 1) * P], p_x[:, t % 2, 4:8, :], ACT.Copy).then_inc(xT_act, 1)
            for t in range(T):
                act.wait_ge(c_read, t + 1)
                if t:
                    act.wait_ge(sq_done, 2 * t)
                nc.scalar.activation(sq[:, :], c[:, t, 0:Q_RANK], ACT.Square, accum_out=ssq[:, 0, t:t + 1]).then_inc(sq_done, 1)
                act.wait_ge(sq_done, 2 * t + 1)
                nc.scalar.activation(sq[:, 0:KV_RANK], c[:, t, Q_RANK:Q_RANK + KV_RANK], ACT.Square,
                                     accum_out=ssq[:, 1, t:t + 1]).then_inc(sq_done, 1)
            act.wait_ge(ms_done, 1)
            nc.scalar.activation(rms[:, :, :], ms[:, :, :], ACT.Sqrt).then_inc(rms_done, 1)
            for n in range(8):
                m, half = n // 2, n % 2
                act.wait_ge(u_done, n + 1)
                nc.scalar.activation(uT[:, m, half * 512:(half + 1) * 512], p_u[:, n % 2, :], ACT.Copy).then_inc(u_read, 1)

        @block.vector
        def _(dve):
            ch = Chain(dve, own)

            def keep_c(t):
                dve.wait_ge(c_done, t + 1)
                nc.vector.tensor_copy(c[:, t, :], p_c[:, t % 2, 0:NCV]).then_inc(c_read, 1)

            for t in range(T):
                dve.wait_ge(x_turned, 2 * t + 1)
                nc.vector.tensor_copy(xT[:, 0:4, t * P:(t + 1) * P], p_x[:, t % 2, 0:4, :]).then_inc(xT_dve, 1)
                if t:
                    keep_c(t - 1)
            keep_c(T - 1)
            dve.wait_ge(sq_done, 2 * T)
            nc.vector.tensor_scalar(ms[:, 0, :], ssq[:, 0, :], 1.0 / Q_RANK, RMS_EPS, ALU.mult, ALU.add)
            nc.vector.tensor_scalar(ms[:, 1, :], ssq[:, 1, :], 1.0 / KV_RANK, RMS_EPS, ALU.mult, ALU.add).then_inc(ms_done, 1)
            c1, c2 = c[:, :, NCV - 32:NCV - 16], c[:, :, NCV - 16:NCV]
            dve.wait_ge(c_read, T)
            nc.vector.tensor_tensor(rot[:, 0], c1, k.cos, ALU.mult)
            nc.vector.tensor_tensor(rot[:, 1], c2, k.sin, ALU.mult)
            nc.vector.tensor_tensor(rot[:, 2], c1, k.sin, ALU.mult)
            ch.link(nc.vector.tensor_tensor(rot[:, 3], c2, k.cos, ALU.mult))
            nc.vector.tensor_tensor(c1, rot[:, 0], rot[:, 1], ALU.subtract)
            ch.link(nc.vector.tensor_tensor(c2, rot[:, 2], rot[:, 3], ALU.add))
            dve.wait_ge(rms_done, 1)
            ch.link(nc.vector.reciprocal(rms[:, :, :], rms[:, :, :]))
            for t in range(T):
                nc.vector.tensor_scalar(c[:, t, 0:Q_RANK], c[:, t, 0:Q_RANK], rms[:, 0, t:t + 1], None, ALU.mult)
                nc.vector.tensor_scalar(c[:, t, Q_RANK:Q_RANK + KV_RANK], c[:, t, Q_RANK:Q_RANK + KV_RANK],
                                        rms[:, 1, t:t + 1], None, ALU.mult).then_inc(scaled, 1)
            dve.wait_ge(g_in, 48)
            for t in range(T):
                cols = slice(t * P, (t + 1) * P)
                dve.wait_ge(c_turned, t + 1)
                nc.vector.tensor_scalar(k.cqT[:, 0, cols], p_c[:, t % 2, 0:P], gq[:, 0:1], None, ALU.mult)
                nc.vector.tensor_scalar(k.cqT[:, 1, cols], p_c[:, t % 2, P:2 * P], gq[:, 1:2], None, ALU.mult)
                nc.vector.tensor_scalar(k.ckvT[:, cols], p_c[:, t % 2, 2 * P:3 * P], gkv[:, 0:1], None, ALU.mult)
                for u in range(2):
                    last = nc.vector.tensor_copy(k.kT[NOPE:DQ, u, cols], p_c[NOPE:DQ, t % 2, 3 * P:4 * P])
                last.then_inc(cT_read, 1)


def attention(nc, k):
    SCALE = DQ ** -0.5
    with ExitStack() as ctx:
        sb, ps, sem = makers(nc, ctx, "att", k.held)
        wq = sb("wq", [P, 2, 2, DQ], f32)
        wkv = sb("wkv", [P, 2, NOPE + DV], f32)
        q = sb("q", [P, T, DQ], f32)
        rot = sb("rot", [P, 4, T, ROPE // 2], f32)
        qT = sb("qT", [DQ, SEQ], f32)
        v = sb("v", [P, T, DV], f32)
        nmax = sb("nmax", [P, 2], f32)
        bias = sb("bias", [P, 2], f32)
        total = sb("total", [P, 4], f32)
        rtotal = sb("rtotal", [P, 2], f32)
        pr = sb("pr", [P, 2, SEQ], f32)
        prT = sb("prT", [P, 2, T, P], f32)
        p_s = ps("p_s", [P, 2, SEQ])
        p_t = ps("p_t", [P, T, P])
        p_o = ps("p_o", [P, 512])
        p_v = ps("p_v", [P, T, DV])
        kT = k.kT
        w_in = [sem(f"w_in{u}") for u in range(2)]
        q_done, kv_done, q_kept, q_rotated, q_turned = sem("q_done"), sem("kv_done"), sem("q_kept"), sem("q_rotated"), sem("q_turned")
        head_dve, head_act = sem("head_dve"), sem("head_act")
        scored, biased, probs, p_turned, pT_dve, pT_act = sem("scored"), sem("biased"), sem("probs"), sem("p_turned"), sem("pT_dve"), sem("pT_act")
        o_done, o_read, own = sem("o_done"), sem("o_read"), sem("own")
        LINKS = 3 + 3 * T
        block = ctx.enter_context(nc.Block())

        @block.sync
        def _(sp):
            def load(h, u):
                sp.dma_start(wq[:, u], k.w_uq[0].rearrange("(k p) n -> p k n", p=P)[:, :, bass.ds(h * DQ, DQ)]).then_inc(w_in[u], 16)
                sp.dma_start(wkv[:, u, :], k.w_ukv[0][:, bass.ds(h * (NOPE + DV), NOPE + DV)]).then_inc(w_in[u], 16)
            load(0, 0)
            load(1, 1)
            with sp.Fori(1, HEADS // 2) as hh:
                for u in range(2):
                    h = hh * 2 + u
                    sp.wait_ge(kv_done, h - 1)
                    load(h, u)

        @block.tensor
        def _(pe):
            def scores(h, t):
                for half in range(2):
                    last = nc.tensor.matmul(p_s[:, t % 2, half * 512:(half + 1) * 512], qT[:, t * P:(t + 1) * P],
                                            kT[:, k.u, half * 512:(half + 1) * 512], start=True, stop=True)
                last.then_inc(scored, 1)

            with pe.Fori(0, HEADS // 2) as hh:
                for u in range(2):
                    h = hh * 2 + u
                    k.u = u
                    pe.wait_ge(w_in[u], hh * 32 + 32)
                    for t in range(T):
                        b, col = t // 4, (t % 4) * DQ
                        for kk in range(2):
                            last = nc.tensor.matmul(p_s[:, 0, b * 512 + col:b * 512 + col + DQ], k.cqT[:, kk, t * P:(t + 1) * P],
                                                    wq[:, u, kk, :], start=(kk == 0), stop=(kk == 1))
                    last.then_inc(q_done, 1)
                    for half in range(2):
                        nc.tensor.matmul(p_s[0:NOPE, 1, half * 512:(half + 1) * 512], wkv[:, u, 0:NOPE],
                                         k.ckvT[:, half * 512:(half + 1) * 512], start=True, stop=True)
                    for t in range(T):
                        last = nc.tensor.matmul(p_v[:, t, :], k.ckvT[:, t * P:(t + 1) * P], wkv[:, u, NOPE:], start=True, stop=True)
                    last.then_inc(kv_done, 1)
                    pe.wait_ge(q_rotated, h + 1)
                    for t in range(T):
                        last = nc.tensor.transpose(p_t[0:DQ, t, :], q[:, t, :], k.ident)
                    last.then_inc(q_turned, 1)
                    pe.wait_ge(head_dve, h + 1)
                    pe.wait_ge(head_act, h + 1)
                    scores(h, 0)
                    scores(h, 1)
                    for t in range(T):
                        n = h * T + t
                        pe.wait_ge(probs, n + 1)
                        for half in range(2):
                            for r in range(4):
                                j = half * 4 + r
                                last = nc.tensor.transpose(p_t[:, j, :], pr[:, t % 2, j * P:(j + 1) * P], k.ident)
                            last.then_inc(p_turned, 1)
                        if t + 2 < T:
                            scores(h, t + 2)
                        pe.wait_ge(pT_dve, n + 1)
                        pe.wait_ge(pT_act, n + 1)
                        if t:
                            pe.wait_ge(o_read, n)
                        for j in range(T):
                            last = nc.tensor.matmul(p_o[:, 0:DV], prT[:, t % 2, j, :], v[:, j, :], start=(j == 0), stop=(j == T - 1))
                        last.then_inc(o_done, 1)
                    pe.wait_ge(o_read, h * T + T)

        @block.scalar
        def _(act):
            with act.Fori(0, HEADS // 2) as hh:
                for u in range(2):
                    h = hh * 2 + u
                    act.wait_ge(q_done, h + 1)
                    for b in range(2):
                        last = nc.scalar.activation(q[:, 4 * b:4 * b + 4, :].rearrange("p t n -> p (t n)"),
                                                    p_s[:, 0, b * 512:b * 512 + 4 * DQ], ACT.Copy)
                    last.then_inc(q_kept, 1)
                    act.wait_ge(kv_done, h + 1)
                    nc.scalar.activation(kT[0:NOPE, u, :], p_s[0:NOPE, 1, :], ACT.Copy)
                    act.wait_ge(q_turned, h + 1)
                    nc.scalar.activation(qT[:, 512:SEQ], p_t[0:DQ, 4:8, :].rearrange("p t c -> p (t c)"), ACT.Copy).then_inc(head_act, 1)
                    for t in range(T):
                        n = h * T + t
                        act.wait_ge(biased, n + 1)
                        nc.scalar.activation(pr[:, t % 2, :], p_s[:, t % 2, :], ACT.Exp, bias=bias[:, t % 2:t % 2 + 1], scale=SCALE,
                                             accum_out=total[:, t % 4:t % 4 + 1]).then_inc(probs, 1)
                        act.wait_ge(p_turned, 2 * n + 2)
                        nc.scalar.activation(prT[:, t % 2, 4:8, :], p_t[:, 4:8, :], ACT.Copy).then_inc(pT_act, 1)

        @block.vector
        def _(dve):
            with dve.Fori(0, HEADS // 2) as hh:
                for u in range(2):
                    h = hh * 2 + u
                    ch = Chain(dve, own, h * LINKS)
                    dve.wait_ge(q_kept, h + 1)
                    q1, q2 = q[:, :, NOPE:NOPE + 16], q[:, :, NOPE + 16:DQ]
                    nc.vector.tensor_tensor(rot[:, 0], q1, k.cos, ALU.mult)
                    nc.vector.tensor_tensor(rot[:, 1], q2, k.sin, ALU.mult)
                    nc.vector.tensor_tensor(rot[:, 2], q1, k.sin, ALU.mult)
                    ch.link(nc.vector.tensor_tensor(rot[:, 3], q2, k.cos, ALU.mult))
                    nc.vector.tensor_tensor(q1, rot[:, 0], rot[:, 1], ALU.subtract)
                    nc.vector.tensor_tensor(q2, rot[:, 2], rot[:, 3], ALU.add).then_inc(q_rotated, 1)
                    dve.wait_ge(kv_done, h + 1)
                    nc.vector.tensor_copy(v[:, :, :], p_v[:, :, :])
                    dve.wait_ge(q_turned, h + 1)
                    nc.vector.tensor_copy(qT[:, 0:512], p_t[0:DQ, 0:4, :].rearrange("p t c -> p (t c)")).then_inc(head_dve, 1)

                    def top(t):
                        dve.wait_ge(scored, h * T + (t + 1))
                        ch.link(nc.vector.tensor_reduce(nmax[:, t % 2:t % 2 + 1], p_s[:, t % 2, :], AX.X, ALU.max, negate=True))
                        nc.vector.tensor_scalar(bias[:, t % 2:t % 2 + 1], nmax[:, t % 2:t % 2 + 1], SCALE, None, ALU.mult).then_inc(biased, 1)

                    def finish(t):
                        n = h * T + t
                        dve.wait_ge(o_done, n + 1)
                        ch.link(nc.vector.reciprocal(rtotal[:, t % 2:t % 2 + 1], total[:, t % 4:t % 4 + 1]))
                        nc.vector.tensor_scalar(k.o[:, t, bass.ds(h * DV, DV)], p_o[:, 0:DV], rtotal[:, t % 2:t % 2 + 1], None,
                                                ALU.mult).then_inc(o_read, 1)

                    top(0)
                    top(1)
                    for t in range(T):
                        dve.wait_ge(p_turned, (h * T + t) * 2 + 1)
                        nc.vector.tensor_copy(prT[:, t % 2, 0:4, :], p_t[:, 0:4, :]).then_inc(pT_dve, 1)
                        if t + 2 < T:
                            top(t + 2)
                        finish(t)
                    for spare in range(LINKS - ch.n):
                        ch.n += 1
                        dve.sem_inc(own, 1)


def s5_parameters(nc, k):
    DG = 2 * G
    C1, C2 = 6.28125, TWO_PI - 6.28125
    PI = 3.1415925
    with ExitStack() as ctx:
        sb, ps, sem = makers(nc, ctx, "par", k.held)
        lr = sb("lr", [DG, P], f32)
        li = sb("li", [DG, P], f32)
        dt = sb("dt", [DG, 2], f32)
        mag = sb("mag", [DG, P], f32)
        th = sb("th", [DG, P], f32)
        n = sb("n", [DG, P], f32)
        tmp = sb("tmp", [DG, 2, P], f32)
        cs = sb("cs", [DG, 2, P], f32)
        par = sb("par", [DG, 6, P], f32)
        ar, ai, kr, ki, t8, m8 = [par[:, i, :] for i in range(6)]
        prm = sb("prm", [P, 6, DG], f32)
        b1 = sb("b1", [P, DG, CH], f32)
        b2 = sb("b2", [P, DG, CH], f32)
        ba = sb("ba", [P, DG, CH], f32)
        bb = sb("bb", [P, DG, CH], f32)
        c_rows = sb("c_rows", [P, 8, 3 * N], f32)
        pt = sb("pt", [P, 4, DG, 4], f32)
        p_p = ps("p_p", [P, 512])
        p_c = ps("p_c", [P, 2, 8, P])
        lam_in, b_in, c_in = sem("lam_in"), sem("b_in"), sem("c_in")
        dt_done, lr_done, mag_done, ang_done, cs_done, par_done = sem("dt_done"), sem("lr_done"), sem("mag_done"), sem("ang_done"), sem("cs_done"), sem("par_done")
        par_turned, c_turned, own = sem("par_turned"), sem("c_turned"), sem("own")
        block = ctx.enter_context(nc.Block())

        @block.sync
        def _(sp):
            for half in range(2):
                cols = slice(half * N, (half + 1) * N)
                sp.dma_start(lr[:, cols], k.lam_re[0].rearrange("d g n -> (d g) n")).then_inc(lam_in, 16)
                sp.dma_start(li[:, cols], k.lam_im[0].rearrange("d g n -> (d g) n")).then_inc(lam_in, 16)
            sp.dma_start(dt[:, 0:1], k.log_dt[0].rearrange("d (g o) -> (d g) o", o=1)).then_inc(lam_in, 16)
            for half in range(2):
                rows, other = slice(half * N, (half + 1) * N), slice((1 - half) * N, (2 - half) * N)
                src = (k.b_re, k.b_im)[half][0].rearrange("d g n p -> n (d g) p")
                sp.dma_start(b1[rows, :, :], src).then_inc(b_in, 16)
                sp.dma_start(b2[other, :, :], src).then_inc(b_in, 16)
            for i, src in enumerate((k.c_re, k.c_im, k.c_re)):
                sp.dma_start(c_rows[:, :, i * N:(i + 1) * N],
                             src[0].rearrange("d g p n -> (d g p) n").rearrange("(a r) n -> r a n", r=P)).then_inc(c_in, 16)

        @block.scalar
        def _(act):
            act.wait_ge(lam_in, 80)
            nc.scalar.activation(dt[:, 1:2], dt[:, 0:1], ACT.Exp).then_inc(dt_done, 1)
            act.wait_ge(lr_done, 1)
            act.wait_ge(dt_done, 1)
            nc.scalar.activation(mag[:, :], lr[:, :], ACT.Exp, scale=dt[:, 1:2]).then_inc(mag_done, 1)
            act.wait_ge(ang_done, 1)
            nc.scalar.activation(cs[:, :, :], tmp[:, :, :], ACT.Sin).then_inc(cs_done, 1)

        @block.tensor
        def _(pe):
            pe.wait_ge(c_in, 48)
            for order in range(2):
                for a in range(8):
                    last = nc.tensor.transpose(p_c[:, order, a, :], c_rows[:, a, order * N:order * N + P], k.ident)
            last.then_inc(c_turned, 1)
            pe.wait_ge(par_done, 1)
            for i in range(6):
                last = nc.tensor.transpose(p_p[:, i * DG:(i + 1) * DG], par[:, i, :], k.ident[0:DG, 0:DG])
            last.then_inc(par_turned, 1)

        @block.vector
        def _(dve):
            ch = Chain(dve, own)
            tt, ts_, stt = nc.vector.tensor_tensor, nc.vector.tensor_scalar, nc.vector.scalar_tensor_tensor
            dve.wait_ge(lam_in, 80)
            ts_(lr[:, :], lr[:, :], -1e-4, None, ALU.min).then_inc(lr_done, 1)
            dve.wait_ge(dt_done, 1)
            dve.wait_ge(lr_done, 1)
            ch.link(ts_(th[:, :], li[:, :], dt[:, 1:2], None, ALU.mult))
            ch.link(ts_(n[:, :], th[:, :], 1.0 / TWO_PI, ROUND, ALU.mult, ALU.add))
            ch.link(ts_(n[:, :], n[:, :], -ROUND, None, ALU.add))
            ch.link(stt(th[:, :], n[:, :], -C1, th[:, :], ALU.mult, ALU.add))
            ch.link(stt(th[:, :], n[:, :], -C2, th[:, :], ALU.mult, ALU.add))
            ch.link(ts_(th[:, :], th[:, :], PI, -PI, ALU.min, ALU.max))
            nc.vector.tensor_copy(tmp[:, 0, :], th[:, :])
            ch.link(stt(tmp[:, 1, :], th[:, :], -1.0, th[:, :], ALU.mult, ALU.max))
            ts_(tmp[:, 1, :], tmp[:, 1, :], -1.0, math.pi / 2, ALU.mult, ALU.add).then_inc(ang_done, 1)
            dve.wait_ge(mag_done, 1)
            dve.wait_ge(cs_done, 1)
            tt(ar, mag[:, :], cs[:, 1, :], ALU.mult)
            ch.link(tt(ai, mag[:, :], cs[:, 0, :], ALU.mult))
            tt(tmp[:, 0, :], lr[:, :], lr[:, :], ALU.mult)
            ch.link(tt(tmp[:, 1, :], li[:, :], li[:, :], ALU.mult))
            ch.link(tt(n[:, :], tmp[:, 0, :], tmp[:, 1, :], ALU.add))
            nc.vector.reciprocal(n[:, :], n[:, :])
            ts_(cs[:, 0, :], ar, -1.0, None, ALU.add)
            ch.link(tt(tmp[:, 1, :], ai, li[:, :], ALU.mult))
            ch.link(tt(tmp[:, 0, :], cs[:, 0, :], lr[:, :], ALU.mult))
            ch.link(tt(kr, tmp[:, 0, :], tmp[:, 1, :], ALU.add))
            tt(tmp[:, 0, :], ai, lr[:, :], ALU.mult)
            ch.link(tt(tmp[:, 1, :], cs[:, 0, :], li[:, :], ALU.mult))
            ch.link(tt(ki, tmp[:, 0, :], tmp[:, 1, :], ALU.subtract))
            tt(kr, kr, n[:, :], ALU.mult)
            tt(ki, ki, n[:, :], ALU.mult)
            ch.link(ts_(th[:, :], th[:, :], T / TWO_PI, None, ALU.mult))
            ch.link(ts_(cs[:, 1, :], th[:, :], ROUND, -ROUND, ALU.add, ALU.add))
            tt(t8, th[:, :], cs[:, 1, :], ALU.subtract)
            ch.link(tt(m8, mag[:, :], mag[:, :], ALU.mult))
            ch.link(tt(m8, m8, m8, ALU.mult))
            tt(m8, m8, m8, ALU.mult).then_inc(par_done, 1)
            dve.wait_ge(c_turned, 1)
            cr = p_c[:, 0].rearrange("p a (g c) -> p (a g) c", c=CH)
            ci = p_c[:, 1].rearrange("p a (g c) -> p (a g) c", c=CH)
            nc.vector.tensor_copy(k.c1[:, :, :], cr)
            nc.vector.tensor_copy(k.c2[:, :, :], ci)
            ts_(k.e1[:, :, :], cr, k.sgn, None, ALU.mult)
            ts_(k.f2[:, :, :], ci, k.sgn, -1.0, ALU.mult, ALU.mult)
            dve.wait_ge(par_turned, 1)
            ch.link(nc.vector.tensor_copy(prm[:, :, :], p_p[:, 0:6 * DG].rearrange("p (i g) -> p i g", i=6)))
            nc.vector.tensor_copy(k.t8[:, :], prm[:, 4, :])
            nc.vector.tensor_copy(k.m8[:, :], prm[:, 5, :])
            dve.wait_ge(b_in, 64)
            wide = [P, DG, CH]
            krb, kib = prm[:, 2, :].unsqueeze(2).to_broadcast(wide), prm[:, 3, :].unsqueeze(2).to_broadcast(wide)
            ch.link(ts_(b2[:, :, :], b2[:, :, :], k.sgn, -1.0, ALU.mult, ALU.mult))
            tt(ba[:, :, :], b1[:, :, :], krb, ALU.mult)
            ch.link(tt(bb[:, :, :], b2[:, :, :], kib, ALU.mult))
            ch.link(tt(k.b1[:, :, :], ba[:, :, :], bb[:, :, :], ALU.add))
            tt(ba[:, :, :], b2[:, :, :], krb, ALU.mult)
            ch.link(tt(bb[:, :, :], b1[:, :, :], kib, ALU.mult))
            ch.link(tt(k.b2[:, :, :], ba[:, :, :], bb[:, :, :], ALU.subtract))
            nc.vector.memset(k.pw[:, 0, :, 0:1], 1.0)
            nc.vector.memset(k.pw[:, 1, :, 0:1], 0.0)
            nc.vector.tensor_copy(k.pw[:, 0, :, 1], prm[:, 0, :])
            ch.link(nc.vector.tensor_copy(k.pw[:, 1, :, 1], prm[:, 1, :]))
            for m in (1, 2, 4):
                w = [P, DG, m]
                re, im = k.pw[:, 0, :, 1:1 + m], k.pw[:, 1, :, 1:1 + m]
                sr, si = k.pw[:, 0, :, m:m + 1].to_broadcast(w), k.pw[:, 1, :, m:m + 1].to_broadcast(w)
                tt(pt[:, 0, :, 0:m], re, sr, ALU.mult)
                tt(pt[:, 1, :, 0:m], im, si, ALU.mult)
                tt(pt[:, 2, :, 0:m], re, si, ALU.mult)
                ch.link(tt(pt[:, 3, :, 0:m], im, sr, ALU.mult))
                tt(k.pw[:, 0, :, 1 + m:1 + 2 * m], pt[:, 0, :, 0:m], pt[:, 1, :, 0:m], ALU.subtract)
                ch.link(tt(k.pw[:, 1, :, 1 + m:1 + 2 * m], pt[:, 2, :, 0:m], pt[:, 3, :, 0:m], ALU.add))
            for i in range(2):
                ch.link(nc.vector.tensor_copy(k.pb[:, i, :, :], k.pw[:, i, :, ::-1]))


def s5_scan(nc, k):
    GB = 8
    NG = 2 * GB
    S = T + 1
    with ExitStack() as ctx:
        sb, ps, sem = makers(nc, ctx, "ssm", k.held)
        U = sb("U", [P, G, NC], f32)
        ta = sb("ta", [P, GB, S, CH], f32)
        tb = sb("tb", [P, GB, S, CH], f32)
        vs = sb("vs", [P, NG, T, CH], f32)
        bs = sb("bs", [P, NG, CH], f32)
        ed1 = sb("ed1", [P, NG, S, CH], f32)
        ed2 = sb("ed2", [P, NG, T, CH], f32)
        w_in = sb("w_in", [P, NG, 3 * N], f32)
        fr = sb("fr", [P, 2, GB, NC], f32)
        rnd = sb("rnd", [P, GB, NC], f32)
        cos_t = sb("tc", [P, NG, NC], f32)
        sin_t = sb("ts", [P, NG, NC], f32)
        ka = sb("ka", [CH, GB, 2 * T - 1, CH], f32)
        kt = sb("kt", [P, GB, T * CH], f32)
        flat = [x[:, :, :, :].rearrange("p g s c -> p (g s c)") for x in (ta, tb)]
        ra = flat[0][:, 0:4 * NC].rearrange("p (r n) -> p r n", r=4)
        rb = flat[1][:, 0:4 * NC].rearrange("p (r n) -> p r n", r=4)
        gr = flat[1][:, 4 * NC:8 * NC].rearrange("p (r n) -> p r n", r=4)
        gc = sb("gc", [P, NG, NC + 1], f32)
        gsn = sb("gsn", [P, NG, NC + 1], f32)
        ysb = rnd
        p_w = ps("p_w", [P, 4, P])
        p_k = ps("p_k", [P, 4, P])
        p_v = ps("p_v", [P, 2, 2, 4, NC])
        p_y = ps("p_y", [P, 2, 4, NC])
        u_in, y_out, kt_in = sem("u_in"), sem("y_out"), sem("kt_in")
        vs_done, vs_turned, win_done = sem("vs_done"), sem("vs_turned"), sem("win_done")
        ph_done, tab_done, ed_done, k_done, k_kept, ka_done = sem("ph_done"), sem("tab_done"), sem("ed_done"), sem("k_done"), sem("k_kept"), sem("ka_done")
        v_done, g_done, y_done, y_kept, own, own_p = sem("v_done"), sem("g_done"), sem("y_done"), sem("y_kept"), sem("own"), sem("own_p")
        cleared = sem("cleared")
        block = ctx.enter_context(nc.Block())
        NBATCH = G // GB

        @block.sync
        def _(sp):
            uv = k.u_d.rearrange("(g c) (j n) -> j c g n", c=CH, j=T)
            for j in range(T):
                sp.dma_start(U[j * CH:(j + 1) * CH, :, :], uv[j]).then_inc(u_in, 16)
            yv = k.ys_d.rearrange("(g c) (j n) -> j c g n", c=CH, j=T)
            with sp.Fori(0, NBATCH) as b:
                sp.wait_ge(ka_done, b + 1)
                for j in range(T):
                    sp.dma_start(kt[j * CH:(j + 1) * CH, :, :],
                                 ka[:, :, T - 1 - j:2 * T - 1 - j, :].rearrange("c g l d -> c g (l d)")).then_inc(kt_in, 16)
                sp.wait_ge(y_kept, b * 2 + 2)
                for j in range(T):
                    sp.dma_start(yv[j][:, bass.ds(b * GB, GB), :], ysb[j * CH:(j + 1) * CH, :, :]).then_inc(y_out, 16)
            sp.wait_ge(y_out, 16 * T * NBATCH)

        @block.tensor
        def _(pe):
            with pe.Fori(0, NBATCH) as b:
                for d in range(2):
                    pe.wait_ge(vs_done, b * 2 + d + 1)
                    for half in range(2):
                        x = 2 * d + half
                        if x:
                            pe.wait_ge(win_done, b * 4 + x)
                        for r in range(4):
                            gd = d * GB + half * 4 + r
                            last = nc.tensor.transpose(p_w[:, r, :], vs[:, gd].rearrange("p j c -> p (j c)"), k.ident)
                        last.then_inc(vs_turned, 1)
                for x, (d, half) in enumerate(((1, 0), (1, 1), (0, 0), (0, 1))):
                    if half == 0:
                        pe.wait_ge(ed_done, b * 2 + 2 - d)
                    if x:
                        pe.wait_ge(k_kept, b * 4 + x)
                    for r in range(4):
                        gd = d * GB + half * 4 + r
                        last = nc.tensor.matmul(p_k[0:CH, r, :], bs[:, gd, :], ed1[:, gd, d:d + T, :].rearrange("p j c -> p (j c)"),
                                                start=True, stop=True)
                    last.then_inc(k_done, 1)
                pe.wait_ge(win_done, b * 4 + 4)
                pe.wait_ge(u_in, 16 * T)
                for x in range(4):
                    d, half = x // 2, x % 2
                    if x >= 2:
                        pe.wait_ge(g_done, b * 4 + x - 1)
                    for part in range(2):
                        for r in range(4):
                            gd = d * GB + half * 4 + r
                            last = nc.tensor.matmul(p_v[:, x % 2, part, r, :], w_in[:, gd, part * N:part * N + P],
                                                    U[:, bass.ds(b * GB + half * 4 + r, 1), :].rearrange("p a n -> p (a n)"),
                                                    start=True, stop=True)
                    last.then_inc(v_done, 1)
                pe.wait_ge(kt_in, b * 16 * T + 16 * T)
                pe.wait_ge(g_done, b * 4 + 4)
                for half in range(2):
                    for r in range(4):
                        g = half * 4 + r
                        out = p_y[:, half, r, :]
                        nc.tensor.matmul(out, kt[:, g, :], U[:, bass.ds(b * GB + g, 1), :].rearrange("p a n -> p (a n)"), start=True, stop=False)
                        for d in range(2):
                            gd = d * GB + g
                            nc.tensor.matmul(out, ed1[:, gd, 1 - d:1 - d + T, :].rearrange("p j c -> p (j c)"), gc[:, gd, d:d + NC],
                                             start=False, stop=False)
                            last = nc.tensor.matmul(out, ed2[:, gd].rearrange("p j c -> p (j c)"), gsn[:, gd, d:d + NC],
                                                    start=False, stop=(d == 1))
                    last.then_inc(y_done, 1)

        @block.scalar
        def _(act):
            with act.Fori(0, NBATCH) as b:
                for x in range(4):
                    act.wait_ge(vs_turned, b * 4 + x + 1)
                    nc.scalar.activation(w_in[:, 4 * x:4 * x + 4, 0:P], p_w[:, :, :], ACT.Copy)
                    nc.scalar.activation(w_in[:, 4 * x:4 * x + 4, P:3 * N], p_w[:, :, 0:N], ACT.Copy).then_inc(win_done, 1)
                for d in range(2):
                    act.wait_ge(ph_done, b * 2 + d + 1)
                    nc.scalar.activation(sin_t[:, d * GB:(d + 1) * GB, :], fr[:, 0], ACT.Sin, scale=k.sgn2pi)
                    nc.scalar.activation(cos_t[:, d * GB:(d + 1) * GB, :], fr[:, 1], ACT.Sin, scale=-6.2831850, bias=k.half_pi).then_inc(tab_done, 1)
                for half in range(2):
                    act.wait_ge(y_done, b * 2 + half + 1)
                    nc.scalar.activation(ysb[:, half * 4:half * 4 + 4, :], p_y[:, half], ACT.Copy).then_inc(y_kept, 1)
                act.wait_ge(y_out, b * 16 * T + 16 * T)
                act.sem_inc(cleared, 1)

        @block.vector
        def _(dve):
            tt = nc.vector.tensor_tensor
            nc.vector.memset(gc[:, :, :], 0.0)
            nc.vector.memset(gsn[:, :, :], 0.0).then_inc(own_p, 1)
            LINKS = 2 * (1 + 2 + 3) + 4 * (1 + 1 + 1)
            with dve.Fori(0, NBATCH) as b:
                ch = Chain(dve, own, b * LINKS)

                def combine(out, pr, pi, x, y, op, n):
                    w = [P, GB, n, CH]
                    nc.vector.tensor_tensor(ta[:, :, 0:n, :], pr.unsqueeze(3).to_broadcast(w), x.unsqueeze(2).to_broadcast(w), ALU.mult)
                    ch.link(nc.vector.tensor_tensor(tb[:, :, 0:n, :], pi.unsqueeze(3).to_broadcast(w), y.unsqueeze(2).to_broadcast(w), ALU.mult))
                    return nc.vector.tensor_tensor(out, ta[:, :, 0:n, :], tb[:, :, 0:n, :], op)

                for d in range(2):
                    dg = bass.ds(b * GB + d * G, GB)
                    pw = k.pb[:, :, dg, 1:S] if d == 0 else k.pw[:, :, dg, 0:T]
                    combine(vs[:, d * GB:(d + 1) * GB], pw[:, 0], pw[:, 1], k.b1[:, dg, :], k.b2[:, dg, :], ALU.add, T).then_inc(vs_done, 1)
                    dve.wait_ge(vs_done, b * 2 + d + 1)
                for d in range(2):
                    dg = bass.ds(b * GB + d * G, GB)
                    w = [P, GB, NC]
                    if d:
                        dve.wait_ge(tab_done, b * 2 + 1)
                    ch.link(tt(fr[:, 0], k.t8[:, dg].unsqueeze(2).to_broadcast(w), (k.chunk, k.chunkr)[d].unsqueeze(1).to_broadcast(w), ALU.mult))
                    ch.link(nc.vector.tensor_scalar(rnd[:, :, :], fr[:, 0], ROUND, -ROUND, ALU.add, ALU.add))
                    tt(fr[:, 0], fr[:, 0], rnd[:, :, :], ALU.subtract).then_inc(own_p, 1)
                    dve.wait_ge(own_p, b * 2 + d + 2)
                    nc.vector.scalar_tensor_tensor(fr[:, 1], fr[:, 0], -1.0, fr[:, 0], ALU.mult, ALU.max).then_inc(ph_done, 1)
                for d in (1, 0):
                    dg = bass.ds(b * GB + d * G, GB)
                    pw = (k.pw, k.pb)[d][:, :, dg, :]
                    nc.vector.tensor_scalar(bs[:, d * GB:(d + 1) * GB, :], k.b1[:, dg, :], 1.0, None, ALU.mult)
                    combine(ed1[:, d * GB:(d + 1) * GB], pw[:, 0], pw[:, 1], k.e1[:, dg, :], k.c2[:, dg, :], ALU.subtract, S).then_inc(ed_done, 1)
                    dve.wait_ge(ed_done, b * 2 + (2 - d))
                    pw = k.pw[:, :, dg, 1:S] if d == 0 else k.pb[:, :, dg, 0:T]
                    ch.link(combine(ed2[:, d * GB:(d + 1) * GB], pw[:, 0], pw[:, 1], k.f2[:, dg, :], k.c1[:, dg, :], ALU.subtract, T))
                for x, (d, half) in enumerate(((1, 0), (1, 1), (0, 0), (0, 1))):
                    gs = slice(half * 4, half * 4 + 4)
                    src = p_k[0:CH, :, :].rearrange("c g (l d) -> c g l d", d=CH)
                    dve.wait_ge(k_done, b * 4 + x + 1)
                    if d:
                        last = nc.vector.tensor_copy(ka[:, gs, 0:T, :], src)
                    else:
                        if half == 0:
                            dve.wait_ge(k_kept, b * 4 + 2)
                        nc.vector.tensor_tensor(ka[:, gs, T - 1, :], ka[:, gs, T - 1, :], src[:, :, 0, :], ALU.add)
                        last = nc.vector.tensor_copy(ka[:, gs, T:, :], src[:, :, 1:, :])
                    last.then_inc(k_kept, 1)
                dve.wait_ge(k_kept, b * 4 + 4)
                dve.sem_inc(ka_done, 1)
                dve.wait_ge(tab_done, b * 2 + 2)
                for x in range(4):
                    d, half = x // 2, x % 2
                    q = slice(4 * x, 4 * x + 4)
                    dve.wait_ge(v_done, b * 4 + x + 1)
                    tt(ra[:, :, :], p_v[:, x % 2, 0], cos_t[:, q, :], ALU.mult)
                    ch.link(tt(rb[:, :, :], p_v[:, x % 2, 1], sin_t[:, q, :], ALU.mult))
                    ch.link(tt(ra[:, :, :], ra[:, :, :], rb[:, :, :], ALU.add))
                    for r in range(4):
                        decay = k.m8[:, bass.ds(b * GB + d * G + half * 4 + r, 1)].to_broadcast([P, NC])
                        src, out = ra[:, r, :], gr[:, r, :]
                        if d:
                            src, out = src[:, ::-1], out[:, ::-1]
                        last = nc.vector.tensor_tensor_scan(out, decay, src, 0.0, ALU.mult, ALU.add)
                    ch.link(last)
                    off = 1 - d
                    tt(gc[:, q, off:off + NC], gr[:, :, :], cos_t[:, q, :], ALU.mult)
                    tt(gsn[:, q, off:off + NC], gr[:, :, :], sin_t[:, q, :], ALU.mult).then_inc(g_done, 1)
                    dve.wait_ge(g_done, b * 4 + x + 1)
                assert ch.n == LINKS, ch.n
                dve.wait_ge(cleared, b + 1)


def s5_gate(nc, k):
    GELU = 2.0 * math.sqrt(2.0 / math.pi)
    with ExitStack() as ctx:
        sb, ps, sem = makers(nc, ctx, "glu", k.held)
        w = sb("w", [P, 4, D_SSM], f32)
        y = sb("y", [P, 4, SEQ], f32)
        u = sb("u", [P, 4, SEQ], f32)
        a = sb("a", [P, 2, SEQ], f32)
        sg = sb("sg", [P, 4, SEQ], f32)
        skip = sb("skip", [P, 4], f32)
        bg = sb("bg", [P, 4], f32)
        p_z = ps("p_z", [P, 2, SEQ])
        w_in, v_in = sem("w_in"), sem("v_in")
        yu_in = [sem(f"yu_in{m}") for m in range(4)]
        cub, sig, s_done, z_done, z_sig, own = sem("cub"), sem("sig"), sem("s_done"), sem("z_done"), sem("z_sig"), sem("own")
        block = ctx.enter_context(nc.Block())

        @block.sync
        def _(sp):
            for m in range(4):
                rows = slice(m * P, (m + 1) * P)
                sp.dma_start(y[:, m, :], k.ys_d[rows, :]).then_inc(yu_in[m], 16)
                sp.dma_start(u[:, m, :], k.u_d[rows, :]).then_inc(yu_in[m], 16)
                sp.dma_start(skip[:, m:m + 1], k.d_skip[0, rows].rearrange("(p o) -> p o", o=1)).then_inc(v_in, 16)
                sp.dma_start(bg[:, m:m + 1], k.b_glu[0, rows].rearrange("(p o) -> p o", o=1)).then_inc(v_in, 16)
            sp.dma_start(w[:, :, :], k.w_glu[0].rearrange("(k p) n -> p k n", p=P)).then_inc(w_in, 16)

        @block.scalar
        def _(act):
            for m in range(4):
                act.wait_ge(cub, m + 1)
                nc.scalar.activation(sg[:, m, :], a[:, m % 2, :], ACT.Sigmoid, scale=GELU).then_inc(sig, 1)
            for m in range(4):
                act.wait_ge(z_done, 2 * m + 2)
                nc.scalar.activation(sg[:, m, :], p_z[:, m % 2, :], ACT.Sigmoid, bias=bg[:, m:m + 1]).then_inc(z_sig, 1)

        @block.tensor
        def _(pe):
            pe.wait_ge(w_in, 16)
            pe.wait_ge(s_done, 4)
            for m in range(4):
                if m >= 2:
                    pe.wait_ge(z_sig, m - 1)
                for half in range(2):
                    for kk in range(4):
                        last = nc.tensor.matmul(p_z[:, m % 2, half * 512:(half + 1) * 512], w[:, kk, m * P:(m + 1) * P],
                                                k.sT[:, kk, half * 512:(half + 1) * 512], start=(kk == 0), stop=(kk == 3))
                    last.then_inc(z_done, 1)

        @block.vector
        def _(dve):
            ch = Chain(dve, own)
            dve.wait_ge(v_in, 16 * 8)
            for m in range(4):
                dve.wait_ge(yu_in[m], 32)
                ch.link(nc.vector.scalar_tensor_tensor(y[:, m, :], u[:, m, :], skip[:, m:m + 1], y[:, m, :], ALU.mult, ALU.add))
                if m >= 2:
                    dve.wait_ge(sig, m - 1)
                ch.link(nc.vector.tensor_tensor(a[:, m % 2, :], y[:, m, :], y[:, m, :], ALU.mult))
                ch.link(nc.vector.tensor_scalar(a[:, m % 2, :], a[:, m % 2, :], 0.044715, 1.0, ALU.mult, ALU.add))
                nc.vector.tensor_tensor(a[:, m % 2, :], a[:, m % 2, :], y[:, m, :], ALU.mult).then_inc(cub, 1)
                if m:
                    dve.wait_ge(sig, m)
                    nc.vector.tensor_tensor(k.sT[:, m - 1, :], y[:, m - 1, :], sg[:, m - 1, :], ALU.mult).then_inc(s_done, 1)
            dve.wait_ge(sig, 4)
            nc.vector.tensor_tensor(k.sT[:, 3, :], y[:, 3, :], sg[:, 3, :], ALU.mult).then_inc(s_done, 1)
            dve.wait_ge(z_done, 8)
            for m in range(4):
                dve.wait_ge(z_sig, m + 1)
                ch.link(nc.vector.tensor_tensor(k.sT[:, m, :], k.sT[:, m, :], sg[:, m, :], ALU.mult))


def mix_norm_route(nc, k):
    with ExitStack() as ctx:
        sb, ps, sem = makers(nc, ctx, "mix", k.held)
        w_o = sb("w_o", [P, KD, D], f32)
        w_r = sb("w_r", [P, KD, N_EXPERTS], f32)
        w_gu = sb("ws_gu", [P, KD, 2 * F], f32)
        w_dn = sb("ws_dn", [P, KF, D], f32)
        r_bias = sb("r_bias", [P, N_EXPERTS], f32)
        zeros = sb("zeros", [P, D], f32)
        g1 = sb("g1", [P, D], f32)
        b1 = sb("b1", [P, D], f32)
        oT = sb("oT", [P, 2, 4, P], f32)
        r = sb("r", [P, D], f32)
        stats = sb("stats", [P, 2, 6], f32)
        mv = sb("mv", [P, 2, 2], f32)
        std = sb("std", [P, 2], f32)
        rstd = sb("rstd", [P, 1], f32)
        x1T = sb("x1T", [P, 2, KD, P], f32)
        score = sb("score", [P, 2, N_EXPERTS], f32)
        choice = sb("choice", [P, N_EXPERTS], f32)
        top2 = sb("top2", [P, EGROUPS, 8], f32)
        gscore = sb("gscore", [P, EGROUPS], f32)
        gtop = sb("gtop", [P, 8], f32)
        gidx = sb("gidx", [P, 8], u32)
        gidxf = sb("gidxf", [P, 8], f32)
        geq = sb("geq", [P, EGROUPS, TOP_GROUPS], f32)
        gmask = sb("gmask", [P, EGROUPS], f32)
        gneg = sb("gneg", [P, EGROUPS], f32)
        top8 = sb("top8", [P, 8], f32)
        idx8 = sb("idx8", [P, 8], u32)
        hot = sb("hot", [P, TOP_K, N_EXPERTS], f32)
        hots = sb("hots", [P, TOP_K, N_EXPERTS], f32)
        wsum = sb("wsum", [P, 1], f32)
        wrec = sb("wrec", [P, 1], f32)
        member = sb("member", [P, 2, N_EXPERTS], f32)
        seen = sb("seen", [P, 2, N_EXPERTS], f32)
        sig = sb("s_sig", [P, 2, F], f32)
        gs = sb("s_gs", [P, F], f32)
        h = sb("s_h", [P, 2, F], f32)
        hT = sb("s_hT", [P, 2, KF, P], f32)
        p_m = ps("p_m", [P, D])
        p_x = ps("p_x", [P, KD, P])
        p_gu = ps("p_gu", [P, 2 * F])
        p_s = ps("p_s", [P, 512])
        p_y = ps("p_y", [P, D])
        p_log, p_rank, p_h = p_s[:, 0:64], p_s[:, 64:128], p_s[:, 256:512]

        wo_in, wr_in, ws_in, ln_in = sem("wo_in"), sem("wr_in"), sem("ws_in"), sem("ln_in")
        zeroed, y_zeroed = sem("zeroed"), sem("y_zeroed")
        x1_out = [sem(f"x1_out{t}") for t in range(T)]
        o_turned, oT_done, mixed, mix_read = sem("o_turned"), sem("oT_done"), sem("mixed"), sem("mix_read")
        var_done, std_done, x1_done = sem("var_done"), sem("std_done"), sem("x1_done")
        x_turned, xT_dve, xT_act, logits = sem("x_turned"), sem("xT_dve"), sem("xT_act"), sem("logits")
        score_done, member_done, ranked, rank_read = sem("score_done"), sem("member_done"), sem("ranked"), sem("rank_read")
        gu_done, sig_done, h_done, h_turned, hT_done = sem("gu_done"), sem("sig_done"), sem("h_done"), sem("h_turned"), sem("hT_done")
        y_done, y_read, own = sem("y_done"), sem("y_read"), sem("own")
        block = ctx.enter_context(nc.Block())

        @block.sync
        def _(sp):
            sp.dma_start(w_o[:, :, :], k.w_o[0].rearrange("(k p) n -> p k n", p=P)).then_inc(wo_in, 16)
            sp.dma_start(w_r[:, :, :], k.w_router[0].rearrange("(p k) n -> p k n", k=KD)).then_inc(wr_in, 16)
            sp.dma_start(r_bias[:, :], k.router_bias.to_broadcast([P, N_EXPERTS])).then_inc(wr_in, 16)
            sp.dma_start(g1[:, :], k.ln1_g.to_broadcast([P, D])).then_inc(ln_in, 16)
            sp.dma_start(b1[:, :], k.ln1_b.to_broadcast([P, D])).then_inc(ln_in, 16)
            sp.dma_start(w_gu[:, :, 0:F], k.ws_gate[0].rearrange("(p k) n -> p k n", k=KD)).then_inc(ws_in, 16)
            sp.dma_start(w_gu[:, :, F:2 * F], k.ws_up[0].rearrange("(p k) n -> p k n", k=KD)).then_inc(ws_in, 16)
            sp.dma_start(w_dn[:, :, :], k.ws_down[0].rearrange("(p k) n -> p k n", k=KF)).then_inc(ws_in, 16)
            sp.wait_ge(zeroed, 1)
            sp.dma_start(k.y_d[N_EXPERTS * P:SLOTS, :].rearrange("(b p) d -> p b d", p=P),
                         zeros[:, :].unsqueeze(1).to_broadcast([P, OVER, D])).then_inc(y_zeroed, 16)
            for t in range(T):
                sp.wait_ge(x1_done, t + 1)
                sp.dma_start(k.x1_d[t * P:(t + 1) * P, :], k.x[:, t, :]).then_inc(x1_out[t], 16)
            for t in range(T):
                sp.wait_ge(x1_out[t], 16)
            sp.wait_ge(y_zeroed, 16)

        @block.tensor
        def _(pe):
            def mix(t):
                for q in range(4):
                    last = nc.tensor.transpose(p_gu[:, q * P:(q + 1) * P],
                                               k.o[:, t, q * P:(q + 1) * P], k.ident)
                last.then_inc(o_turned, 1)
                if t == 0:
                    pe.wait_ge(wo_in, 16)
                if t >= 1:
                    pe.wait_ge(mix_read, 2 * t)
                for half in range(2):
                    for kk in range(4):
                        nc.tensor.matmul(p_m[:, half * 512:(half + 1) * 512], k.sT[:, kk, t * P:(t + 1) * P],
                                         w_o[:, kk, half * 512:(half + 1) * 512], start=(kk == 0), stop=False)
                    if half == 0:
                        pe.wait_ge(oT_done, t + 1)
                    for kk in range(4):
                        last = nc.tensor.matmul(p_m[:, half * 512:(half + 1) * 512], oT[:, t % 2, kk, :],
                                                w_o[:, 4 + kk, half * 512:(half + 1) * 512],
                                                start=False, stop=(kk == 3))
                    last.then_inc(mixed, 1)

            def turn_x(t):
                pe.wait_ge(x1_done, t + 1)
                for half in range(2):
                    for q in range(4):
                        kk = half * 4 + q
                        last = nc.tensor.transpose(p_x[:, kk, :], k.x[:, t, kk::KD], k.ident)
                    last.then_inc(x_turned, 1)

            def products(t):
                pe.wait_ge(xT_dve, t + 1)
                pe.wait_ge(xT_act, t + 1)
                if t == 0:
                    pe.wait_ge(wr_in, 32)
                    pe.wait_ge(ws_in, 48)
                else:
                    pe.wait_ge(rank_read, t)
                for kk in range(KD):
                    last = nc.tensor.matmul(p_log, x1T[:, t % 2, kk, :], w_r[:, kk, :], start=(kk == 0), stop=(kk == KD - 1))
                last.then_inc(logits, 1)
                for kk in range(KD):
                    last = nc.tensor.matmul(p_gu[:, :], x1T[:, t % 2, kk, :], w_gu[:, kk, :], start=(kk == 0), stop=(kk == KD - 1))
                last.then_inc(gu_done, 1)

            def down(t):
                pe.wait_ge(hT_done, t + 1)
                if t >= 1:
                    pe.wait_ge(y_read, 2 * t)
                for half in range(2):
                    for kk in range(KF):
                        last = nc.tensor.matmul(p_y[:, half * 512:(half + 1) * 512], hT[:, t % 2, kk, :],
                                                w_dn[:, kk, half * 512:(half + 1) * 512], start=(kk == 0), stop=(kk == KF - 1))
                    last.then_inc(y_done, 1)

            def rank_and_turn_h(t):
                pe.wait_ge(member_done, t + 1)
                nc.tensor.matmul(p_rank, k.tri, member[:, t % 2, :], start=True, stop=(t == 0))
                if t:
                    nc.tensor.matmul(p_rank, k.ones, seen[:, t % 2, :], start=False, stop=True)
                pe.wait_ge(h_done, t + 1)
                for kk in range(KF):
                    last = nc.tensor.transpose(p_h[:, kk * P:(kk + 1) * P], h[:, t % 2, kk::KF], k.ident)
                last.then_inc(h_turned, 1)

            mix(0)
            for t in range(T):
                turn_x(t)
                products(t)
                if t >= 1:
                    down(t - 1)
                pe.wait_ge(sig_done, t + 1)
                pe.wait_ge(h_done, t + 1)
                if t + 1 < T:
                    mix(t + 1)
                rank_and_turn_h(t)
            down(T - 1)
            pe.wait_ge(rank_read, T)
            pe.wait_ge(member_done, T + 1)
            nc.tensor.matmul(p_rank, k.ones, seen[:, T % 2, :], start=True, stop=True).then_inc(ranked, 1)

        @block.scalar
        def _(act):
            for t in range(T):
                act.wait_ge(o_turned, t + 1)
                nc.scalar.activation(oT[:, t % 2, :, :].rearrange("p k t -> p (k t)"), p_gu[:, :], ACT.Copy).then_inc(oT_done, 1)
                act.wait_ge(var_done, t + 1)
                nc.scalar.activation(std[:, t % 2:t % 2 + 1], mv[:, t % 2, 1:2], ACT.Sqrt).then_inc(std_done, 1)
                act.wait_ge(x_turned, 2 * t + 2)
                nc.scalar.activation(x1T[:, t % 2, 4:8, :], p_x[:, 4:8, :], ACT.Copy).then_inc(xT_act, 1)
                act.wait_ge(logits, t + 1)
                nc.scalar.activation(score[:, t % 2, :], p_log, ACT.Sigmoid).then_inc(score_done, 1)
                act.wait_ge(gu_done, t + 1)
                nc.scalar.activation(sig[:, t % 2, :], p_gu[:, 0:F], ACT.Sigmoid).then_inc(sig_done, 1)

        @block.vector
        def _(dve):
            ch = Chain(dve, own)

            def norm(t):
                xt = k.x[:, t, :]
                for half in range(2):
                    cols = slice(half * 512, (half + 1) * 512)
                    dve.wait_ge(mixed, 2 * t + half + 1)
                    nc.vector.scalar_tensor_tensor(r[:, cols], k.x[:, t, cols], ALPHA, p_m[:, cols], ALU.mult, ALU.add).then_inc(mix_read, 1)
                dve.wait_ge(mix_read, 2 * t + 2)
                nc.vector.bn_stats(stats[:, 0, :], r[:, 0:512])
                ch.link(nc.vector.bn_stats(stats[:, 1, :], r[:, 512:D]))
                ch.link(nc.vector.bn_aggr(mv[:, t % 2, :], stats[:, :, :].rearrange("p a b -> p (a b)")))
                ch.link(nc.vector.tensor_scalar(mv[:, t % 2, 1:2], mv[:, t % 2, 1:2], LN_EPS, None, ALU.add))
                nc.vector.tensor_copy(rstd[:, :], mv[:, t % 2, 1:2]).then_inc(var_done, 1)
                dve.wait_ge(std_done, t + 1)
                ch.link(nc.vector.reciprocal(rstd[:, :], std[:, t % 2:t % 2 + 1]))
                ch.link(nc.vector.tensor_scalar(r[:, :], r[:, :], mv[:, t % 2, 0:1], rstd[:, 0:1], ALU.subtract, ALU.mult))
                if t == 0:
                    dve.wait_ge(ln_in, 32)
                ch.link(nc.vector.tensor_tensor(r[:, :], r[:, :], g1[:, :], ALU.mult))
                nc.vector.tensor_tensor(xt, r[:, :], b1[:, :], ALU.add).then_inc(x1_done, 1)

            def route(t):
                sc = score[:, t % 2, :]
                dve.wait_ge(score_done, t + 1)
                ch.link(nc.vector.tensor_tensor(choice[:, :], sc, r_bias[:, :], ALU.add))
                for g in range(EGROUPS):
                    last = nc.vector.max(top2[:, g, :], choice[:, g * 8:(g + 1) * 8])
                ch.link(last)
                ch.link(nc.vector.tensor_tensor(gscore[:, :], top2[:, :, 0], top2[:, :, 1], ALU.add))
                ch.link(nc.vector.max(gtop[:, :], gscore[:, :]))
                ch.link(nc.vector.max_index(gidx[:, :], gtop[:, :], gscore[:, :]))
                ch.link(nc.vector.tensor_copy(gidxf[:, :], gidx[:, :]))
                ch.link(nc.vector.tensor_tensor(geq[:, :, :], k.iota_e[:, 0:EGROUPS].unsqueeze(2).to_broadcast([P, EGROUPS, TOP_GROUPS]),
                                                gidxf[:, 0:TOP_GROUPS].unsqueeze(1).to_broadcast([P, EGROUPS, TOP_GROUPS]), ALU.is_equal))
                ch.link(nc.vector.tensor_reduce(gmask[:, :], geq[:, :, :], AX.X, ALU.add))
                ch.link(nc.vector.tensor_scalar(gneg[:, :], gmask[:, :], BIG, -BIG, ALU.mult, ALU.add))
                v3 = choice[:, :].rearrange("p (g e) -> p g e", g=EGROUPS)
                ch.link(nc.vector.tensor_tensor(v3, v3, gmask[:, :].unsqueeze(2).to_broadcast([P, EGROUPS, 8]), ALU.mult))
                ch.link(nc.vector.tensor_tensor(v3, v3, gneg[:, :].unsqueeze(2).to_broadcast([P, EGROUPS, 8]), ALU.add))
                ch.link(nc.vector.max(top8[:, :], choice[:, :]))
                ch.link(nc.vector.max_index(idx8[:, :], top8[:, :], choice[:, :]))
                ch.link(nc.vector.tensor_copy(k.picked[:, t, :], idx8[:, 0:TOP_K]))
                ch.link(nc.vector.tensor_tensor(hot[:, :, :], k.iota_e.unsqueeze(1).to_broadcast([P, TOP_K, N_EXPERTS]),
                                                k.picked[:, t, :].unsqueeze(2).to_broadcast([P, TOP_K, N_EXPERTS]), ALU.is_equal))
                nc.vector.tensor_reduce(member[:, t % 2, :], hot[:, :, :].rearrange("p k e -> p e k"), AX.X, ALU.add).then_inc(member_done, 1)
                ch.link(nc.vector.tensor_tensor(hots[:, :, :], hot[:, :, :], sc.unsqueeze(1).to_broadcast([P, TOP_K, N_EXPERTS]), ALU.mult))
                ch.link(nc.vector.tensor_reduce(k.top_w[:, t, :], hots[:, :, :], AX.X, ALU.add))
                ch.link(nc.vector.tensor_reduce(wsum[:, :], k.top_w[:, t, :], AX.X, ALU.add))
                ch.link(nc.vector.tensor_scalar(wsum[:, :], wsum[:, :], 1e-20, None, ALU.add))
                ch.link(nc.vector.reciprocal(wrec[:, :], wsum[:, :]))
                ch.link(nc.vector.tensor_scalar(k.top_w[:, t, :], k.top_w[:, t, :], wrec[:, 0:1], ROUTED_SCALE, ALU.mult, ALU.mult))

            def hidden(t):
                dve.wait_ge(sig_done, t + 1)
                ch.link(nc.vector.tensor_tensor(gs[:, :], sig[:, t % 2, :], p_gu[:, 0:F], ALU.mult))
                nc.vector.tensor_tensor(h[:, t % 2, :], gs[:, :], p_gu[:, F:2 * F], ALU.mult).then_inc(h_done, 1)

            def add_shared(t):
                for half in range(2):
                    cols = slice(half * 512, (half + 1) * 512)
                    dve.wait_ge(y_done, 2 * t + half + 1)
                    nc.vector.scalar_tensor_tensor(k.x[:, t, cols], k.x[:, t, cols], ALPHA, p_y[:, cols], ALU.mult, ALU.add).then_inc(y_read, 1)

            nc.vector.memset(zeros[:, :], 0.0).then_inc(zeroed, 1)
            norm(0)
            for t in range(T):
                dve.wait_ge(x_turned, 2 * t + 1)
                nc.vector.tensor_copy(x1T[:, t % 2, 0:4, :], p_x[:, 0:4, :]).then_inc(xT_dve, 1)
                hidden(t)
                route(t)
                if t >= 1:
                    dve.wait_ge(x1_out[t - 1], 16)
                    add_shared(t - 1)
                dve.wait_ge(h_turned, t + 1)
                nc.vector.tensor_copy(hT[:, t % 2, :, :].rearrange("p k t -> p (k t)"), p_h).then_inc(hT_done, 1)
                nc.vector.tensor_copy(k.rank[:, t, :], p_rank).then_inc(rank_read, 1)
                if t == 0:
                    ch.link(nc.vector.tensor_copy(seen[:, 1, :], member[:, 0, :]))
                else:
                    ch.link(nc.vector.tensor_tensor(seen[:, (t + 1) % 2, :], seen[:, t % 2, :], member[:, t % 2, :], ALU.add))
                if t + 1 < T:
                    norm(t + 1)
            nc.vector.tensor_copy(choice[:, :], member[:, 1, :]).then_inc(member_done, 1)
            dve.wait_ge(x1_out[T - 1], 16)
            add_shared(T - 1)
            dve.wait_ge(ranked, 1)
            ch.link(nc.vector.tensor_copy(k.counts[:, :], p_rank))


def dispatch(nc, k):
    E = N_EXPERTS
    with ExitStack() as ctx:
        sb, ps, sem = makers(nc, ctx, "disp", k.held)
        over = sb("over", [P, E], f32)
        over_end = sb("over_end", [P, E], f32)
        base = sb("base", [P, E], f32)
        far = sb("far", [P, T, E], f32)
        slot = sb("slot", [P, T, E], f32)
        hot = sb("d_hot", [P, TOP_K, E], f32)
        dest = sb("dest", [P, T, TOP_K], f32)
        le = sb("le", [P, E], f32)
        expert_f = sb("expert_f", [P, 2], f32)
        expert_i = sb("expert_i", [P, 2], i32)
        zero = sb("zero", [E + OVER, P], f32)
        toks = sb("toks", [E + OVER, P], f32)
        p_t = ps("p_t", [P, P])
        own, dest_done, zeroed, zeroed_d = sem("d_own"), sem("dest_done"), sem("zeroed"), sem("zeroed_d")
        scattered, toks_in, toks_turned = sem("scattered"), sem("toks_in"), sem("toks_turned")
        expert_done, expert_d, expert_in = sem("expert_done"), sem("expert_d"), sem("expert_in")
        block = ctx.enter_context(nc.Block())

        @block.vector
        def _(dve):
            ch = Chain(dve, own)
            nc.vector.memset(zero[:, :], 0.0).then_inc(zeroed, 1)
            ch.link(nc.vector.tensor_scalar(over[:, :], k.counts[:, :], float(P), None, ALU.is_gt))
            for m in range(2, SEQ // P):
                ch.link(nc.vector.scalar_tensor_tensor(over[:, :], k.counts[:, :], float(P * m), over[:, :], ALU.is_gt, ALU.add))
            ch.link(nc.vector.tensor_tensor_scan(over_end[:, :], k.ones[:, 0:E], over[:, :], 0.0, ALU.mult, ALU.add))
            ch.link(nc.vector.tensor_scalar(le[:, :], over_end[:, :], k.part, None, ALU.is_le))
            ch.link(nc.vector.tensor_reduce(expert_f[:, 0:1], le[:, :], AX.X, ALU.add))
            ch.link(nc.vector.tensor_scalar(expert_f[:, 0:1], expert_f[:, 0:1], float(E - 1), None, ALU.min))
            ch.link(nc.vector.tensor_copy(expert_f[:, 1:2], over_end[:, E - 1:E]))
            ch.link(nc.vector.tensor_copy(k.n_over[0:1, 0:1], expert_f[0:1, 1:2]))
            nc.vector.tensor_copy(expert_i[:, :], expert_f[:, :]).then_inc(expert_done, 1)
            ch.link(nc.vector.tensor_tensor(base[:, :], over_end[:, :], over[:, :], ALU.subtract))
            ch.link(nc.vector.tensor_scalar(base[:, :], base[:, :], float(P), float(P * E - P), ALU.mult, ALU.add))
            ch.link(nc.vector.tensor_tensor(base[:, :], base[:, :], k.iota_e128, ALU.subtract))
            wide = [P, T, E]
            ch.link(nc.vector.tensor_scalar(far[:, :, :], k.rank[:, :, :], float(P), None, ALU.is_ge))
            ch.link(nc.vector.tensor_tensor(far[:, :, :], far[:, :, :], base[:, :].unsqueeze(1).to_broadcast(wide), ALU.mult))
            ch.link(nc.vector.tensor_tensor(slot[:, :, :], k.rank[:, :, :], k.iota_e128.unsqueeze(1).to_broadcast(wide), ALU.add))
            ch.link(nc.vector.tensor_tensor(slot[:, :, :], slot[:, :, :], far[:, :, :], ALU.add))
            many = [P, TOP_K, E]
            for t in range(T):
                ch.link(nc.vector.tensor_tensor(hot[:, :, :], k.iota_e.unsqueeze(1).to_broadcast(many),
                                                k.picked[:, t, :].unsqueeze(2).to_broadcast(many), ALU.is_equal))
                ch.link(nc.vector.tensor_tensor(hot[:, :, :], hot[:, :, :], slot[:, t, :].unsqueeze(1).to_broadcast(many), ALU.mult))
                ch.link(nc.vector.tensor_reduce(dest[:, t, :], hot[:, :, :], AX.X, ALU.add))
                nc.vector.tensor_copy(k.dest[:, t * TOP_K:(t + 1) * TOP_K], dest[:, t, :]).then_inc(dest_done, 1)
            dve.wait_ge(toks_turned, 1)
            nc.vector.tensor_copy(k.block_tok[:, :], p_t[:, 0:E + OVER])

        @block.gpsimd
        def _(pool):
            pool.wait_ge(zeroed_d, 16)
            for t in range(T):
                pool.wait_ge(dest_done, t + 1)
                for q in range(TOP_K):
                    nc.gpsimd.indirect_dma_start(k.slot_tok_d[:, :],
                                                 bass.IndirectOffsetOnAxis(ap=k.dest[:, t * TOP_K + q:t * TOP_K + q + 1], axis=0),
                                                 k.tok[:, t:t + 1], None).then_inc(scattered, 16)

        @block.sync
        def _(sp):
            sp.wait_ge(zeroed, 1)
            sp.dma_start(k.slot_tok_d.rearrange("(b s) o -> b (s o)", s=P), zero[:, :]).then_inc(zeroed_d, 16)
            sp.wait_ge(expert_done, 1)
            sp.dma_start(k.expert_d.rearrange("(p o) -> p o", o=1), expert_i[:, 0:1]).then_inc(expert_d, 16)
            sp.wait_ge(expert_d, 16)
            sp.dma_start(k.over_expert[0:1, :], k.expert_d[0:OVER].rearrange("(o p) -> o p", o=1)).then_inc(expert_in, 16)
            sp.wait_ge(scattered, 16 * T * TOP_K)
            sp.dma_start(toks[:, :], k.slot_tok_d.rearrange("(b s) o -> b (s o)", s=P)).then_inc(toks_in, 16)
            sp.wait_ge(expert_in, 16)

        @block.tensor
        def _(pe):
            pe.wait_ge(toks_in, 16)
            nc.tensor.transpose(p_t[:, 0:E + OVER], toks[:, :], k.ident[0:E + OVER, 0:E + OVER]).then_inc(toks_turned, 1)



def moe_experts(nc, k):
    E = N_EXPERTS
    wg = k.we_gate[0].rearrange("e (p k) f -> e p k f", k=KD)
    wu = k.we_up[0].rearrange("e (p k) f -> e p k f", k=KD)
    wd = k.we_down[0].rearrange("e (p k) n -> e p k n", k=KF)
    with ExitStack() as ctx:
        sb, ps, sem = makers(nc, ctx, "moe", k.held)
        w_gu = sb("w_gu", [P, 2, KD, 2 * F], f32)
        w_dn = sb("w_dn", [P, 2, KF, D], f32)
        xg = sb("xg", [P, 2, D], f32)
        xgT = sb("xgT", [P, 2, KD, P], f32)
        sig = sb("sig", [P, 2, F], f32)
        gs = sb("gs", [P, 2, F], f32)
        h = sb("h", [P, 2, F], f32)
        hT = sb("hT", [P, 2, KF, P], f32)
        y = sb("y", [P, 2, D], f32)
        idx = sb("idx", [P, 2], i32)
        p_x = ps("p_x", [P, KD, P])
        p_gu = ps("p_gu", [P, 2, 2 * F])
        p_h = ps("p_h", [P, 512])
        p_y = ps("p_y", [P, D])

        wgu_in = [sem(f"wgu_in{u}") for u in range(2)]
        wdn_in = [sem(f"wdn_in{u}") for u in range(2)]
        xg_in = [sem(f"xg_in{u}") for u in range(2)]
        y_out = [sem(f"y_out{u}") for u in range(2)]
        x_turned = sem("x_turned")
        gu_done = sem("gu_done")
        h_turned = sem("h_turned")
        y_done = sem("y_done")
        xT_dve = sem("xT_dve")
        xT_act = sem("xT_act")
        sig_done = sem("sig_done")
        gs_done = sem("gs_done")
        h_done = sem("h_done")
        hT_done = sem("hT_done")
        y_dve = sem("y_dve")
        y_act = sem("y_act")
        idx_done = sem("idx_done")
        idx_seen = sem("idx_seen")
        all_out = sem("all_out")
        block = ctx.enter_context(nc.Block())

        @block.sync
        def _(sp):
            def load_gu(e, u, expert):
                sp.dma_start(w_gu[:, u, :, 0:F], wg[bass.ds(expert, 1)].rearrange("e p k f -> (e p) k f")).then_inc(wgu_in[u], 16)
                sp.dma_start(w_gu[:, u, :, F:2 * F], wu[bass.ds(expert, 1)].rearrange("e p k f -> (e p) k f")).then_inc(wgu_in[u], 16)

            def load_dn(e, u, expert):
                sp.dma_start(w_dn[:, u], wd[bass.ds(expert, 1)].rearrange("e p k n -> (e p) k n")).then_inc(wdn_in[u], 16)

            for e in range(2):
                load_gu(e, e, e)
                load_dn(e, e, e)
            with sp.Fori(1, E // 2) as ee:
                for u in range(2):
                    e = ee * 2 + u
                    sp.wait_ge(gu_done, e - 1)
                    load_gu(e, u, e)
                    sp.wait_ge(y_done, e * 2 - 2)
                    load_dn(e, u, e)
            n_over = sp.value_load(k.n_over[0:1, 0:1], min_val=0, max_val=OVER)
            with sp.Fori(0, OVER // 2) as jj:
                for u in range(2):
                    j = jj * 2 + u
                    with sp.If(n_over > j):
                        expert = sp.value_load(k.over_expert[0:1, bass.ds(j, 1)], min_val=0, max_val=E - 1)
                        sp.wait_ge(gu_done, j + (E - 1))
                        load_gu(j + E, u, expert)
                        sp.wait_ge(y_done, j * 2 + (2 * E - 2))
                        load_dn(j + E, u, expert)

        @block.gpsimd
        def _(pool):
            def gather(e, u):
                nc.gpsimd.tensor_copy(idx[:, u:u + 1], k.block_tok[:, bass.ds(e, 1)]).then_inc(idx_done, 1)
                pool.wait_ge(idx_done, e + 1)
                pool.sem_inc(idx_seen, 1)
                nc.gpsimd.indirect_dma_start(xg[:, u, :], None, k.x1_d[:, :],
                                             bass.IndirectOffsetOnAxis(ap=idx[:, u:u + 1], axis=0)).then_inc(xg_in[u], 16)

            for e in range(2):
                gather(e, e)
            with pool.Fori(1, E // 2) as ee:
                for u in range(2):
                    e = ee * 2 + u
                    pool.wait_ge(x_turned, e * 2 - 2)
                    gather(e, u)
            n_over = pool.value_load(k.n_over[0:1, 0:1], min_val=0, max_val=OVER)
            with pool.Fori(0, OVER // 2) as jj:
                for u in range(2):
                    j = jj * 2 + u
                    with pool.If(n_over > j):
                        pool.wait_ge(x_turned, j * 2 + (2 * E - 2))
                        gather(j + E, u)

        @block.tensor
        def _(pe):
            def turn_x(e, u, n):
                pe.wait_ge(xg_in[u], n)
                for half in range(2):
                    for q in range(4):
                        kk = half * 4 + q
                        last = nc.tensor.transpose(p_x[:, kk, :], xg[:, u, kk::KD], k.ident)
                    last.then_inc(x_turned, 1)

            def gate_up(e, u, n):
                pe.wait_ge(xT_dve, e + 1)
                pe.wait_ge(xT_act, e + 1)
                pe.wait_ge(wgu_in[u], n)
                for kk in range(KD):
                    last = nc.tensor.matmul(p_gu[:, u, :], xgT[:, u, kk, :], w_gu[:, u, kk, :],
                                            start=(kk == 0), stop=(kk == KD - 1))
                last.then_inc(gu_done, 1)

            def turn_h(e, u):
                pe.wait_ge(h_done, e + 1)
                for kk in range(KF):
                    last = nc.tensor.transpose(p_h[:, kk * P:(kk + 1) * P], h[:, u, kk::KF], k.ident)
                last.then_inc(h_turned, 1)

            def down(e, u, n, first=False):
                pe.wait_ge(hT_done, e + 1)
                pe.wait_ge(wdn_in[u], n)
                if not first:
                    pe.wait_ge(y_dve, e)
                    pe.wait_ge(y_act, e)
                for half in range(2):
                    for kk in range(KF):
                        last = nc.tensor.matmul(p_y[:, half * 512:(half + 1) * 512], hT[:, u, kk, :],
                                                w_dn[:, u, kk, half * 512:(half + 1) * 512],
                                                start=(kk == 0), stop=(kk == KF - 1))
                    last.then_inc(y_done, 1)

            turn_x(0, 0, 16)
            gate_up(0, 0, 32)
            turn_x(1, 1, 16)
            turn_h(0, 0)
            gate_up(1, 1, 32)
            down(0, 0, 16, first=True)
            turn_x(2, 0, 32)
            turn_h(1, 1)
            with pe.Fori(0, (E - 4) // 2) as ii:
                for u in range(2):
                    i = ii * 2 + (u + 1)
                    a, b = (u + 1) % 2, u
                    gate_up(i + 1, b, ii * 32 + 64)
                    down(i, a, ii * 16 + 16 * (1 + u))
                    turn_x(i + 2, a, ii * 16 + 16 * (2 + u))
                    turn_h(i + 1, b)
            i = E - 3
            gate_up(i + 1, 0, 32 * (E // 2))
            down(i, 1, 16 * (E // 2 - 1))
            turn_x(i + 2, 1, 16 * (E // 2))
            turn_h(i + 1, 0)
            gate_up(E - 1, 1, 32 * (E // 2))
            down(E - 2, 0, 16 * (E // 2))
            turn_h(E - 1, 1)
            down(E - 1, 1, 16 * (E // 2))
            n_over = pe.value_load(k.n_over[0:1, 0:1], min_val=0, max_val=OVER)
            with pe.Fori(0, OVER // 2) as jj:
                for u in range(2):
                    j = jj * 2 + u
                    with pe.If(n_over > j):
                        turn_x(j + E, u, jj * 16 + 16 * (E // 2 + 1))
                        gate_up(j + E, u, jj * 32 + 32 * (E // 2 + 1))
                        turn_h(j + E, u)
                        down(j + E, u, jj * 16 + 16 * (E // 2 + 1))

        @block.scalar
        def _(act):
            def keep_xT(e, u):
                act.wait_ge(x_turned, e * 2 + 2)
                nc.scalar.activation(xgT[:, u, 4:8, :], p_x[:, 4:8, :], ACT.Copy).then_inc(xT_act, 1)

            def gate(e, u):
                act.wait_ge(gu_done, e + 1)
                nc.scalar.activation(sig[:, u, :], p_gu[:, u, 0:F], ACT.Sigmoid).then_inc(sig_done, 1)

            def keep_y(e, u, n):
                act.wait_ge(y_done, e * 2 + 1)
                if n is not None:
                    act.wait_ge(y_out[u], n)
                nc.scalar.activation(y[:, u, 0:512], p_y[:, 0:512], ACT.Copy).then_inc(y_act, 1)
                act.wait_ge(y_act, e + 1)
                act.wait_ge(y_dve, e + 1)
                act.dma_start(k.y_d[bass.ds(e * P, P), :], y[:, u, :]).then_inc(y_out[u], 16)

            keep_xT(0, 0)
            gate(0, 0)
            keep_xT(1, 1)
            gate(1, 1)
            keep_y(0, 0, None)
            keep_xT(2, 0)
            gate(2, 0)
            keep_y(1, 1, None)
            keep_xT(3, 1)
            with act.Fori(1, E // 2 - 1) as ii:
                for u in range(2):
                    i = ii * 2 + u
                    gate(i + 1, 1 - u)
                    keep_y(i, u, ii * 16)
                    keep_xT(i + 2, u)
            gate(E - 1, 1)
            keep_y(E - 2, 0, 16 * (E // 2 - 1))
            keep_y(E - 1, 1, 16 * (E // 2 - 1))
            n_over = act.value_load(k.n_over[0:1, 0:1], min_val=0, max_val=OVER)
            with act.Fori(0, OVER // 2) as jj:
                for u in range(2):
                    j = jj * 2 + u
                    with act.If(n_over > j):
                        keep_xT(j + E, u)
                        gate(j + E, u)
                        keep_y(j + E, u, jj * 16 + 16 * (E // 2))
            for u in range(2):
                act.wait_ge(y_out[u], (n_over + (1 - u)) // 2 * 16 + 16 * (E // 2))
                act.sem_inc(all_out, 1)

        @block.vector
        def _(dve):
            def keep_xT(e, u):
                dve.wait_ge(x_turned, e * 2 + 1)
                nc.vector.tensor_copy(xgT[:, u, 0:4, :], p_x[:, 0:4, :]).then_inc(xT_dve, 1)

            def hidden(e, u):
                dve.wait_ge(sig_done, e + 1)
                nc.vector.tensor_tensor(gs[:, u, :], sig[:, u, :], p_gu[:, u, 0:F], ALU.mult).then_inc(gs_done, 1)
                dve.wait_ge(gs_done, e + 1)
                nc.vector.tensor_tensor(h[:, u, :], gs[:, u, :], p_gu[:, u, F:2 * F], ALU.mult).then_inc(h_done, 1)

            def keep_hT(e, u):
                dve.wait_ge(h_turned, e + 1)
                nc.vector.tensor_copy(hT[:, u, :, :].rearrange("p k t -> p (k t)"), p_h[:, 0:KF * P]).then_inc(hT_done, 1)

            def keep_y(e, u, n):
                dve.wait_ge(y_done, e * 2 + 2)
                if n is not None:
                    dve.wait_ge(y_out[u], n)
                nc.vector.tensor_copy(y[:, u, 512:D], p_y[:, 512:D]).then_inc(y_dve, 1)

            keep_xT(0, 0)
            hidden(0, 0)
            keep_xT(1, 1)
            keep_hT(0, 0)
            hidden(1, 1)
            keep_y(0, 0, None)
            keep_xT(2, 0)
            keep_hT(1, 1)
            hidden(2, 0)
            keep_y(1, 1, None)
            keep_xT(3, 1)
            keep_hT(2, 0)
            with dve.Fori(1, E // 2 - 1) as ii:
                for u in range(2):
                    i = ii * 2 + u
                    hidden(i + 1, 1 - u)
                    keep_y(i, u, ii * 16)
                    keep_xT(i + 2, u)
                    keep_hT(i + 1, 1 - u)
            hidden(E - 1, 1)
            keep_y(E - 2, 0, 16 * (E // 2 - 1))
            keep_hT(E - 1, 1)
            keep_y(E - 1, 1, 16 * (E // 2 - 1))
            n_over = dve.value_load(k.n_over[0:1, 0:1], min_val=0, max_val=OVER)
            with dve.Fori(0, OVER // 2) as jj:
                for u in range(2):
                    j = jj * 2 + u
                    with dve.If(n_over > j):
                        keep_xT(j + E, u)
                        hidden(j + E, u)
                        keep_hT(j + E, u)
                        keep_y(j + E, u, jj * 16 + 16 * (E // 2))


def combine(nc, k):
    with ExitStack() as ctx:
        sb, ps, sem = makers(nc, ctx, "comb", k.held)
        g2 = sb("g2", [P, D], f32)
        b2 = sb("b2", [P, D], f32)
        NB = 4
        yb = sb("yb", [P, NB, D], f32)
        stats = sb("stats2", [P, 2, 6], f32)
        mv = sb("mv2", [P, 2, 2], f32)
        std = sb("std2", [P, 2], f32)
        rstd = sb("rstd2", [P, 1], f32)
        ln_in, own, var_done, std_done, out_done, out_sent = sem("ln2_in"), sem("c_own"), sem("var2"), sem("std2s"), sem("out_done"), sem("out_sent")
        y_in = [sem(f"y_in{b}") for b in range(NB)]
        y_used = sem("y_used")
        block = ctx.enter_context(nc.Block())

        @block.sync
        def _(sp):
            sp.dma_start(g2[:, :], k.ln2_g.to_broadcast([P, D])).then_inc(ln_in, 16)
            sp.dma_start(b2[:, :], k.ln2_b.to_broadcast([P, D])).then_inc(ln_in, 16)
            out = k.out[0].rearrange("(c j) d -> j c d", j=T)
            for t in range(T):
                sp.wait_ge(out_done, t + 1)
                sp.dma_start(out[t], k.x[:, t, :]).then_inc(out_sent, 16)
            sp.wait_ge(out_sent, 16 * T)

        @block.gpsimd
        def _(pool):
            for n in range(T * TOP_K):
                if n >= NB:
                    pool.wait_ge(y_used, n - NB + 1)
                nc.gpsimd.indirect_dma_start(yb[:, n % NB, :], None, k.y_d[:, :],
                                             bass.IndirectOffsetOnAxis(ap=k.dest[:, n:n + 1], axis=0)).then_inc(y_in[n % NB], 16)

        @block.scalar
        def _(act):
            for t in range(T):
                act.wait_ge(var_done, t + 1)
                nc.scalar.activation(std[:, t % 2:t % 2 + 1], mv[:, t % 2, 1:2], ACT.Sqrt).then_inc(std_done, 1)

        @block.vector
        def _(dve):
            ch = Chain(dve, own)
            for t in range(T):
                xt = k.x[:, t, :]
                for q in range(TOP_K):
                    n = t * TOP_K + q
                    dve.wait_ge(y_in[n % NB], 16 * (n // NB + 1))
                    if n:
                        dve.wait_ge(y_used, n)
                    nc.vector.scalar_tensor_tensor(xt, yb[:, n % NB, :], k.top_w[:, t, q:q + 1], xt, ALU.mult, ALU.add).then_inc(y_used, 1)
                dve.wait_ge(y_used, n + 1)
                nc.vector.bn_stats(stats[:, 0, :], k.x[:, t, 0:512])
                ch.link(nc.vector.bn_stats(stats[:, 1, :], k.x[:, t, 512:D]))
                ch.link(nc.vector.bn_aggr(mv[:, t % 2, :], stats[:, :, :].rearrange("p a b -> p (a b)")))
                nc.vector.tensor_scalar(mv[:, t % 2, 1:2], mv[:, t % 2, 1:2], LN_EPS, None, ALU.add).then_inc(var_done, 1)
                dve.wait_ge(std_done, t + 1)
                ch.link(nc.vector.reciprocal(rstd[:, :], std[:, t % 2:t % 2 + 1]))
                ch.link(nc.vector.tensor_scalar(xt, xt, mv[:, t % 2, 0:1], rstd[:, 0:1], ALU.subtract, ALU.mult))
                if t == 0:
                    dve.wait_ge(ln_in, 32)
                ch.link(nc.vector.tensor_tensor(xt, xt, g2[:, :], ALU.mult))
                nc.vector.tensor_tensor(xt, xt, b2[:, :], ALU.add).then_inc(out_done, 1)


def build(nc, k):
    with ExitStack() as ctx:
        k.held = []
        persistent(nc, ctx, k)
        with ExitStack() as mixers:
            mixer_tile, _, _ = makers(nc, mixers, "mixers")
            k.o = mixer_tile("o", [P, T, 512], f32)
            with ExitStack() as latents:
                sb, _, _ = makers(nc, latents, "latents")
                k.cqT = sb("cqT", [P, 2, SEQ], f32)
                k.ckvT = sb("ckvT", [P, SEQ], f32)
                k.kT = sb("kT", [DQ, 2, SEQ], f32)
                project(nc, k)
                attention(nc, k)
            with ExitStack() as states:
                sb, _, _ = makers(nc, states, "states")
                k.b1, k.b2, k.c1, k.c2, k.e1, k.f2 = [sb(n, [P, 2 * G, CH], f32) for n in ("b1", "b2", "c1", "c2", "e1", "f2")]
                k.pw = sb("pw", [P, 2, 2 * G, T + 1], f32)
                k.pb = sb("pb", [P, 2, 2 * G, T + 1], f32)
                k.t8 = sb("t8", [P, 2 * G], f32)
                k.m8 = sb("m8", [P, 2 * G], f32)
                s5_parameters(nc, k)
                s5_scan(nc, k)
            k.sT = mixer_tile("sT", [P, 4, SEQ], f32)
            s5_gate(nc, k)
            hand_back(nc, k.held)
            mix_norm_route(nc, k)
        dispatch(nc, k)
        moe_experts(nc, k)
        combine(nc, k)


_INS = ['x', 'w_in', 'lam_re', 'lam_im', 'log_dt', 'b_re', 'b_im', 'c_re', 'c_im', 'd_skip', 'w_glu', 'b_glu',
        'q_norm_g', 'w_uq', 'kv_norm_g', 'w_ukv', 'w_o', 'ln1_g', 'ln1_b', 'w_router', 'router_bias',
        'we_gate', 'we_up', 'we_down', 'ws_gate', 'ws_up', 'ws_down', 'ln2_g', 'ln2_b']


def kernel(**inputs):
    import numpy as _np
    import concourse.bacc as _bacc
    from concourse.bass_utils import run_bass_kernel_spmd as _run

    nc = _bacc.Bacc("TRN2", target_bir_lowering=False, num_devices=1)
    arrays, aps = {}, {}
    for name in _INS:
        a = _np.ascontiguousarray(inputs[name])
        arrays[f"in_{name}_dram"] = a
        aps[name] = nc.dram_tensor(f"in_{name}_dram", a.shape, mybir.dt.from_np(a.dtype), kind="ExternalInput").ap()
    c = constants()
    arrays["in_consts_dram"] = c
    aps["consts"] = nc.dram_tensor("in_consts_dram", c.shape, f32, kind="ExternalInput").ap()
    aps["out"] = nc.dram_tensor("out_0_dram", (1, SEQ, D), f32, kind="ExternalOutput").ap()
    build(nc, Kit(aps))
    r = _run(nc, [arrays], core_ids=[0])
    return r.results[0]["out_0_dram"]
```

```python
import math
from contextlib import ExitStack

import concourse.bass as bass
from concourse import mybir

f32 = mybir.dt.float32
i32 = mybir.dt.int32
u32 = mybir.dt.uint32
ALU = mybir.AluOpType
ACT = mybir.ActivationFunctionType
AX = mybir.AxisListType

P = 128
D = 1024
SEQ = 1024
T = 8
NC = SEQ // T
KD = D // P
D_SSM = 512
G = 32
CH = 16
N = 64
Q_RANK = 256
KV_RANK = 128
HEADS = 8
NOPE = 64
ROPE = 32
DQ = NOPE + ROPE
DV = 64
N_EXPERTS = 64
TOP_K = 6
EGROUPS = 8
TOP_GROUPS = 4
F = 256
KF = F // P
RING = 4
EARLY = 3
OVER = SEQ * TOP_K // P
SLOTS = (N_EXPERTS + OVER) * P
ROUTED_SCALE = 2.5
ALPHA = 2.0 ** 0.25
LN_EPS = 1e-5
RMS_EPS = 1e-6
BIG = 1e30
TWO_PI = 2.0 * math.pi
ROUND = 1.5 * 2.0 ** 23


def makers(nc, ctx, stage, held=None, side=None):
    def sb(name, shape, dt):
        return ctx.enter_context(nc.sbuf_tensor(f"{stage}_{name}", shape, dt, side=side))

    def ps(name, shape):
        return ctx.enter_context(nc.psum_tensor(f"{stage}_{name}", shape, f32))

    def sem(name):
        held.append(nc.alloc_semaphore(name=f"{stage}_{name}"))
        return held[-1]
    return sb, ps, sem


def hand_back(nc, held):
    nc.all_engine_barrier()
    nc.clear_and_free_semaphores(held)
    nc.all_engine_barrier()
    held.clear()


class Kit:

    def __init__(self, given):
        self.x_in = given["x"]
        self.w_in, self.lam_re, self.lam_im, self.log_dt = [given[n] for n in ("w_in", "lam_re", "lam_im", "log_dt")]
        self.b_re, self.b_im, self.c_re, self.c_im = [given[n] for n in ("b_re", "b_im", "c_re", "c_im")]
        self.d_skip, self.w_glu, self.b_glu, self.q_norm_g = [given[n] for n in ("d_skip", "w_glu", "b_glu", "q_norm_g")]
        self.w_uq, self.kv_norm_g, self.w_ukv, self.w_o = [given[n] for n in ("w_uq", "kv_norm_g", "w_ukv", "w_o")]
        self.ln1_g, self.ln1_b, self.w_router, self.router_bias = [given[n] for n in ("ln1_g", "ln1_b", "w_router", "router_bias")]
        self.we_gate, self.we_up, self.we_down, self.ws_gate = [given[n] for n in ("we_gate", "we_up", "we_down", "ws_gate")]
        self.ws_up, self.ws_down, self.ln2_g, self.ln2_b = [given[n] for n in ("ws_up", "ws_down", "ln2_g", "ln2_b")]
        self.consts, self.out = [given[n] for n in ("consts", "out")]


class Chain:

    def __init__(self, eng, sem, base=0):
        self.eng, self.sem, self.base, self.n = eng, sem, base, 0

    def link(self, ins):
        self.n += 1
        ins.then_inc(self.sem, 1)
        self.eng.wait_ge(self.sem, self.base + self.n)


C_ID, C_TRI, C_ONE, C_CHUNK, C_CHUNKR, C_COS, C_SIN, C_E, C_E128, C_TOK, C_PART, C_SGN, C_END = [
    0, 128, 256, 384, 512, 640, 768, 896, 960, 1024, 1032, 1033, 1036]


def constants():
    import numpy as np
    c = np.zeros((P, C_END), np.float32)
    p = np.arange(P)
    c[:, C_ID:C_ID + P] = np.eye(P)
    c[:, C_TRI:C_TRI + P] = p[:, None] < p[None, :]
    c[:, C_ONE:C_ONE + P] = 1.0
    c[:, C_CHUNK:C_CHUNK + P] = p[None, :]
    c[:, C_CHUNKR:C_CHUNKR + P] = P - 1 - p[None, :]
    inv = (np.float32(10000.0) ** (-np.arange(0, ROPE, 2, dtype=np.float32) / np.float32(ROPE))).astype(np.float32)
    pos = (T * p[:, None] + np.arange(T)[None, :]).astype(np.float32)
    ang = (pos[:, :, None] * inv[None, None, :]).astype(np.float32).astype(np.float64)
    c[:, C_COS:C_COS + P] = np.cos(ang).reshape(P, P)
    c[:, C_SIN:C_SIN + P] = np.sin(ang).reshape(P, P)
    c[:, C_E:C_E + N_EXPERTS] = np.arange(N_EXPERTS)[None, :]
    c[:, C_E128:C_E128 + N_EXPERTS] = P * np.arange(N_EXPERTS)[None, :]
    c[:, C_TOK:C_TOK + T] = p[:, None] + P * np.arange(T)[None, :]
    c[:, C_PART] = p
    c[:, C_SGN] = np.where(p < N, 1.0, -1.0)
    c[:, C_SGN + 2] = math.pi / 2
    c[:, C_SGN + 1] = np.float32(6.2831850) * c[:, C_SGN]
    return c


def persistent(nc, ctx, k):
    sb, _, _ = makers(nc, ctx, "all")
    const = sb("const", [P, C_END], f32)
    k.const = const
    k.ident = const[:, C_ID:C_ID + P]
    k.tri = const[:, C_TRI:C_TRI + P]
    k.ones = const[:, C_ONE:C_ONE + P]
    k.iota_e = const[:, C_E:C_E + N_EXPERTS]
    k.iota_e128 = const[:, C_E128:C_E128 + N_EXPERTS]
    k.tok = const[:, C_TOK:C_TOK + T]
    k.cos = const[:, C_COS:C_COS + P].rearrange("p (t f) -> p t f", t=T)
    k.sin = const[:, C_SIN:C_SIN + P].rearrange("p (t f) -> p t f", t=T)
    k.chunk = const[:, C_CHUNK:C_CHUNK + NC]
    k.chunkr = const[:, C_CHUNKR:C_CHUNKR + NC]
    k.sgn = const[:, C_SGN:C_SGN + 1]
    k.sgn2pi = const[:, C_SGN + 1:C_SGN + 2]
    k.half_pi = const[:, C_SGN + 2:C_SGN + 3]
    k.part = const[:, C_PART:C_PART + 1]
    k.x = sb("x_sb", [P, T, D], f32)
    k.rank = sb("rank", [P, T, N_EXPERTS], f32)
    k.counts = sb("counts", [P, N_EXPERTS], f32)
    k.picked = sb("picked", [P, T, TOP_K], f32)
    k.top_w = sb("top_w", [P, T, TOP_K], f32)
    k.dest = sb("dest_i", [P, T * TOP_K], i32)
    k.block_tok = sb("block_tok", [P, N_EXPERTS + OVER], i32)
    k.over_expert = sb("over_expert", [1, OVER], i32)
    k.n_over = sb("n_over", [1, 1], i32)
    k.x1_d = nc.dram_tensor("x1_d", (SEQ, D), f32).ap()
    k.y_d = nc.dram_tensor("y_d", (SLOTS, D), f32).ap()
    k.slot_tok_d = nc.dram_tensor("slot_tok_d", (SLOTS, 1), f32).ap()
    k.u_d = nc.dram_tensor("u_d", (D_SSM, SEQ), f32).ap()
    k.ys_d = nc.dram_tensor("ys_d", (D_SSM, SEQ), f32).ap()
    k.expert_d = nc.dram_tensor("expert_d", (P,), i32).ap()


def project(nc, k):
    NCV = Q_RANK + KV_RANK + ROPE
    with ExitStack() as ctx:
        sb, ps, sem = makers(nc, ctx, "proj", k.held)
        w = sb("w", [P, KD, D_SSM + NCV], f32)
        xT = sb("xT", [P, KD, SEQ], f32)
        uT = sb("uT", [P, 4, SEQ], f32)
        c = sb("c", [P, T, NCV], f32)
        sq = sb("sq", [P, Q_RANK], f32)
        ssq = sb("ssq", [P, 2, T], f32)
        ms = sb("ms", [P, 2, T], f32)
        rms = sb("rms", [P, 2, T], f32)
        rot = sb("rot", [P, 4, T, ROPE // 2], f32)
        gq = sb("gq", [P, 2], f32)
        gkv = sb("gkv", [P, 1], f32)
        p_x = ps("p_x", [P, 2, KD, P])
        p_c = ps("p_c", [P, 2, 512])
        p_u = ps("p_u", [P, 2, 512])
        const_in, w_in, g_in, u_out = sem("const_in"), sem("w_in"), sem("g_in"), sem("u_out")
        x_in = [sem(f"x_in{t}") for t in range(T)]
        x_turned, xT_dve, xT_act = sem("x_turned"), sem("xT_dve"), sem("xT_act")
        c_done, c_read, sq_done, ms_done, rms_done = sem("c_done"), sem("c_read"), sem("sq_done"), sem("ms_done"), sem("rms_done")
        u_done, u_read, scaled, c_turned, cT_read, own = sem("u_done"), sem("u_read"), sem("scaled"), sem("c_turned"), sem("cT_read"), sem("own")
        block = ctx.enter_context(nc.Block())

        @block.sync
        def _(sp):
            sp.dma_start(k.const[:, :], k.consts).then_inc(const_in, 16)
            xv = k.x_in[0].rearrange("(c j) d -> c j d", j=T)
            wv = k.w_in[0].rearrange("(p k) n -> p k n", k=KD)
            for t in range(T):
                sp.dma_start(k.x[:, t, :], xv[:, t, :]).then_inc(x_in[t], 16)
                if t == 1:
                    sp.dma_start(w[:, :, :], wv).then_inc(w_in, 16)
            for kk in range(2):
                sp.dma_start(gq[:, kk:kk + 1], k.q_norm_g[0, kk * P:(kk + 1) * P].rearrange("(p o) -> p o", o=1)).then_inc(g_in, 16)
            sp.dma_start(gkv[:, :], k.kv_norm_g[0].rearrange("(p o) -> p o", o=1)).then_inc(g_in, 16)
            sp.wait_ge(u_read, 8)
            sp.dma_start(k.u_d.rearrange("(m p) t -> p m t", p=P), uT[:, :, :]).then_inc(u_out, 16)
            sp.wait_ge(u_out, 16)

        @block.tensor
        def _(pe):
            def turn_x(t):
                pe.wait_ge(x_in[t], 16)
                if t >= 2:
                    pe.wait_ge(xT_dve, t - 1)
                    pe.wait_ge(xT_act, t - 1)
                for half in range(2):
                    for q in range(4):
                        kk = half * 4 + q
                        last = nc.tensor.transpose(p_x[:, t % 2, kk, :], k.x[:, t, kk::KD], k.ident)
                    last.then_inc(x_turned, 1)

            pe.wait_ge(const_in, 16)
            turn_x(0)
            for t in range(T):
                if t + 1 < T:
                    turn_x(t + 1)
                pe.wait_ge(xT_dve, t + 1)
                pe.wait_ge(xT_act, t + 1)
                if t == 0:
                    pe.wait_ge(w_in, 16)
                if t >= 2:
                    pe.wait_ge(c_read, t - 1)
                for kk in range(KD):
                    last = nc.tensor.matmul(p_c[:, t % 2, 0:NCV], xT[:, kk, t * P:(t + 1) * P], w[:, kk, D_SSM:],
                                            start=(kk == 0), stop=(kk == KD - 1))
                last.then_inc(c_done, 1)
            for n in range(8):
                m, half = n // 2, n % 2
                if n >= 2:
                    pe.wait_ge(u_read, n - 1)
                for kk in range(KD):
                    last = nc.tensor.matmul(p_u[:, n % 2, :], w[:, kk, m * P:(m + 1) * P], xT[:, kk, half * 512:(half + 1) * 512],
                                            start=(kk == 0), stop=(kk == KD - 1))
                last.then_inc(u_done, 1)
            pe.wait_ge(c_read, T)
            for t in range(T):
                pe.wait_ge(scaled, t + 1)
                if t >= 2:
                    pe.wait_ge(cT_read, t - 1)
                nc.tensor.transpose(p_c[:, t % 2, 0:P], c[:, t, 0:P], k.ident)
                nc.tensor.transpose(p_c[:, t % 2, P:2 * P], c[:, t, P:2 * P], k.ident)
                nc.tensor.transpose(p_c[:, t % 2, 2 * P:3 * P], c[:, t, 2 * P:3 * P], k.ident)
                nc.tensor.transpose(p_c[0:DQ, t % 2, 3 * P:4 * P], c[:, t, NCV - DQ:NCV], k.ident).then_inc(c_turned, 1)

        @block.scalar
        def _(act):
            for t in range(T):
                act.wait_ge(x_turned, 2 * t + 2)
                nc.scalar.activation(xT[:, 4:8, t * P:(t + 1) * P], p_x[:, t % 2, 4:8, :], ACT.Copy).then_inc(xT_act, 1)
            for t in range(T):
                act.wait_ge(c_read, t + 1)
                if t:
                    act.wait_ge(sq_done, 2 * t)
                nc.scalar.activation(sq[:, :], c[:, t, 0:Q_RANK], ACT.Square, accum_out=ssq[:, 0, t:t + 1]).then_inc(sq_done, 1)
                act.wait_ge(sq_done, 2 * t + 1)
                nc.scalar.activation(sq[:, 0:KV_RANK], c[:, t, Q_RANK:Q_RANK + KV_RANK], ACT.Square,
                                     accum_out=ssq[:, 1, t:t + 1]).then_inc(sq_done, 1)
            act.wait_ge(ms_done, 1)
            nc.scalar.activation(rms[:, :, :], ms[:, :, :], ACT.Sqrt).then_inc(rms_done, 1)
            for n in range(8):
                m, half = n // 2, n % 2
                act.wait_ge(u_done, n + 1)
                nc.scalar.activation(uT[:, m, half * 512:(half + 1) * 512], p_u[:, n % 2, :], ACT.Copy).then_inc(u_read, 1)

        @block.vector
        def _(dve):
            ch = Chain(dve, own)

            def keep_c(t):
                dve.wait_ge(c_done, t + 1)
                nc.vector.tensor_copy(c[:, t, :], p_c[:, t % 2, 0:NCV]).then_inc(c_read, 1)

            for t in range(T):
                dve.wait_ge(x_turned, 2 * t + 1)
                nc.vector.tensor_copy(xT[:, 0:4, t * P:(t + 1) * P], p_x[:, t % 2, 0:4, :]).then_inc(xT_dve, 1)
                if t:
                    keep_c(t - 1)
            keep_c(T - 1)
            dve.wait_ge(sq_done, 2 * T)
            nc.vector.tensor_scalar(ms[:, 0, :], ssq[:, 0, :], 1.0 / Q_RANK, RMS_EPS, ALU.mult, ALU.add)
            nc.vector.tensor_scalar(ms[:, 1, :], ssq[:, 1, :], 1.0 / KV_RANK, RMS_EPS, ALU.mult, ALU.add).then_inc(ms_done, 1)
            c1, c2 = c[:, :, NCV - 32:NCV - 16], c[:, :, NCV - 16:NCV]
            dve.wait_ge(c_read, T)
            nc.vector.tensor_tensor(rot[:, 0], c1, k.cos, ALU.mult)
            nc.vector.tensor_tensor(rot[:, 1], c2, k.sin, ALU.mult)
            nc.vector.tensor_tensor(rot[:, 2], c1, k.sin, ALU.mult)
            ch.link(nc.vector.tensor_tensor(rot[:, 3], c2, k.cos, ALU.mult))
            nc.vector.tensor_tensor(c1, rot[:, 0], rot[:, 1], ALU.subtract)
            ch.link(nc.vector.tensor_tensor(c2, rot[:, 2], rot[:, 3], ALU.add))
            dve.wait_ge(rms_done, 1)
            ch.link(nc.vector.reciprocal(rms[:, :, :], rms[:, :, :]))
            for t in range(T):
                nc.vector.tensor_scalar(c[:, t, 0:Q_RANK], c[:, t, 0:Q_RANK], rms[:, 0, t:t + 1], None, ALU.mult)
                nc.vector.tensor_scalar(c[:, t, Q_RANK:Q_RANK + KV_RANK], c[:, t, Q_RANK:Q_RANK + KV_RANK],
                                        rms[:, 1, t:t + 1], None, ALU.mult).then_inc(scaled, 1)
            dve.wait_ge(g_in, 48)
            for t in range(T):
                cols = slice(t * P, (t + 1) * P)
                dve.wait_ge(c_turned, t + 1)
                nc.vector.tensor_scalar(k.cqT[:, 0, cols], p_c[:, t % 2, 0:P], gq[:, 0:1], None, ALU.mult)
                nc.vector.tensor_scalar(k.cqT[:, 1, cols], p_c[:, t % 2, P:2 * P], gq[:, 1:2], None, ALU.mult)
                nc.vector.tensor_scalar(k.ckvT[:, cols], p_c[:, t % 2, 2 * P:3 * P], gkv[:, 0:1], None, ALU.mult)
                for u in range(2):
                    last = nc.vector.tensor_copy(k.kT[NOPE:DQ, u, cols], p_c[NOPE:DQ, t % 2, 3 * P:4 * P])
                last.then_inc(cT_read, 1)


def attention(nc, k):
    SCALE = DQ ** -0.5
    with ExitStack() as ctx:
        sb, ps, sem = makers(nc, ctx, "att", k.held)
        wq = sb("wq", [P, 2, 2, DQ], f32)
        wkv = sb("wkv", [P, 2, NOPE + DV], f32)
        q = sb("q", [P, T, DQ], f32)
        rot = sb("rot", [P, 4, T, ROPE // 2], f32)
        qT = sb("qT", [DQ, SEQ], f32)
        v = sb("v", [P, T, DV], f32)
        nmax = sb("nmax", [P, 2], f32)
        bias = sb("bias", [P, 2], f32)
        total = sb("total", [P, 4], f32)
        rtotal = sb("rtotal", [P, 2], f32)
        pr = sb("pr", [P, 2, SEQ], f32)
        prT = sb("prT", [P, 2, T, P], f32)
        p_s = ps("p_s", [P, 2, SEQ])
        p_t = ps("p_t", [P, T, P])
        p_o = ps("p_o", [P, 512])
        p_v = ps("p_v", [P, T, DV])
        kT = k.kT
        w_in = [sem(f"w_in{u}") for u in range(2)]
        q_done, kv_done, q_kept, q_rotated, q_turned = sem("q_done"), sem("kv_done"), sem("q_kept"), sem("q_rotated"), sem("q_turned")
        head_dve, head_act = sem("head_dve"), sem("head_act")
        scored, biased, probs, p_turned, pT_dve, pT_act = sem("scored"), sem("biased"), sem("probs"), sem("p_turned"), sem("pT_dve"), sem("pT_act")
        o_done, o_read, own = sem("o_done"), sem("o_read"), sem("own")
        LINKS = 3 + 3 * T
        block = ctx.enter_context(nc.Block())

        @block.sync
        def _(sp):
            def load(h, u):
                sp.dma_start(wq[:, u], k.w_uq[0].rearrange("(k p) n -> p k n", p=P)[:, :, bass.ds(h * DQ, DQ)]).then_inc(w_in[u], 16)
                sp.dma_start(wkv[:, u, :], k.w_ukv[0][:, bass.ds(h * (NOPE + DV), NOPE + DV)]).then_inc(w_in[u], 16)
            load(0, 0)
            load(1, 1)
            with sp.Fori(1, HEADS // 2) as hh:
                for u in range(2):
                    h = hh * 2 + u
                    sp.wait_ge(kv_done, h - 1)
                    load(h, u)

        @block.tensor
        def _(pe):
            def scores(h, t):
                for half in range(2):
                    last = nc.tensor.matmul(p_s[:, t % 2, half * 512:(half + 1) * 512], qT[:, t * P:(t + 1) * P],
                                            kT[:, k.u, half * 512:(half + 1) * 512], start=True, stop=True)
                last.then_inc(scored, 1)

            with pe.Fori(0, HEADS // 2) as hh:
                for u in range(2):
                    h = hh * 2 + u
                    k.u = u
                    pe.wait_ge(w_in[u], hh * 32 + 32)
                    for t in range(T):
                        b, col = t // 4, (t % 4) * DQ
                        for kk in range(2):
                            last = nc.tensor.matmul(p_s[:, 0, b * 512 + col:b * 512 + col + DQ], k.cqT[:, kk, t * P:(t + 1) * P],
                                                    wq[:, u, kk, :], start=(kk == 0), stop=(kk == 1))
                    last.then_inc(q_done, 1)
                    for half in range(2):
                        nc.tensor.matmul(p_s[0:NOPE, 1, half * 512:(half + 1) * 512], wkv[:, u, 0:NOPE],
                                         k.ckvT[:, half * 512:(half + 1) * 512], start=True, stop=True)
                    for t in range(T):
                        last = nc.tensor.matmul(p_v[:, t, :], k.ckvT[:, t * P:(t + 1) * P], wkv[:, u, NOPE:], start=True, stop=True)
                    last.then_inc(kv_done, 1)
                    pe.wait_ge(q_rotated, h + 1)
                    for t in range(T):
                        last = nc.tensor.transpose(p_t[0:DQ, t, :], q[:, t, :], k.ident)
                    last.then_inc(q_turned, 1)
                    pe.wait_ge(head_dve, h + 1)
                    pe.wait_ge(head_act, h + 1)
                    scores(h, 0)
                    scores(h, 1)
                    for t in range(T):
                        n = h * T + t
                        pe.wait_ge(probs, n + 1)
                        for half in range(2):
                            for r in range(4):
                                j = half * 4 + r
                                last = nc.tensor.transpose(p_t[:, j, :], pr[:, t % 2, j * P:(j + 1) * P], k.ident)
                            last.then_inc(p_turned, 1)
                        if t + 2 < T:
                            scores(h, t + 2)
                        pe.wait_ge(pT_dve, n + 1)
                        pe.wait_ge(pT_act, n + 1)
                        if t:
                            pe.wait_ge(o_read, n)
                        for j in range(T):
                            last = nc.tensor.matmul(p_o[:, 0:DV], prT[:, t % 2, j, :], v[:, j, :], start=(j == 0), stop=(j == T - 1))
                        last.then_inc(o_done, 1)
                    pe.wait_ge(o_read, h * T + T)

        @block.scalar
        def _(act):
            with act.Fori(0, HEADS // 2) as hh:
                for u in range(2):
                    h = hh * 2 + u
                    act.wait_ge(q_done, h + 1)
                    for b in range(2):
                        last = nc.scalar.activation(q[:, 4 * b:4 * b + 4, :].rearrange("p t n -> p (t n)"),
                                                    p_s[:, 0, b * 512:b * 512 + 4 * DQ], ACT.Copy)
                    last.then_inc(q_kept, 1)
                    act.wait_ge(kv_done, h + 1)
                    nc.scalar.activation(kT[0:NOPE, u, :], p_s[0:NOPE, 1, :], ACT.Copy)
                    act.wait_ge(q_turned, h + 1)
                    nc.scalar.activation(qT[:, 512:SEQ], p_t[0:DQ, 4:8, :].rearrange("p t c -> p (t c)"), ACT.Copy).then_inc(head_act, 1)
                    for t in range(T):
                        n = h * T + t
                        act.wait_ge(biased, n + 1)
                        nc.scalar.activation(pr[:, t % 2, :], p_s[:, t % 2, :], ACT.Exp, bias=bias[:, t % 2:t % 2 + 1], scale=SCALE,
                                             accum_out=total[:, t % 4:t % 4 + 1]).then_inc(probs, 1)
                        act.wait_ge(p_turned, 2 * n + 2)
                        nc.scalar.activation(prT[:, t % 2, 4:8, :], p_t[:, 4:8, :], ACT.Copy).then_inc(pT_act, 1)

        @block.vector
        def _(dve):
            with dve.Fori(0, HEADS // 2) as hh:
                for u in range(2):
                    h = hh * 2 + u
                    ch = Chain(dve, own, h * LINKS)
                    dve.wait_ge(q_kept, h + 1)
                    q1, q2 = q[:, :, NOPE:NOPE + 16], q[:, :, NOPE + 16:DQ]
                    nc.vector.tensor_tensor(rot[:, 0], q1, k.cos, ALU.mult)
                    nc.vector.tensor_tensor(rot[:, 1], q2, k.sin, ALU.mult)
                    nc.vector.tensor_tensor(rot[:, 2], q1, k.sin, ALU.mult)
                    ch.link(nc.vector.tensor_tensor(rot[:, 3], q2, k.cos, ALU.mult))
                    nc.vector.tensor_tensor(q1, rot[:, 0], rot[:, 1], ALU.subtract)
                    nc.vector.tensor_tensor(q2, rot[:, 2], rot[:, 3], ALU.add).then_inc(q_rotated, 1)
                    dve.wait_ge(kv_done, h + 1)
                    nc.vector.tensor_copy(v[:, :, :], p_v[:, :, :])
                    dve.wait_ge(q_turned, h + 1)
                    nc.vector.tensor_copy(qT[:, 0:512], p_t[0:DQ, 0:4, :].rearrange("p t c -> p (t c)")).then_inc(head_dve, 1)

                    def top(t):
                        dve.wait_ge(scored, h * T + (t + 1))
                        ch.link(nc.vector.tensor_reduce(nmax[:, t % 2:t % 2 + 1], p_s[:, t % 2, :], AX.X, ALU.max, negate=True))
                        nc.vector.tensor_scalar(bias[:, t % 2:t % 2 + 1], nmax[:, t % 2:t % 2 + 1], SCALE, None, ALU.mult).then_inc(biased, 1)

                    def finish(t):
                        n = h * T + t
                        dve.wait_ge(o_done, n + 1)
                        ch.link(nc.vector.reciprocal(rtotal[:, t % 2:t % 2 + 1], total[:, t % 4:t % 4 + 1]))
                        nc.vector.tensor_scalar(k.o[:, t, bass.ds(h * DV, DV)], p_o[:, 0:DV], rtotal[:, t % 2:t % 2 + 1], None,
                                                ALU.mult).then_inc(o_read, 1)

                    top(0)
                    top(1)
                    for t in range(T):
                        dve.wait_ge(p_turned, (h * T + t) * 2 + 1)
                        nc.vector.tensor_copy(prT[:, t % 2, 0:4, :], p_t[:, 0:4, :]).then_inc(pT_dve, 1)
                        if t + 2 < T:
                            top(t + 2)
                        finish(t)
                    for spare in range(LINKS - ch.n):
                        ch.n += 1
                        dve.sem_inc(own, 1)


def s5_parameters(nc, k):
    DG = 2 * G
    C1, C2 = 6.28125, TWO_PI - 6.28125
    PI = 3.1415925
    with ExitStack() as ctx:
        sb, ps, sem = makers(nc, ctx, "par", k.held)
        lr = sb("lr", [DG, P], f32)
        li = sb("li", [DG, P], f32)
        dt = sb("dt", [DG, 2], f32)
        mag = sb("mag", [DG, P], f32)
        th = sb("th", [DG, P], f32)
        n = sb("n", [DG, P], f32)
        tmp = sb("tmp", [DG, 2, P], f32)
        cs = sb("cs", [DG, 2, P], f32)
        par = sb("par", [DG, 6, P], f32)
        ar, ai, kr, ki, t8, m8 = [par[:, i, :] for i in range(6)]
        prm = sb("prm", [P, 6, DG], f32)
        b1 = sb("b1", [P, DG, CH], f32)
        b2 = sb("b2", [P, DG, CH], f32)
        ba = sb("ba", [P, DG, CH], f32)
        bb = sb("bb", [P, DG, CH], f32)
        c_rows = sb("c_rows", [P, 8, 3 * N], f32)
        pt = sb("pt", [P, 4, DG, 4], f32)
        p_p = ps("p_p", [P, 512])
        p_c = ps("p_c", [P, 2, 8, P])
        lam_in, b_in, c_in = sem("lam_in"), sem("b_in"), sem("c_in")
        dt_done, lr_done, mag_done, ang_done, cs_done, par_done = sem("dt_done"), sem("lr_done"), sem("mag_done"), sem("ang_done"), sem("cs_done"), sem("par_done")
        par_turned, c_turned, own = sem("par_turned"), sem("c_turned"), sem("own")
        block = ctx.enter_context(nc.Block())

        @block.sync
        def _(sp):
            for half in range(2):
                cols = slice(half * N, (half + 1) * N)
                sp.dma_start(lr[:, cols], k.lam_re[0].rearrange("d g n -> (d g) n")).then_inc(lam_in, 16)
                sp.dma_start(li[:, cols], k.lam_im[0].rearrange("d g n -> (d g) n")).then_inc(lam_in, 16)
            sp.dma_start(dt[:, 0:1], k.log_dt[0].rearrange("d (g o) -> (d g) o", o=1)).then_inc(lam_in, 16)
            for half in range(2):
                rows, other = slice(half * N, (half + 1) * N), slice((1 - half) * N, (2 - half) * N)
                src = (k.b_re, k.b_im)[half][0].rearrange("d g n p -> n (d g) p")
                sp.dma_start(b1[rows, :, :], src).then_inc(b_in, 16)
                sp.dma_start(b2[other, :, :], src).then_inc(b_in, 16)
            for i, src in enumerate((k.c_re, k.c_im, k.c_re)):
                sp.dma_start(c_rows[:, :, i * N:(i + 1) * N],
                             src[0].rearrange("d g p n -> (d g p) n").rearrange("(a r) n -> r a n", r=P)).then_inc(c_in, 16)

        @block.scalar
        def _(act):
            act.wait_ge(lam_in, 80)
            nc.scalar.activation(dt[:, 1:2], dt[:, 0:1], ACT.Exp).then_inc(dt_done, 1)
            act.wait_ge(lr_done, 1)
            act.wait_ge(dt_done, 1)
            nc.scalar.activation(mag[:, :], lr[:, :], ACT.Exp, scale=dt[:, 1:2]).then_inc(mag_done, 1)
            act.wait_ge(ang_done, 1)
            nc.scalar.activation(cs[:, :, :], tmp[:, :, :], ACT.Sin).then_inc(cs_done, 1)

        @block.tensor
        def _(pe):
            pe.wait_ge(c_in, 48)
            for order in range(2):
                for a in range(8):
                    last = nc.tensor.transpose(p_c[:, order, a, :], c_rows[:, a, order * N:order * N + P], k.ident)
            last.then_inc(c_turned, 1)
            pe.wait_ge(par_done, 1)
            for i in range(6):
                last = nc.tensor.transpose(p_p[:, i * DG:(i + 1) * DG], par[:, i, :], k.ident[0:DG, 0:DG])
            last.then_inc(par_turned, 1)

        @block.vector
        def _(dve):
            ch = Chain(dve, own)
            tt, ts_, stt = nc.vector.tensor_tensor, nc.vector.tensor_scalar, nc.vector.scalar_tensor_tensor
            dve.wait_ge(lam_in, 80)
            ts_(lr[:, :], lr[:, :], -1e-4, None, ALU.min).then_inc(lr_done, 1)
            dve.wait_ge(dt_done, 1)
            dve.wait_ge(lr_done, 1)
            ch.link(ts_(th[:, :], li[:, :], dt[:, 1:2], None, ALU.mult))
            ch.link(ts_(n[:, :], th[:, :], 1.0 / TWO_PI, ROUND, ALU.mult, ALU.add))
            ch.link(ts_(n[:, :], n[:, :], -ROUND, None, ALU.add))
            ch.link(stt(th[:, :], n[:, :], -C1, th[:, :], ALU.mult, ALU.add))
            ch.link(stt(th[:, :], n[:, :], -C2, th[:, :], ALU.mult, ALU.add))
            ch.link(ts_(th[:, :], th[:, :], PI, -PI, ALU.min, ALU.max))
            nc.vector.tensor_copy(tmp[:, 0, :], th[:, :])
            ch.link(stt(tmp[:, 1, :], th[:, :], -1.0, th[:, :], ALU.mult, ALU.max))
            ts_(tmp[:, 1, :], tmp[:, 1, :], -1.0, math.pi / 2, ALU.mult, ALU.add).then_inc(ang_done, 1)
            dve.wait_ge(mag_done, 1)
            dve.wait_ge(cs_done, 1)
            tt(ar, mag[:, :], cs[:, 1, :], ALU.mult)
            ch.link(tt(ai, mag[:, :], cs[:, 0, :], ALU.mult))
            tt(tmp[:, 0, :], lr[:, :], lr[:, :], ALU.mult)
            ch.link(tt(tmp[:, 1, :], li[:, :], li[:, :], ALU.mult))
            ch.link(tt(n[:, :], tmp[:, 0, :], tmp[:, 1, :], ALU.add))
            nc.vector.reciprocal(n[:, :], n[:, :])
            ts_(cs[:, 0, :], ar, -1.0, None, ALU.add)
            ch.link(tt(tmp[:, 1, :], ai, li[:, :], ALU.mult))
            ch.link(tt(tmp[:, 0, :], cs[:, 0, :], lr[:, :], ALU.mult))
            ch.link(tt(kr, tmp[:, 0, :], tmp[:, 1, :], ALU.add))
            tt(tmp[:, 0, :], ai, lr[:, :], ALU.mult)
            ch.link(tt(tmp[:, 1, :], cs[:, 0, :], li[:, :], ALU.mult))
            ch.link(tt(ki, tmp[:, 0, :], tmp[:, 1, :], ALU.subtract))
            tt(kr, kr, n[:, :], ALU.mult)
            tt(ki, ki, n[:, :], ALU.mult)
            ch.link(ts_(th[:, :], th[:, :], T / TWO_PI, None, ALU.mult))
            ch.link(ts_(cs[:, 1, :], th[:, :], ROUND, -ROUND, ALU.add, ALU.add))
            tt(t8, th[:, :], cs[:, 1, :], ALU.subtract)
            ch.link(tt(m8, mag[:, :], mag[:, :], ALU.mult))
            ch.link(tt(m8, m8, m8, ALU.mult))
            tt(m8, m8, m8, ALU.mult).then_inc(par_done, 1)
            dve.wait_ge(c_turned, 1)
            cr = p_c[:, 0].rearrange("p a (g c) -> p (a g) c", c=CH)
            ci = p_c[:, 1].rearrange("p a (g c) -> p (a g) c", c=CH)
            nc.vector.tensor_copy(k.c1[:, :, :], cr)
            nc.vector.tensor_copy(k.c2[:, :, :], ci)
            ts_(k.e1[:, :, :], cr, k.sgn, None, ALU.mult)
            ts_(k.f2[:, :, :], ci, k.sgn, -1.0, ALU.mult, ALU.mult)
            dve.wait_ge(par_turned, 1)
            ch.link(nc.vector.tensor_copy(prm[:, :, :], p_p[:, 0:6 * DG].rearrange("p (i g) -> p i g", i=6)))
            nc.vector.tensor_copy(k.t8[:, :], prm[:, 4, :])
            nc.vector.tensor_copy(k.m8[:, :], prm[:, 5, :])
            dve.wait_ge(b_in, 64)
            wide = [P, DG, CH]
            krb, kib = prm[:, 2, :].unsqueeze(2).to_broadcast(wide), prm[:, 3, :].unsqueeze(2).to_broadcast(wide)
            ch.link(ts_(b2[:, :, :], b2[:, :, :], k.sgn, -1.0, ALU.mult, ALU.mult))
            tt(ba[:, :, :], b1[:, :, :], krb, ALU.mult)
            ch.link(tt(bb[:, :, :], b2[:, :, :], kib, ALU.mult))
            ch.link(tt(k.b1[:, :, :], ba[:, :, :], bb[:, :, :], ALU.add))
            tt(ba[:, :, :], b2[:, :, :], krb, ALU.mult)
            ch.link(tt(bb[:, :, :], b1[:, :, :], kib, ALU.mult))
            ch.link(tt(k.b2[:, :, :], ba[:, :, :], bb[:, :, :], ALU.subtract))
            nc.vector.memset(k.pw[:, 0, :, 0:1], 1.0)
            nc.vector.memset(k.pw[:, 1, :, 0:1], 0.0)
            nc.vector.tensor_copy(k.pw[:, 0, :, 1], prm[:, 0, :])
            ch.link(nc.vector.tensor_copy(k.pw[:, 1, :, 1], prm[:, 1, :]))
            for m in (1, 2, 4):
                w = [P, DG, m]
                re, im = k.pw[:, 0, :, 1:1 + m], k.pw[:, 1, :, 1:1 + m]
                sr, si = k.pw[:, 0, :, m:m + 1].to_broadcast(w), k.pw[:, 1, :, m:m + 1].to_broadcast(w)
                tt(pt[:, 0, :, 0:m], re, sr, ALU.mult)
                tt(pt[:, 1, :, 0:m], im, si, ALU.mult)
                tt(pt[:, 2, :, 0:m], re, si, ALU.mult)
                ch.link(tt(pt[:, 3, :, 0:m], im, sr, ALU.mult))
                tt(k.pw[:, 0, :, 1 + m:1 + 2 * m], pt[:, 0, :, 0:m], pt[:, 1, :, 0:m], ALU.subtract)
                ch.link(tt(k.pw[:, 1, :, 1 + m:1 + 2 * m], pt[:, 2, :, 0:m], pt[:, 3, :, 0:m], ALU.add))
            for i in range(2):
                ch.link(nc.vector.tensor_copy(k.pb[:, i, :, :], k.pw[:, i, :, ::-1]))


def s5_scan(nc, k):
    GB = 8
    NG = 2 * GB
    S = T + 1
    with ExitStack() as ctx:
        sb, ps, sem = makers(nc, ctx, "ssm", k.held)
        U = sb("U", [P, G, NC], f32)
        ta = sb("ta", [P, GB, S, CH], f32)
        tb = sb("tb", [P, GB, S, CH], f32)
        vs = sb("vs", [P, NG, T, CH], f32)
        bs = sb("bs", [P, NG, CH], f32)
        ed1 = sb("ed1", [P, NG, S, CH], f32)
        ed2 = sb("ed2", [P, NG, T, CH], f32)
        w_in = sb("w_in", [P, NG, 3 * N], f32)
        fr = sb("fr", [P, 2, GB, NC], f32)
        ysb = sb("ysb", [P, GB, NC], f32)
        cos_t = sb("tc", [P, NG, NC], f32)
        sin_t = sb("ts", [P, NG, NC], f32)
        ka = sb("ka", [CH, GB, 2 * T - 1, CH], f32)
        kt = sb("kt", [P, GB, T * CH], f32)
        flat = [x[:, :, :, :].rearrange("p g s c -> p (g s c)") for x in (ta, tb)]
        ra = flat[0][:, 0:4 * NC].rearrange("p (r n) -> p r n", r=4)
        rb = flat[1][:, 0:4 * NC].rearrange("p (r n) -> p r n", r=4)
        gr = flat[1][:, 4 * NC:8 * NC].rearrange("p (r n) -> p r n", r=4)
        rnd = flat[0][:, 0:GB * NC].rearrange("p (g n) -> p g n", g=GB)
        gc = sb("gc", [P, NG, NC + 1], f32)
        gsn = sb("gsn", [P, NG, NC + 1], f32)
        p_w = ps("p_w", [P, 4, P])
        p_k = ps("p_k", [P, 4, P])
        p_v = ps("p_v", [P, 2, 2, 4, NC])
        p_y = ps("p_y", [P, 2, 4, NC])
        u_in, y_out, kt_in = sem("u_in"), sem("y_out"), sem("kt_in")
        vs_done, vs_turned, win_done = sem("vs_done"), sem("vs_turned"), sem("win_done")
        ph_done, tab_done, ed_done, k_done, k_kept, ka_done = sem("ph_done"), sem("tab_done"), sem("ed_done"), sem("k_done"), sem("k_kept"), sem("ka_done")
        v_done, g_done, y_done, y_kept, own, own_p = sem("v_done"), sem("g_done"), sem("y_done"), sem("y_kept"), sem("own"), sem("own_p")
        block = ctx.enter_context(nc.Block())
        NBATCH = G // GB

        @block.sync
        def _(sp):
            sp.sem_inc(y_out, 1)
            uv = k.u_d.rearrange("(g c) (j n) -> j c g n", c=CH, j=T)
            for j in range(T):
                sp.dma_start(U[j * CH:(j + 1) * CH, :, :], uv[j]).then_inc(u_in, 16)
            yv = k.ys_d.rearrange("(g c) (j n) -> j c g n", c=CH, j=T)
            with sp.Fori(0, NBATCH) as b:
                sp.wait_ge(ka_done, b + 1)
                for j in range(T):
                    sp.dma_start(kt[j * CH:(j + 1) * CH, :, :],
                                 ka[:, :, T - 1 - j:2 * T - 1 - j, :].rearrange("c g l d -> c g (l d)")).then_inc(kt_in, 16)
                sp.wait_ge(y_kept, b * 2 + 2)
                for j in range(T):
                    sp.dma_start(yv[j][:, bass.ds(b * GB, GB), :], ysb[j * CH:(j + 1) * CH, :, :]).then_inc(y_out, 16)
            sp.wait_ge(y_out, 16 * T * NBATCH + 1)

        @block.tensor
        def _(pe):
            def effects(b, x):
                d, half = x // 2, x % 2
                for part in range(2):
                    for r in range(4):
                        gd = d * GB + half * 4 + r
                        last = nc.tensor.matmul(p_v[:, x % 2, part, r, :], w_in[:, gd, part * N:part * N + P],
                                                U[:, bass.ds(b * GB + half * 4 + r, 1), :].rearrange("p a n -> p (a n)"),
                                                start=True, stop=True)
                last.then_inc(v_done, 1)

            with pe.Fori(0, NBATCH) as b:
                for d in range(2):
                    pe.wait_ge(vs_done, b * 2 + d + 1)
                    for half in range(2):
                        x = 2 * d + half
                        if x:
                            pe.wait_ge(win_done, b * 4 + x)
                        for r in range(4):
                            gd = d * GB + half * 4 + r
                            last = nc.tensor.transpose(p_w[:, r, :], vs[:, gd].rearrange("p j c -> p (j c)"), k.ident)
                        last.then_inc(vs_turned, 1)
                pe.wait_ge(win_done, b * 4 + 4)
                pe.wait_ge(u_in, 16 * T)
                effects(b, 0)
                effects(b, 1)
                for x, (d, half) in enumerate(((1, 0), (1, 1), (0, 0), (0, 1))):
                    if half == 0:
                        pe.wait_ge(ed_done, b * 2 + 2 - d)
                    if x >= 2:
                        pe.wait_ge(k_kept, b * 4 + x - 1)
                    for r in range(4):
                        gd = d * GB + half * 4 + r
                        last = nc.tensor.matmul((p_k, p_w)[x % 2][0:CH, r, :], bs[:, gd, :], ed1[:, gd, d:d + T, :].rearrange("p j c -> p (j c)"),
                                                start=True, stop=True)
                    last.then_inc(k_done, 1)
                for x in (2, 3):
                    pe.wait_ge(g_done, b * 4 + x - 1)
                    effects(b, x)
                pe.wait_ge(kt_in, b * 16 * T + 16 * T)
                pe.wait_ge(g_done, b * 4 + 4)
                for half in range(2):
                    for r in range(4):
                        g = half * 4 + r
                        out = p_y[:, half, r, :]
                        nc.tensor.matmul(out, kt[:, g, :], U[:, bass.ds(b * GB + g, 1), :].rearrange("p a n -> p (a n)"), start=True, stop=False)
                        for d in range(2):
                            gd = d * GB + g
                            nc.tensor.matmul(out, ed1[:, gd, 1 - d:1 - d + T, :].rearrange("p j c -> p (j c)"), gc[:, gd, d:d + NC],
                                             start=False, stop=False)
                            last = nc.tensor.matmul(out, ed2[:, gd].rearrange("p j c -> p (j c)"), gsn[:, gd, d:d + NC],
                                                    start=False, stop=(d == 1))
                    last.then_inc(y_done, 1)

        @block.scalar
        def _(act):
            with act.Fori(0, NBATCH) as b:
                for x in range(4):
                    act.wait_ge(vs_turned, b * 4 + x + 1)
                    nc.scalar.activation(w_in[:, 4 * x:4 * x + 4, 0:P], p_w[:, :, :], ACT.Copy)
                    nc.scalar.activation(w_in[:, 4 * x:4 * x + 4, P:3 * N], p_w[:, :, 0:N], ACT.Copy).then_inc(win_done, 1)
                for d in range(2):
                    act.wait_ge(ph_done, b * 2 + d + 1)
                    nc.scalar.activation(sin_t[:, d * GB:(d + 1) * GB, :], fr[:, 0], ACT.Sin, scale=k.sgn2pi)
                    nc.scalar.activation(cos_t[:, d * GB:(d + 1) * GB, :], fr[:, 1], ACT.Sin, scale=-6.2831850, bias=k.half_pi).then_inc(tab_done, 1)
                act.wait_ge(y_out, b * 16 * T + 1)
                for half in range(2):
                    act.wait_ge(y_done, b * 2 + half + 1)
                    nc.scalar.activation(ysb[:, half * 4:half * 4 + 4, :], p_y[:, half], ACT.Copy).then_inc(y_kept, 1)

        @block.vector
        def _(dve):
            tt = nc.vector.tensor_tensor
            nc.vector.memset(gc[:, :, :], 0.0)
            nc.vector.memset(gsn[:, :, :], 0.0).then_inc(own_p, 1)
            LINKS = 2 * (1 + 2 + 3) + 4 * (1 + 1 + 1)

            def keep_kernels(b, x):
                d, half = 1 - x // 2, x % 2
                gs = slice(half * 4, half * 4 + 4)
                src = (p_k, p_w)[x % 2][0:CH, :, :].rearrange("c g (l d) -> c g l d", d=CH)
                dve.wait_ge(k_done, b * 4 + x + 1)
                if d:
                    last = nc.vector.tensor_copy(ka[:, gs, 0:T, :], src)
                else:
                    if half == 0:
                        dve.wait_ge(k_kept, b * 4 + 2)
                    nc.vector.tensor_tensor(ka[:, gs, T - 1, :], ka[:, gs, T - 1, :], src[:, :, 0, :], ALU.add)
                    last = nc.vector.tensor_copy(ka[:, gs, T:, :], src[:, :, 1:, :])
                last.then_inc(k_kept, 1)

            def run_states(ch, b, x):
                d, half = x // 2, x % 2
                q = slice(4 * x, 4 * x + 4)
                dve.wait_ge(v_done, b * 4 + x + 1)
                tt(ra[:, :, :], p_v[:, x % 2, 0], cos_t[:, q, :], ALU.mult)
                ch.link(tt(rb[:, :, :], p_v[:, x % 2, 1], sin_t[:, q, :], ALU.mult))
                ch.link(tt(ra[:, :, :], ra[:, :, :], rb[:, :, :], ALU.add))
                for r in range(4):
                    decay = k.m8[:, bass.ds(b * GB + d * G + half * 4 + r, 1)].to_broadcast([P, NC])
                    src, out = ra[:, r, :], gr[:, r, :]
                    if d:
                        src, out = src[:, ::-1], out[:, ::-1]
                    last = nc.vector.tensor_tensor_scan(out, decay, src, 0.0, ALU.mult, ALU.add)
                ch.link(last)
                off = 1 - d
                tt(gc[:, q, off:off + NC], gr[:, :, :], cos_t[:, q, :], ALU.mult)
                tt(gsn[:, q, off:off + NC], gr[:, :, :], sin_t[:, q, :], ALU.mult).then_inc(g_done, 1)
                dve.wait_ge(g_done, b * 4 + x + 1)

            with dve.Fori(0, NBATCH) as b:
                ch = Chain(dve, own, b * LINKS)

                def combine(out, pr, pi, x, y, op, n):
                    w = [P, GB, n, CH]
                    nc.vector.tensor_tensor(ta[:, :, 0:n, :], pr.unsqueeze(3).to_broadcast(w), x.unsqueeze(2).to_broadcast(w), ALU.mult)
                    ch.link(nc.vector.tensor_tensor(tb[:, :, 0:n, :], pi.unsqueeze(3).to_broadcast(w), y.unsqueeze(2).to_broadcast(w), ALU.mult))
                    return nc.vector.tensor_tensor(out, ta[:, :, 0:n, :], tb[:, :, 0:n, :], op)

                for d in range(2):
                    dg = bass.ds(b * GB + d * G, GB)
                    pw = k.pb[:, :, dg, 1:S] if d == 0 else k.pw[:, :, dg, 0:T]
                    combine(vs[:, d * GB:(d + 1) * GB], pw[:, 0], pw[:, 1], k.b1[:, dg, :], k.b2[:, dg, :], ALU.add, T).then_inc(vs_done, 1)
                    dve.wait_ge(vs_done, b * 2 + d + 1)
                for d in range(2):
                    dg = bass.ds(b * GB + d * G, GB)
                    w = [P, GB, NC]
                    if d:
                        dve.wait_ge(tab_done, b * 2 + 1)
                    ch.link(tt(fr[:, 0], k.t8[:, dg].unsqueeze(2).to_broadcast(w), (k.chunk, k.chunkr)[d].unsqueeze(1).to_broadcast(w), ALU.mult))
                    ch.link(nc.vector.tensor_scalar(rnd, fr[:, 0], ROUND, -ROUND, ALU.add, ALU.add))
                    tt(fr[:, 0], fr[:, 0], rnd, ALU.subtract).then_inc(own_p, 1)
                    dve.wait_ge(own_p, b * 2 + d + 2)
                    nc.vector.scalar_tensor_tensor(fr[:, 1], fr[:, 0], -1.0, fr[:, 0], ALU.mult, ALU.max).then_inc(ph_done, 1)
                dve.wait_ge(vs_turned, b * 4 + 1)
                for d in (1, 0):
                    dg = bass.ds(b * GB + d * G, GB)
                    pw = (k.pw, k.pb)[d][:, :, dg, :]
                    nc.vector.tensor_scalar(bs[:, d * GB:(d + 1) * GB, :], k.b1[:, dg, :], 1.0, None, ALU.mult)
                    combine(ed1[:, d * GB:(d + 1) * GB], pw[:, 0], pw[:, 1], k.e1[:, dg, :], k.c2[:, dg, :], ALU.subtract, S).then_inc(ed_done, 1)
                    dve.wait_ge(ed_done, b * 2 + (2 - d))
                    pw = k.pw[:, :, dg, 1:S] if d == 0 else k.pb[:, :, dg, 0:T]
                    ch.link(combine(ed2[:, d * GB:(d + 1) * GB], pw[:, 0], pw[:, 1], k.f2[:, dg, :], k.c1[:, dg, :], ALU.subtract, T))
                keep_kernels(b, 0)
                keep_kernels(b, 1)
                dve.wait_ge(tab_done, b * 2 + 2)
                run_states(ch, b, 0)
                keep_kernels(b, 2)
                keep_kernels(b, 3)
                dve.wait_ge(k_kept, b * 4 + 4)
                dve.sem_inc(ka_done, 1)
                for x in (1, 2, 3):
                    run_states(ch, b, x)
                assert ch.n == LINKS, ch.n


def s5_gate(nc, k):
    GELU = 2.0 * math.sqrt(2.0 / math.pi)
    with ExitStack() as ctx:
        sb, ps, sem = makers(nc, ctx, "glu", k.held)
        w = sb("w", [P, 4, D_SSM], f32)
        y = sb("y", [P, 4, SEQ], f32)
        u = sb("u", [P, 4, SEQ], f32)
        a = sb("a", [P, 2, SEQ], f32)
        sg = sb("sg", [P, 4, SEQ], f32)
        skip = sb("skip", [P, 4], f32)
        bg = sb("bg", [P, 4], f32)
        p_z = ps("p_z", [P, 2, SEQ])
        w_in, v_in = sem("w_in"), sem("v_in")
        yu_in = [sem(f"yu_in{m}") for m in range(4)]
        cub, sig, s_done, z_done, z_sig, own = sem("cub"), sem("sig"), sem("s_done"), sem("z_done"), sem("z_sig"), sem("own")
        block = ctx.enter_context(nc.Block())

        @block.sync
        def _(sp):
            for m in range(4):
                rows = slice(m * P, (m + 1) * P)
                sp.dma_start(y[:, m, :], k.ys_d[rows, :]).then_inc(yu_in[m], 16)
                sp.dma_start(u[:, m, :], k.u_d[rows, :]).then_inc(yu_in[m], 16)
                sp.dma_start(skip[:, m:m + 1], k.d_skip[0, rows].rearrange("(p o) -> p o", o=1)).then_inc(v_in, 16)
                sp.dma_start(bg[:, m:m + 1], k.b_glu[0, rows].rearrange("(p o) -> p o", o=1)).then_inc(v_in, 16)
            sp.dma_start(w[:, :, :], k.w_glu[0].rearrange("(k p) n -> p k n", p=P)).then_inc(w_in, 16)

        @block.scalar
        def _(act):
            for m in range(4):
                act.wait_ge(cub, m + 1)
                nc.scalar.activation(sg[:, m, :], a[:, m % 2, :], ACT.Sigmoid, scale=GELU).then_inc(sig, 1)
            for m in range(4):
                act.wait_ge(z_done, 2 * m + 2)
                nc.scalar.activation(sg[:, m, :], p_z[:, m % 2, :], ACT.Sigmoid, bias=bg[:, m:m + 1]).then_inc(z_sig, 1)

        @block.tensor
        def _(pe):
            pe.wait_ge(w_in, 16)
            pe.wait_ge(s_done, 4)
            for m in range(4):
                if m >= 2:
                    pe.wait_ge(z_sig, m - 1)
                for half in range(2):
                    for kk in range(4):
                        last = nc.tensor.matmul(p_z[:, m % 2, half * 512:(half + 1) * 512], w[:, kk, m * P:(m + 1) * P],
                                                k.sT[:, kk, half * 512:(half + 1) * 512], start=(kk == 0), stop=(kk == 3))
                    last.then_inc(z_done, 1)

        @block.vector
        def _(dve):
            ch = Chain(dve, own)
            dve.wait_ge(v_in, 16 * 8)
            for m in range(4):
                dve.wait_ge(yu_in[m], 32)
                ch.link(nc.vector.scalar_tensor_tensor(y[:, m, :], u[:, m, :], skip[:, m:m + 1], y[:, m, :], ALU.mult, ALU.add))
                if m >= 2:
                    dve.wait_ge(sig, m - 1)
                ch.link(nc.vector.tensor_tensor(a[:, m % 2, :], y[:, m, :], y[:, m, :], ALU.mult))
                ch.link(nc.vector.tensor_scalar(a[:, m % 2, :], a[:, m % 2, :], 0.044715, 1.0, ALU.mult, ALU.add))
                nc.vector.tensor_tensor(a[:, m % 2, :], a[:, m % 2, :], y[:, m, :], ALU.mult).then_inc(cub, 1)
                if m:
                    dve.wait_ge(sig, m)
                    nc.vector.tensor_tensor(k.sT[:, m - 1, :], y[:, m - 1, :], sg[:, m - 1, :], ALU.mult).then_inc(s_done, 1)
            dve.wait_ge(sig, 4)
            nc.vector.tensor_tensor(k.sT[:, 3, :], y[:, 3, :], sg[:, 3, :], ALU.mult).then_inc(s_done, 1)
            dve.wait_ge(z_done, 8)
            for m in range(4):
                dve.wait_ge(z_sig, m + 1)
                ch.link(nc.vector.tensor_tensor(k.sT[:, m, :], k.sT[:, m, :], sg[:, m, :], ALU.mult))


def load_expert(eng, k, slot, expert):
    gate_up, down = k.moe_gu[slot], k.moe_dn[slot]
    one = bass.ds(expert, 1)
    eng.dma_start(gate_up[:, :, 0:F], k.we_gate[0].rearrange("e (p k) f -> e p k f", k=KD)[one].rearrange("e p k f -> (e p) k f")).then_inc(k.gu_in[slot], 16)
    eng.dma_start(gate_up[:, :, F:2 * F], k.we_up[0].rearrange("e (p k) f -> e p k f", k=KD)[one].rearrange("e p k f -> (e p) k f")).then_inc(k.gu_in[slot], 16)
    eng.dma_start(down[:, :, :], k.we_down[0].rearrange("e (p k) n -> e p k n", k=KF)[one].rearrange("e p k n -> (e p) k n")).then_inc(k.dn_in[slot], 16)


def mix_norm_route(nc, k):
    with ExitStack() as ctx:
        sb, ps, sem = makers(nc, ctx, "mix", k.held)
        w_o = sb("w_o", [P, KD, D], f32)
        w_r = sb("w_r", [P, KD, N_EXPERTS], f32)
        r_bias = sb("r_bias", [P, N_EXPERTS], f32)
        zeros = sb("zeros", [P, D], f32)
        g1 = sb("g1", [P, D], f32)
        b1 = sb("b1", [P, D], f32)
        oT = sb("oT", [P, 2, 4, P], f32)
        r = sb("r", [P, D], f32)
        stats = sb("stats", [P, 2, 6], f32)
        mv = sb("mv", [P, 2, 2], f32)
        std = sb("std", [P, 2], f32)
        rstd = sb("rstd", [P, 1], f32)
        score = sb("score", [P, 2, N_EXPERTS], f32)
        choice = sb("choice", [P, N_EXPERTS], f32)
        top2 = sb("top2", [P, EGROUPS, 8], f32)
        gscore = sb("gscore", [P, EGROUPS], f32)
        gtop = sb("gtop", [P, 8], f32)
        gidx = sb("gidx", [P, 8], u32)
        gidxf = sb("gidxf", [P, 8], f32)
        geq = sb("geq", [P, EGROUPS, TOP_GROUPS], f32)
        gmask = sb("gmask", [P, EGROUPS], f32)
        gneg = sb("gneg", [P, EGROUPS], f32)
        top8 = sb("top8", [P, 8], f32)
        idx8 = sb("idx8", [P, 8], u32)
        hot = sb("hot", [P, TOP_K, N_EXPERTS], f32)
        hots = sb("hots", [P, TOP_K, N_EXPERTS], f32)
        wsum = sb("wsum", [P, 1], f32)
        wrec = sb("wrec", [P, 1], f32)
        member = sb("member", [P, 2, N_EXPERTS], f32)
        seen = sb("seen", [P, 2, N_EXPERTS], f32)
        p_m = ps("p_m", [P, 2, D])
        p_x = ps("p_x", [P, KD, P])
        p_o = ps("p_o", [P, 512])
        p_log = ps("p_log", [P, 512])
        p_rank, p_log = p_o[:, 0:N_EXPERTS], p_log[:, 0:N_EXPERTS]

        wo_in, wr_in, ln_in = sem("wo_in"), sem("wr_in"), sem("ln_in")
        zeroed, y_zeroed = sem("zeroed"), sem("y_zeroed")
        x1_out = [sem(f"x1_out{t}") for t in range(T)]
        o_turned, oT_done, mixed, mix_read = sem("o_turned"), sem("oT_done"), sem("mixed"), sem("mix_read")
        var_done, std_done, x1_done = sem("var_done"), sem("std_done"), sem("x1_done")
        x_turned, xT_dve, xT_act, logits = sem("x_turned"), sem("xT_dve"), sem("xT_act"), sem("logits")
        score_done, member_done, ranked, rank_read, own = sem("score_done"), sem("member_done"), sem("ranked"), sem("rank_read"), sem("own")
        block = ctx.enter_context(nc.Block())

        @block.sync
        def _(sp):
            sp.dma_start(w_o[:, :, :], k.w_o[0].rearrange("(k p) n -> p k n", p=P)).then_inc(wo_in, 16)
            sp.dma_start(g1[:, :], k.ln1_g.to_broadcast([P, D])).then_inc(ln_in, 16)
            sp.dma_start(b1[:, :], k.ln1_b.to_broadcast([P, D])).then_inc(ln_in, 16)
            sp.dma_start(w_r[:, :, :], k.w_router[0].rearrange("(p k) n -> p k n", k=KD)).then_inc(wr_in, 16)
            sp.dma_start(r_bias[:, :], k.router_bias.to_broadcast([P, N_EXPERTS])).then_inc(wr_in, 16)
            sp.dma_start(k.ws_gu[:, :, 0:F], k.ws_gate[0].rearrange("(p k) n -> p k n", k=KD)).then_inc(k.ws_in, 16)
            sp.dma_start(k.ws_gu[:, :, F:2 * F], k.ws_up[0].rearrange("(p k) n -> p k n", k=KD)).then_inc(k.ws_in, 16)
            sp.dma_start(k.ws_dn[:, :, :], k.ws_down[0].rearrange("(k p) n -> p k n", p=P)).then_inc(k.ws_in, 16)
            sp.wait_ge(zeroed, 1)
            sp.dma_start(k.y_d[N_EXPERTS * P:SLOTS, :].rearrange("(b p) d -> p b d", p=P),
                         zeros[:, :].unsqueeze(1).to_broadcast([P, OVER, D])).then_inc(y_zeroed, 16)
            for t in range(T):
                sp.wait_ge(x1_done, t + 1)
                sp.dma_start(k.x1_d[t * P:(t + 1) * P, :], k.x[:, t, :]).then_inc(x1_out[t], 16)
            for t in range(T):
                sp.wait_ge(x1_out[t], 16)
            sp.wait_ge(y_zeroed, 16)

        @block.tensor
        def _(pe):
            def turn_o(t):
                if t >= 5:
                    pe.wait_ge(rank_read, t - 4)
                elif t:
                    pe.wait_ge(oT_done, t)
                for q in range(4):
                    last = nc.tensor.transpose(p_o[:, q * P:(q + 1) * P], k.o[:, t, q * P:(q + 1) * P], k.ident)
                last.then_inc(o_turned, 1)

            def mix(t):
                if t == 0:
                    pe.wait_ge(wo_in, 16)
                if t >= 2:
                    pe.wait_ge(mix_read, 2 * t - 2)
                for half in range(2):
                    cols = slice(half * 512, (half + 1) * 512)
                    for kk in range(4):
                        nc.tensor.matmul(p_m[:, t % 2, cols], k.sT[:, kk, t * P:(t + 1) * P], w_o[:, kk, cols],
                                         start=(kk == 0), stop=False)
                    if half == 0:
                        pe.wait_ge(oT_done, t + 1)
                    for kk in range(4):
                        last = nc.tensor.matmul(p_m[:, t % 2, cols], oT[:, t % 2, kk, :], w_o[:, 4 + kk, cols],
                                                start=False, stop=(kk == 3))
                    last.then_inc(mixed, 1)

            def turn_x(t):
                pe.wait_ge(x1_done, t + 1)
                for half in range(2):
                    for q in range(4):
                        kk = half * 4 + q
                        last = nc.tensor.transpose(p_x[:, kk, :], k.x[:, t, kk::KD], k.ident)
                    last.then_inc(x_turned, 1)

            def route(t):
                pe.wait_ge(xT_dve, t + 1)
                pe.wait_ge(xT_act, t + 1)
                if t == 0:
                    pe.wait_ge(wr_in, 32)
                else:
                    pe.wait_ge(score_done, t)
                for kk in range(KD):
                    last = nc.tensor.matmul(p_log, k.x1T[:, kk, t * P:(t + 1) * P], w_r[:, kk, :], start=(kk == 0), stop=(kk == KD - 1))
                last.then_inc(logits, 1)

            def rank(t):
                pe.wait_ge(member_done, t + 1)
                pe.wait_ge(oT_done, min(t + 5, T))
                last = nc.tensor.matmul(p_rank, k.tri, member[:, t % 2, :], start=True, stop=(t == 0))
                if t:
                    last = nc.tensor.matmul(p_rank, k.ones, seen[:, t % 2, :], start=False, stop=True)
                last.then_inc(ranked, 1)

            turn_o(0)
            turn_o(1)
            mix(0)
            turn_o(2)
            mix(1)
            for t in range(T):
                turn_x(t)
                if t + 3 < T:
                    turn_o(t + 3)
                if t + 2 < T:
                    mix(t + 2)
                if t:
                    rank(t - 1)
                route(t)
            pe.wait_ge(rank_read, T - 1)
            rank(T - 1)
            pe.wait_ge(rank_read, T)
            pe.wait_ge(member_done, T + 1)
            nc.tensor.matmul(p_rank, k.ones, seen[:, T % 2, :], start=True, stop=True).then_inc(ranked, 1)

        @block.scalar
        def _(act):
            def keep_oT(t):
                act.wait_ge(o_turned, t + 1)
                nc.scalar.activation(oT[:, t % 2, :, :].rearrange("p k t -> p (k t)"), p_o[:, :], ACT.Copy).then_inc(oT_done, 1)

            def deviation(t):
                act.wait_ge(var_done, t + 1)
                nc.scalar.activation(std[:, t % 2:t % 2 + 1], mv[:, t % 2, 1:2], ACT.Sqrt).then_inc(std_done, 1)

            keep_oT(0)
            keep_oT(1)
            keep_oT(2)
            deviation(0)
            for t in range(T):
                act.wait_ge(x_turned, 2 * t + 2)
                nc.scalar.activation(k.x1T[:, 4:8, t * P:(t + 1) * P], p_x[:, 4:8, :], ACT.Copy).then_inc(xT_act, 1)
                if t + 3 < T:
                    keep_oT(t + 3)
                if t + 1 < T:
                    deviation(t + 1)
                act.wait_ge(logits, t + 1)
                nc.scalar.activation(score[:, t % 2, :], p_log, ACT.Sigmoid).then_inc(score_done, 1)

        @block.vector
        def _(dve):
            ch = Chain(dve, own)

            def norm(t):
                xt = k.x[:, t, :]
                for half in range(2):
                    cols = slice(half * 512, (half + 1) * 512)
                    dve.wait_ge(mixed, 2 * t + half + 1)
                    nc.vector.scalar_tensor_tensor(r[:, cols], k.x[:, t, cols], ALPHA, p_m[:, t % 2, cols], ALU.mult, ALU.add).then_inc(mix_read, 1)
                dve.wait_ge(mix_read, 2 * t + 2)
                nc.vector.bn_stats(stats[:, 0, :], r[:, 0:512])
                ch.link(nc.vector.bn_stats(stats[:, 1, :], r[:, 512:D]))
                ch.link(nc.vector.bn_aggr(mv[:, t % 2, :], stats[:, :, :].rearrange("p a b -> p (a b)")))
                ch.link(nc.vector.tensor_scalar(mv[:, t % 2, 1:2], mv[:, t % 2, 1:2], LN_EPS, None, ALU.add))
                nc.vector.tensor_copy(rstd[:, :], mv[:, t % 2, 1:2]).then_inc(var_done, 1)
                dve.wait_ge(std_done, t + 1)
                ch.link(nc.vector.reciprocal(rstd[:, :], std[:, t % 2:t % 2 + 1]))
                ch.link(nc.vector.tensor_scalar(r[:, :], r[:, :], mv[:, t % 2, 0:1], rstd[:, 0:1], ALU.subtract, ALU.mult))
                if t == 0:
                    dve.wait_ge(ln_in, 32)
                ch.link(nc.vector.tensor_tensor(r[:, :], r[:, :], g1[:, :], ALU.mult))
                nc.vector.tensor_tensor(xt, r[:, :], b1[:, :], ALU.add).then_inc(x1_done, 1)

            def route(t):
                sc = score[:, t % 2, :]
                dve.wait_ge(score_done, t + 1)
                ch.link(nc.vector.tensor_tensor(choice[:, :], sc, r_bias[:, :], ALU.add))
                for g in range(EGROUPS):
                    last = nc.vector.max(top2[:, g, :], choice[:, g * 8:(g + 1) * 8])
                ch.link(last)
                ch.link(nc.vector.tensor_tensor(gscore[:, :], top2[:, :, 0], top2[:, :, 1], ALU.add))
                ch.link(nc.vector.max(gtop[:, :], gscore[:, :]))
                ch.link(nc.vector.max_index(gidx[:, :], gtop[:, :], gscore[:, :]))
                ch.link(nc.vector.tensor_copy(gidxf[:, :], gidx[:, :]))
                ch.link(nc.vector.tensor_tensor(geq[:, :, :], k.iota_e[:, 0:EGROUPS].unsqueeze(2).to_broadcast([P, EGROUPS, TOP_GROUPS]),
                                                gidxf[:, 0:TOP_GROUPS].unsqueeze(1).to_broadcast([P, EGROUPS, TOP_GROUPS]), ALU.is_equal))
                ch.link(nc.vector.tensor_reduce(gmask[:, :], geq[:, :, :], AX.X, ALU.add))
                ch.link(nc.vector.tensor_scalar(gneg[:, :], gmask[:, :], BIG, -BIG, ALU.mult, ALU.add))
                v3 = choice[:, :].rearrange("p (g e) -> p g e", g=EGROUPS)
                ch.link(nc.vector.tensor_tensor(v3, v3, gmask[:, :].unsqueeze(2).to_broadcast([P, EGROUPS, 8]), ALU.mult))
                ch.link(nc.vector.tensor_tensor(v3, v3, gneg[:, :].unsqueeze(2).to_broadcast([P, EGROUPS, 8]), ALU.add))
                ch.link(nc.vector.max(top8[:, :], choice[:, :]))
                ch.link(nc.vector.max_index(idx8[:, :], top8[:, :], choice[:, :]))
                ch.link(nc.vector.tensor_copy(k.picked[:, t, :], idx8[:, 0:TOP_K]))
                ch.link(nc.vector.tensor_tensor(hot[:, :, :], k.iota_e.unsqueeze(1).to_broadcast([P, TOP_K, N_EXPERTS]),
                                                k.picked[:, t, :].unsqueeze(2).to_broadcast([P, TOP_K, N_EXPERTS]), ALU.is_equal))
                nc.vector.tensor_reduce(member[:, t % 2, :], hot[:, :, :].rearrange("p k e -> p e k"), AX.X, ALU.add).then_inc(member_done, 1)
                ch.link(nc.vector.tensor_tensor(hots[:, :, :], hot[:, :, :], sc.unsqueeze(1).to_broadcast([P, TOP_K, N_EXPERTS]), ALU.mult))
                ch.link(nc.vector.tensor_reduce(k.top_w[:, t, :], hots[:, :, :], AX.X, ALU.add))
                ch.link(nc.vector.tensor_reduce(wsum[:, :], k.top_w[:, t, :], AX.X, ALU.add))
                ch.link(nc.vector.tensor_scalar(wsum[:, :], wsum[:, :], 1e-20, None, ALU.add))
                ch.link(nc.vector.reciprocal(wrec[:, :], wsum[:, :]))
                ch.link(nc.vector.tensor_scalar(k.top_w[:, t, :], k.top_w[:, t, :], wrec[:, 0:1], ROUTED_SCALE, ALU.mult, ALU.mult))

            def keep_rank(t):
                dve.wait_ge(ranked, t + 1)
                nc.vector.tensor_copy(k.rank[:, t, :], p_rank).then_inc(rank_read, 1)

            nc.vector.memset(zeros[:, :], 0.0).then_inc(zeroed, 1)
            norm(0)
            for t in range(T):
                dve.wait_ge(x_turned, 2 * t + 1)
                nc.vector.tensor_copy(k.x1T[:, 0:4, t * P:(t + 1) * P], p_x[:, 0:4, :]).then_inc(xT_dve, 1)
                if t + 1 < T:
                    norm(t + 1)
                if t:
                    keep_rank(t - 1)
                route(t)
                if t == 0:
                    ch.link(nc.vector.tensor_copy(seen[:, 1, :], member[:, 0, :]))
                else:
                    ch.link(nc.vector.tensor_tensor(seen[:, (t + 1) % 2, :], seen[:, t % 2, :], member[:, t % 2, :], ALU.add))
            dve.sem_inc(member_done, 1)
            keep_rank(T - 1)
            dve.wait_ge(ranked, T + 1)
            ch.link(nc.vector.tensor_copy(k.counts[:, :], p_rank))


def dispatch(nc, k):
    E = N_EXPERTS
    with ExitStack() as ctx:
        sb, ps, sem = makers(nc, ctx, "disp", k.held)
        over = sb("over", [P, E], f32)
        over_end = sb("over_end", [P, E], f32)
        base = sb("base", [P, E], f32)
        far = sb("far", [P, T, E], f32)
        slot = sb("slot", [P, T, E], f32)
        hot = sb("d_hot", [P, TOP_K, E], f32)
        dest = sb("dest", [P, T, TOP_K], f32)
        le = sb("le", [P, E], f32)
        expert_f = sb("expert_f", [P, 2], f32)
        expert_i = sb("expert_i", [P, 2], i32)
        zero = sb("zero", [E + OVER, P], f32)
        toks = sb("toks", [E + OVER, P], f32)
        p_t = ps("p_t", [P, P])
        own, dest_done, zeroed, zeroed_d = sem("d_own"), sem("dest_done"), sem("zeroed"), sem("zeroed_d")
        scattered, toks_in, toks_turned = sem("scattered"), sem("toks_in"), sem("toks_turned")
        expert_done, expert_d, expert_in = sem("expert_done"), sem("expert_d"), sem("expert_in")
        sig = sb("s_sig", [P, 2, 512], f32)
        hT = sb("s_hT", [P, KF, SEQ], f32)
        p_gu = ps("p_gu", [P, 2, 2, 512])
        p_y = ps("p_y", [P, 2, 512])
        gu_done, sig_done, gs_done, h_done, y_done, y_read = sem("gu_done"), sem("sig_done"), sem("gs_done"), sem("h_done"), sem("y_done"), sem("y_read")
        units = [(half, f) for half in range(2) for f in range(KF)]
        block = ctx.enter_context(nc.Block())

        @block.scalar
        def _(act):
            for e in range(EARLY):
                load_expert(act, k, e, e)
            for n, (half, f) in enumerate(units):
                act.wait_ge(gu_done, n + 1)
                if n >= 2:
                    act.wait_ge(gs_done, n - 1)
                nc.scalar.activation(sig[:, n % 2, :], p_gu[:, n % 2, 0, :], ACT.Sigmoid).then_inc(sig_done, 1)

        @block.vector
        def _(dve):
            ch = Chain(dve, own)
            nc.vector.memset(zero[:, :], 0.0).then_inc(zeroed, 1)
            ch.link(nc.vector.tensor_scalar(over[:, :], k.counts[:, :], float(P), None, ALU.is_gt))
            for m in range(2, SEQ // P):
                ch.link(nc.vector.scalar_tensor_tensor(over[:, :], k.counts[:, :], float(P * m), over[:, :], ALU.is_gt, ALU.add))
            ch.link(nc.vector.tensor_tensor_scan(over_end[:, :], k.ones[:, 0:E], over[:, :], 0.0, ALU.mult, ALU.add))
            ch.link(nc.vector.tensor_scalar(le[:, :], over_end[:, :], k.part, None, ALU.is_le))
            ch.link(nc.vector.tensor_reduce(expert_f[:, 0:1], le[:, :], AX.X, ALU.add))
            ch.link(nc.vector.tensor_scalar(expert_f[:, 0:1], expert_f[:, 0:1], float(E - 1), None, ALU.min))
            ch.link(nc.vector.tensor_copy(expert_f[:, 1:2], over_end[:, E - 1:E]))
            ch.link(nc.vector.tensor_copy(k.n_over[0:1, 0:1], expert_f[0:1, 1:2]))
            nc.vector.tensor_copy(expert_i[:, :], expert_f[:, :]).then_inc(expert_done, 1)
            ch.link(nc.vector.tensor_tensor(base[:, :], over_end[:, :], over[:, :], ALU.subtract))
            ch.link(nc.vector.tensor_scalar(base[:, :], base[:, :], float(P), float(P * E - P), ALU.mult, ALU.add))
            ch.link(nc.vector.tensor_tensor(base[:, :], base[:, :], k.iota_e128, ALU.subtract))
            wide = [P, T, E]
            ch.link(nc.vector.tensor_scalar(far[:, :, :], k.rank[:, :, :], float(P), None, ALU.is_ge))
            ch.link(nc.vector.tensor_tensor(far[:, :, :], far[:, :, :], base[:, :].unsqueeze(1).to_broadcast(wide), ALU.mult))
            ch.link(nc.vector.tensor_tensor(slot[:, :, :], k.rank[:, :, :], k.iota_e128.unsqueeze(1).to_broadcast(wide), ALU.add))
            ch.link(nc.vector.tensor_tensor(slot[:, :, :], slot[:, :, :], far[:, :, :], ALU.add))
            many = [P, TOP_K, E]
            for t in range(T):
                ch.link(nc.vector.tensor_tensor(hot[:, :, :], k.iota_e.unsqueeze(1).to_broadcast(many),
                                                k.picked[:, t, :].unsqueeze(2).to_broadcast(many), ALU.is_equal))
                ch.link(nc.vector.tensor_tensor(hot[:, :, :], hot[:, :, :], slot[:, t, :].unsqueeze(1).to_broadcast(many), ALU.mult))
                ch.link(nc.vector.tensor_reduce(dest[:, t, :], hot[:, :, :], AX.X, ALU.add))
                nc.vector.tensor_copy(k.dest[:, t * TOP_K:(t + 1) * TOP_K], dest[:, t, :]).then_inc(dest_done, 1)
            for n, (half, f) in enumerate(units):
                out = hT[:, f, half * 512:(half + 1) * 512]
                dve.wait_ge(sig_done, n + 1)
                nc.vector.tensor_tensor(out, sig[:, n % 2, :], p_gu[:, n % 2, 0, :], ALU.mult).then_inc(gs_done, 1)
                dve.wait_ge(gs_done, n + 1)
                nc.vector.tensor_tensor(out, out, p_gu[:, n % 2, 1, :], ALU.mult).then_inc(h_done, 1)
            for n in range(2 * T):
                t, cols = n // 2, slice(n % 2 * 512, (n % 2 + 1) * 512)
                dve.wait_ge(y_done, n + 1)
                nc.vector.scalar_tensor_tensor(k.x[:, t, cols], k.x[:, t, cols], ALPHA, p_y[:, n % 2, :], ALU.mult, ALU.add).then_inc(y_read, 1)
            dve.wait_ge(toks_turned, 1)
            nc.vector.tensor_copy(k.block_tok[:, :], p_t[:, 0:E + OVER])

        @block.gpsimd
        def _(pool):
            pool.wait_ge(zeroed_d, 16)
            for t in range(T):
                pool.wait_ge(dest_done, t + 1)
                for q in range(TOP_K):
                    nc.gpsimd.indirect_dma_start(k.slot_tok_d[:, :],
                                                 bass.IndirectOffsetOnAxis(ap=k.dest[:, t * TOP_K + q:t * TOP_K + q + 1], axis=0),
                                                 k.tok[:, t:t + 1], None).then_inc(scattered, 16)

        @block.sync
        def _(sp):
            sp.wait_ge(zeroed, 1)
            sp.dma_start(k.slot_tok_d.rearrange("(b s) o -> b (s o)", s=P), zero[:, :]).then_inc(zeroed_d, 16)
            sp.wait_ge(expert_done, 1)
            sp.dma_start(k.expert_d.rearrange("(p o) -> p o", o=1), expert_i[:, 0:1]).then_inc(expert_d, 16)
            sp.wait_ge(expert_d, 16)
            sp.dma_start(k.over_expert[0:1, :], k.expert_d[0:OVER].rearrange("(o p) -> o p", o=1)).then_inc(expert_in, 16)
            sp.wait_ge(scattered, 16 * T * TOP_K)
            sp.dma_start(toks[:, :], k.slot_tok_d.rearrange("(b s) o -> b (s o)", s=P)).then_inc(toks_in, 16)
            sp.wait_ge(expert_in, 16)

        @block.tensor
        def _(pe):
            pe.wait_ge(k.ws_in, 48)
            for n, (half, f) in enumerate(units):
                if n >= 2:
                    pe.wait_ge(h_done, n - 1)
                for part in range(2):
                    for kk in range(KD):
                        last = nc.tensor.matmul(p_gu[:, n % 2, part, :], k.ws_gu[:, kk, part * F + f * P:part * F + (f + 1) * P],
                                                k.x1T[:, kk, half * 512:(half + 1) * 512], start=(kk == 0), stop=(kk == KD - 1))
                last.then_inc(gu_done, 1)
            for n in range(2 * T):
                t, cols = n // 2, slice(n % 2 * 512, (n % 2 + 1) * 512)
                if n % T == 0:
                    pe.wait_ge(h_done, 2 + 2 * (n // T))
                if n >= 2:
                    pe.wait_ge(y_read, n - 1)
                for f in range(KF):
                    last = nc.tensor.matmul(p_y[:, n % 2, :], hT[:, f, t * P:(t + 1) * P], k.ws_dn[:, f, cols],
                                            start=(f == 0), stop=(f == KF - 1))
                last.then_inc(y_done, 1)
            pe.wait_ge(toks_in, 16)
            nc.tensor.transpose(p_t[:, 0:E + OVER], toks[:, :], k.ident[0:E + OVER, 0:E + OVER]).then_inc(toks_turned, 1)



def moe_experts(nc, k):
    E = N_EXPERTS
    with ExitStack() as ctx:
        sb, ps, sem = makers(nc, ctx, "moe", k.held)
        for e in range(EARLY, RING):
            k.moe_gu.append(sb(f"gu{e}", [P, KD, 2 * F], f32))
            k.moe_dn.append(sb(f"dn{e}", [P, KF, D], f32))
        xg = sb("xg", [P, 2, D], f32)
        xgT = sb("xgT", [P, 2, KD, P], f32)
        sig = sb("sig", [P, 2, F], f32)
        gs = sb("gs", [P, 2, F], f32)
        h = sb("h", [P, 2, F], f32)
        hT = sb("hT", [P, 2, KF, P], f32)
        y = sb("y", [P, 2, D], f32)
        idx = sb("idx", [P, 2], i32)
        p_x = ps("p_x", [P, KD, P])
        p_gu = ps("p_gu", [P, 2, 2 * F])
        p_h = ps("p_h", [P, 512])
        p_y = ps("p_y", [P, D])

        xg_in = [sem(f"xg_in{u}") for u in range(2)]
        y_out = [sem(f"y_out{u}") for u in range(2)]
        x_turned = sem("x_turned")
        gu_done = sem("gu_done")
        h_turned = sem("h_turned")
        y_done = sem("y_done")
        xT_dve = sem("xT_dve")
        xT_act = sem("xT_act")
        sig_done = sem("sig_done")
        gs_done = sem("gs_done")
        h_done = sem("h_done")
        hT_done = sem("hT_done")
        y_dve = sem("y_dve")
        y_act = sem("y_act")
        idx_done = sem("idx_done")
        idx_seen = sem("idx_seen")
        all_out = sem("all_out")
        block = ctx.enter_context(nc.Block())

        @block.sync
        def _(sp):
            for e in range(EARLY, RING):
                load_expert(sp, k, e, e)
            with sp.Fori(1, E // RING) as ee:
                for v in range(RING):
                    e = ee * RING + v
                    sp.wait_ge(gu_done, e - (RING - 1))
                    sp.wait_ge(y_done, e * 2 - (2 * RING - 2))
                    load_expert(sp, k, v, e)
            n_over = sp.value_load(k.n_over[0:1, 0:1], min_val=0, max_val=OVER)
            with sp.Fori(0, OVER // RING) as jj:
                for v in range(RING):
                    j = jj * RING + v
                    with sp.If(n_over > j):
                        expert = sp.value_load(k.over_expert[0:1, bass.ds(j, 1)], min_val=0, max_val=E - 1)
                        sp.wait_ge(gu_done, j + (E - (RING - 1)))
                        sp.wait_ge(y_done, j * 2 + (2 * E - (2 * RING - 2)))
                        load_expert(sp, k, v, expert)

        @block.gpsimd
        def _(pool):
            def gather(e, u):
                nc.gpsimd.tensor_copy(idx[:, u:u + 1], k.block_tok[:, bass.ds(e, 1)]).then_inc(idx_done, 1)
                pool.wait_ge(idx_done, e + 1)
                pool.sem_inc(idx_seen, 1)
                nc.gpsimd.indirect_dma_start(xg[:, u, :], None, k.x1_d[:, :],
                                             bass.IndirectOffsetOnAxis(ap=idx[:, u:u + 1], axis=0)).then_inc(xg_in[u], 16)

            for e in range(2):
                gather(e, e)
            with pool.Fori(1, E // 2) as ee:
                for u in range(2):
                    e = ee * 2 + u
                    pool.wait_ge(x_turned, e * 2 - 2)
                    gather(e, u)
            n_over = pool.value_load(k.n_over[0:1, 0:1], min_val=0, max_val=OVER)
            with pool.Fori(0, OVER // 2) as jj:
                for u in range(2):
                    j = jj * 2 + u
                    with pool.If(n_over > j):
                        pool.wait_ge(x_turned, j * 2 + (2 * E - 2))
                        gather(j + E, u)

        @block.tensor
        def _(pe):
            def turn_x(n, c):
                u = c % 2
                pe.wait_ge(xg_in[u], n * (16 * RING // 2) + (c // 2 + 1) * 16)
                for half in range(2):
                    for q in range(4):
                        kk = half * 4 + q
                        last = nc.tensor.transpose(p_x[:, kk, :], xg[:, u, kk::KD], k.ident)
                    last.then_inc(x_turned, 1)

            def gate_up(n, c):
                e, u, v = n * RING + c, c % 2, c % RING
                pe.wait_ge(xT_dve, e + 1)
                pe.wait_ge(xT_act, e + 1)
                pe.wait_ge(k.gu_in[v], n * 32 + (c // RING + 1) * 32)
                for kk in range(KD):
                    last = nc.tensor.matmul(p_gu[:, u, :], xgT[:, u, kk, :], k.moe_gu[v][:, kk, :],
                                            start=(kk == 0), stop=(kk == KD - 1))
                last.then_inc(gu_done, 1)

            def turn_h(n, c):
                e, u = n * RING + c, c % 2
                pe.wait_ge(h_done, e + 1)
                for kk in range(KF):
                    last = nc.tensor.transpose(p_h[:, kk * P:(kk + 1) * P], h[:, u, kk::KF], k.ident)
                last.then_inc(h_turned, 1)

            def down(n, c, first=False):
                e, u, v = n * RING + c, c % 2, c % RING
                pe.wait_ge(hT_done, e + 1)
                pe.wait_ge(k.dn_in[v], n * 16 + (c // RING + 1) * 16)
                if not first:
                    pe.wait_ge(y_dve, e)
                    pe.wait_ge(y_act, e)
                for half in range(2):
                    for kk in range(KF):
                        last = nc.tensor.matmul(p_y[:, half * 512:(half + 1) * 512], hT[:, u, kk, :],
                                                k.moe_dn[v][:, kk, half * 512:(half + 1) * 512],
                                                start=(kk == 0), stop=(kk == KF - 1))
                    last.then_inc(y_done, 1)

            def step(n, c, first=False):
                gate_up(n, c + 1)
                turn_x(n, c + 2)
                down(n, c, first)
                turn_h(n, c + 1)

            turn_x(0, 0)
            gate_up(0, 0)
            turn_x(0, 1)
            turn_h(0, 0)
            step(0, 0, first=True)
            step(0, 1)
            with pe.Fori(0, E // RING - 1) as n:
                for v in range(RING):
                    step(n, v + 2)
            last = E // RING - 1
            gate_up(last, RING - 1)
            down(last, RING - 2)
            turn_h(last, RING - 1)
            down(last, RING - 1)
            n_over = pe.value_load(k.n_over[0:1, 0:1], min_val=0, max_val=OVER)
            with pe.Fori(0, OVER // RING) as jj:
                for v in range(RING):
                    with pe.If(n_over > jj * RING + v):
                        turn_x(jj, v + E)
                        gate_up(jj, v + E)
                        turn_h(jj, v + E)
                        down(jj, v + E)

        @block.scalar
        def _(act):
            def keep_xT(e, u):
                act.wait_ge(x_turned, e * 2 + 2)
                nc.scalar.activation(xgT[:, u, 4:8, :], p_x[:, 4:8, :], ACT.Copy).then_inc(xT_act, 1)

            def gate(e, u):
                act.wait_ge(gu_done, e + 1)
                nc.scalar.activation(sig[:, u, :], p_gu[:, u, 0:F], ACT.Sigmoid).then_inc(sig_done, 1)

            def keep_y(e, u, n):
                act.wait_ge(y_done, e * 2 + 1)
                if n is not None:
                    act.wait_ge(y_out[u], n)
                nc.scalar.activation(y[:, u, 0:512], p_y[:, 0:512], ACT.Copy).then_inc(y_act, 1)
                act.wait_ge(y_act, e + 1)
                act.wait_ge(y_dve, e + 1)
                act.dma_start(k.y_d[bass.ds(e * P, P), :], y[:, u, :]).then_inc(y_out[u], 16)

            keep_xT(0, 0)
            gate(0, 0)
            keep_xT(1, 1)
            gate(1, 1)
            keep_xT(2, 0)
            keep_y(0, 0, None)
            gate(2, 0)
            keep_xT(3, 1)
            keep_y(1, 1, None)
            with act.Fori(1, E // 2 - 1) as ii:
                for u in range(2):
                    i = ii * 2 + u
                    gate(i + 1, 1 - u)
                    keep_xT(i + 2, u)
                    keep_y(i, u, ii * 16)
            gate(E - 1, 1)
            keep_y(E - 2, 0, 16 * (E // 2 - 1))
            keep_y(E - 1, 1, 16 * (E // 2 - 1))
            n_over = act.value_load(k.n_over[0:1, 0:1], min_val=0, max_val=OVER)
            with act.Fori(0, OVER // 2) as jj:
                for u in range(2):
                    j = jj * 2 + u
                    with act.If(n_over > j):
                        keep_xT(j + E, u)
                        gate(j + E, u)
                        keep_y(j + E, u, jj * 16 + 16 * (E // 2))
            for u in range(2):
                act.wait_ge(y_out[u], (n_over + (1 - u)) // 2 * 16 + 16 * (E // 2))
                act.sem_inc(all_out, 1)

        @block.vector
        def _(dve):
            def keep_xT(e, u):
                dve.wait_ge(x_turned, e * 2 + 1)
                nc.vector.tensor_copy(xgT[:, u, 0:4, :], p_x[:, 0:4, :]).then_inc(xT_dve, 1)

            def hidden(e, u):
                dve.wait_ge(sig_done, e + 1)
                nc.vector.tensor_tensor(gs[:, u, :], sig[:, u, :], p_gu[:, u, 0:F], ALU.mult).then_inc(gs_done, 1)
                dve.wait_ge(gs_done, e + 1)
                nc.vector.tensor_tensor(h[:, u, :], gs[:, u, :], p_gu[:, u, F:2 * F], ALU.mult).then_inc(h_done, 1)

            def keep_hT(e, u):
                dve.wait_ge(h_turned, e + 1)
                nc.vector.tensor_copy(hT[:, u, :, :].rearrange("p k t -> p (k t)"), p_h[:, 0:KF * P]).then_inc(hT_done, 1)

            def keep_y(e, u, n):
                dve.wait_ge(y_done, e * 2 + 2)
                if n is not None:
                    dve.wait_ge(y_out[u], n)
                nc.vector.tensor_copy(y[:, u, 512:D], p_y[:, 512:D]).then_inc(y_dve, 1)

            keep_xT(0, 0)
            hidden(0, 0)
            keep_xT(1, 1)
            keep_hT(0, 0)
            keep_xT(2, 0)
            hidden(1, 1)
            keep_y(0, 0, None)
            keep_hT(1, 1)
            keep_xT(3, 1)
            hidden(2, 0)
            keep_y(1, 1, None)
            keep_hT(2, 0)
            with dve.Fori(1, E // 2 - 1) as ii:
                for u in range(2):
                    i = ii * 2 + u
                    keep_xT(i + 2, u)
                    hidden(i + 1, 1 - u)
                    keep_y(i, u, ii * 16)
                    keep_hT(i + 1, 1 - u)
            hidden(E - 1, 1)
            keep_y(E - 2, 0, 16 * (E // 2 - 1))
            keep_hT(E - 1, 1)
            keep_y(E - 1, 1, 16 * (E // 2 - 1))
            n_over = dve.value_load(k.n_over[0:1, 0:1], min_val=0, max_val=OVER)
            with dve.Fori(0, OVER // 2) as jj:
                for u in range(2):
                    j = jj * 2 + u
                    with dve.If(n_over > j):
                        keep_xT(j + E, u)
                        hidden(j + E, u)
                        keep_hT(j + E, u)
                        keep_y(j + E, u, jj * 16 + 16 * (E // 2))


def combine(nc, k):
    with ExitStack() as ctx:
        sb, ps, sem = makers(nc, ctx, "comb", k.held)
        g2 = sb("g2", [P, D], f32)
        b2 = sb("b2", [P, D], f32)
        NB = 12
        yb = sb("yb", [P, NB, D], f32)
        stats = sb("stats2", [P, 2, 6], f32)
        mv = sb("mv2", [P, 2, 2], f32)
        std = sb("std2", [P, 2], f32)
        rstd = sb("rstd2", [P, 1], f32)
        ln_in, own, var_done, std_done, out_done, out_sent = sem("ln2_in"), sem("c_own"), sem("var2"), sem("std2s"), sem("out_done"), sem("out_sent")
        y_in = [sem(f"y_in{b}") for b in range(NB)]
        y_used = sem("y_used")
        block = ctx.enter_context(nc.Block())

        @block.sync
        def _(sp):
            sp.dma_start(g2[:, :], k.ln2_g.to_broadcast([P, D])).then_inc(ln_in, 16)
            sp.dma_start(b2[:, :], k.ln2_b.to_broadcast([P, D])).then_inc(ln_in, 16)
            out = k.out[0].rearrange("(c j) d -> j c d", j=T)
            for t in range(T):
                sp.wait_ge(out_done, t + 1)
                sp.dma_start(out[t], k.x[:, t, :]).then_inc(out_sent, 16)
            sp.wait_ge(out_sent, 16 * T)

        @block.gpsimd
        def _(pool):
            for n in range(T * TOP_K):
                if n >= NB:
                    pool.wait_ge(y_used, n - NB + 1)
                nc.gpsimd.indirect_dma_start(yb[:, n % NB, :], None, k.y_d[:, :],
                                             bass.IndirectOffsetOnAxis(ap=k.dest[:, n:n + 1], axis=0)).then_inc(y_in[n % NB], 16)

        @block.scalar
        def _(act):
            for t in range(T):
                act.wait_ge(var_done, t + 1)
                nc.scalar.activation(std[:, t % 2:t % 2 + 1], mv[:, t % 2, 1:2], ACT.Sqrt).then_inc(std_done, 1)

        @block.vector
        def _(dve):
            ch = Chain(dve, own)
            for t in range(T):
                xt = k.x[:, t, :]
                for q in range(TOP_K):
                    n = t * TOP_K + q
                    dve.wait_ge(y_in[n % NB], 16 * (n // NB + 1))
                    if n:
                        dve.wait_ge(y_used, n)
                    nc.vector.scalar_tensor_tensor(xt, yb[:, n % NB, :], k.top_w[:, t, q:q + 1], xt, ALU.mult, ALU.add).then_inc(y_used, 1)
                dve.wait_ge(y_used, n + 1)
                nc.vector.bn_stats(stats[:, 0, :], k.x[:, t, 0:512])
                ch.link(nc.vector.bn_stats(stats[:, 1, :], k.x[:, t, 512:D]))
                ch.link(nc.vector.bn_aggr(mv[:, t % 2, :], stats[:, :, :].rearrange("p a b -> p (a b)")))
                nc.vector.tensor_scalar(mv[:, t % 2, 1:2], mv[:, t % 2, 1:2], LN_EPS, None, ALU.add).then_inc(var_done, 1)
                dve.wait_ge(std_done, t + 1)
                ch.link(nc.vector.reciprocal(rstd[:, :], std[:, t % 2:t % 2 + 1]))
                ch.link(nc.vector.tensor_scalar(xt, xt, mv[:, t % 2, 0:1], rstd[:, 0:1], ALU.subtract, ALU.mult))
                if t == 0:
                    dve.wait_ge(ln_in, 32)
                ch.link(nc.vector.tensor_tensor(xt, xt, g2[:, :], ALU.mult))
                nc.vector.tensor_tensor(xt, xt, b2[:, :], ALU.add).then_inc(out_done, 1)


def build(nc, k):
    with ExitStack() as ctx:
        k.held = []
        persistent(nc, ctx, k)
        shared = ctx.enter_context(ExitStack())
        with ExitStack() as mixers:
            mixer_tile, _, _ = makers(nc, mixers, "mixers")
            k.o = mixer_tile("o", [P, T, 512], f32)
            with ExitStack() as latents:
                sb, _, _ = makers(nc, latents, "latents")
                k.cqT = sb("cqT", [P, 2, SEQ], f32)
                k.ckvT = sb("ckvT", [P, SEQ], f32)
                k.kT = sb("kT", [DQ, 2, SEQ], f32)
                project(nc, k)
                attention(nc, k)
            with ExitStack() as states:
                sb, _, _ = makers(nc, states, "states")
                k.b1, k.b2, k.c1, k.c2, k.e1, k.f2 = [sb(n, [P, 2 * G, CH], f32) for n in ("b1", "b2", "c1", "c2", "e1", "f2")]
                k.pw = sb("pw", [P, 2, 2 * G, T + 1], f32)
                k.pb = sb("pb", [P, 2, 2 * G, T + 1], f32)
                k.t8 = sb("t8", [P, 2 * G], f32)
                k.m8 = sb("m8", [P, 2 * G], f32)
                s5_parameters(nc, k)
                s5_scan(nc, k)
            k.sT = mixer_tile("sT", [P, 4, SEQ], f32)
            s5_gate(nc, k)
            hand_back(nc, k.held)
            sb, _, sem = makers(nc, shared, "shared", k.held, side="right")
            k.x1T = sb("x1T", [P, KD, SEQ], f32)
            k.ws_gu = sb("gu", [P, KD, 2 * F], f32)
            k.ws_dn = sb("dn", [P, KF, D], f32)
            k.ws_in = sem("ws_in")
            mix_norm_route(nc, k)
        with ExitStack() as experts:
            sb, _, sem = makers(nc, experts, "ring", k.held)
            k.moe_gu = [sb(f"gu{e}", [P, KD, 2 * F], f32) for e in range(EARLY)]
            k.moe_dn = [sb(f"dn{e}", [P, KF, D], f32) for e in range(EARLY)]
            k.gu_in = [sem(f"gu_in{e}") for e in range(RING)]
            k.dn_in = [sem(f"dn_in{e}") for e in range(RING)]
            dispatch(nc, k)
            shared.close()
            moe_experts(nc, k)
        combine(nc, k)


_INS = ['x', 'w_in', 'lam_re', 'lam_im', 'log_dt', 'b_re', 'b_im', 'c_re', 'c_im', 'd_skip', 'w_glu', 'b_glu',
        'q_norm_g', 'w_uq', 'kv_norm_g', 'w_ukv', 'w_o', 'ln1_g', 'ln1_b', 'w_router', 'router_bias',
        'we_gate', 'we_up', 'we_down', 'ws_gate', 'ws_up', 'ws_down', 'ln2_g', 'ln2_b']


def kernel(**inputs):
    import numpy as _np
    import concourse.bacc as _bacc
    from concourse.bass_utils import run_bass_kernel_spmd as _run

    nc = _bacc.Bacc("TRN2", target_bir_lowering=False, num_devices=1)
    arrays, aps = {}, {}
    for name in _INS:
        a = _np.ascontiguousarray(inputs[name])
        arrays[f"in_{name}_dram"] = a
        aps[name] = nc.dram_tensor(f"in_{name}_dram", a.shape, mybir.dt.from_np(a.dtype), kind="ExternalInput").ap()
    c = constants()
    arrays["in_consts_dram"] = c
    aps["consts"] = nc.dram_tensor("in_consts_dram", c.shape, f32, kind="ExternalInput").ap()
    aps["out"] = nc.dram_tensor("out_0_dram", (1, SEQ, D), f32, kind="ExternalOutput").ap()
    build(nc, Kit(aps))
    r = _run(nc, [arrays], core_ids=[0])
    return r.results[0]["out_0_dram"]
```

```python
import math
from contextlib import ExitStack

import concourse.bass as bass
from concourse import mybir

f32 = mybir.dt.float32
i32 = mybir.dt.int32
u32 = mybir.dt.uint32
ALU = mybir.AluOpType
ACT = mybir.ActivationFunctionType
AX = mybir.AxisListType

P = 128
D = 1024
SEQ = 1024
T = 8
NC = SEQ // T
KD = D // P
D_SSM = 512
G = 32
CH = 16
N = 64
Q_RANK = 256
KV_RANK = 128
HEADS = 8
NOPE = 64
ROPE = 32
DQ = NOPE + ROPE
DV = 64
N_EXPERTS = 64
TOP_K = 6
EGROUPS = 8
TOP_GROUPS = 4
F = 256
KF = F // P
RING = 4
EARLY = 3
OVER = SEQ * TOP_K // P
SPAN = 16
SLOTS = (N_EXPERTS + OVER) * P
ROUTED_SCALE = 2.5
ALPHA = 2.0 ** 0.25
LN_EPS = 1e-5
RMS_EPS = 1e-6
BIG = 1e30
TWO_PI = 2.0 * math.pi
ROUND = 1.5 * 2.0 ** 23


def makers(nc, ctx, stage, held=None, side=None):
    def sb(name, shape, dt):
        return ctx.enter_context(nc.sbuf_tensor(f"{stage}_{name}", shape, dt, side=side))

    def ps(name, shape):
        return ctx.enter_context(nc.psum_tensor(f"{stage}_{name}", shape, f32))

    def sem(name):
        held.append(nc.alloc_semaphore(name=f"{stage}_{name}"))
        return held[-1]
    return sb, ps, sem


def hand_back(nc, held):
    nc.all_engine_barrier()
    nc.clear_and_free_semaphores(held)
    nc.all_engine_barrier()
    held.clear()


class Kit:

    def __init__(self, given):
        self.x_in = given["x"]
        self.w_in, self.lam_re, self.lam_im, self.log_dt = [given[n] for n in ("w_in", "lam_re", "lam_im", "log_dt")]
        self.b_re, self.b_im, self.c_re, self.c_im = [given[n] for n in ("b_re", "b_im", "c_re", "c_im")]
        self.d_skip, self.w_glu, self.b_glu, self.q_norm_g = [given[n] for n in ("d_skip", "w_glu", "b_glu", "q_norm_g")]
        self.w_uq, self.kv_norm_g, self.w_ukv, self.w_o = [given[n] for n in ("w_uq", "kv_norm_g", "w_ukv", "w_o")]
        self.ln1_g, self.ln1_b, self.w_router, self.router_bias = [given[n] for n in ("ln1_g", "ln1_b", "w_router", "router_bias")]
        self.we_gate, self.we_up, self.we_down, self.ws_gate = [given[n] for n in ("we_gate", "we_up", "we_down", "ws_gate")]
        self.ws_up, self.ws_down, self.ln2_g, self.ln2_b = [given[n] for n in ("ws_up", "ws_down", "ln2_g", "ln2_b")]
        self.consts, self.out = [given[n] for n in ("consts", "out")]


class Chain:

    def __init__(self, eng, sem, base=0):
        self.eng, self.sem, self.base, self.n = eng, sem, base, 0

    def link(self, ins):
        self.n += 1
        ins.then_inc(self.sem, 1)
        self.eng.wait_ge(self.sem, self.base + self.n)


C_ID, C_TRI, C_ONE, C_CHUNK, C_CHUNKR, C_COS, C_SIN, C_E, C_E128, C_TOK, C_PART, C_SGN, C_END = [
    0, 128, 256, 384, 512, 640, 768, 896, 960, 1024, 1032, 1033, 1036]


def constants():
    import numpy as np
    c = np.zeros((P, C_END), np.float32)
    p = np.arange(P)
    c[:, C_ID:C_ID + P] = np.eye(P)
    c[:, C_TRI:C_TRI + P] = p[:, None] < p[None, :]
    c[:, C_ONE:C_ONE + P] = 1.0
    c[:, C_CHUNK:C_CHUNK + P] = p[None, :]
    c[:, C_CHUNKR:C_CHUNKR + P] = P - 1 - p[None, :]
    inv = (np.float32(10000.0) ** (-np.arange(0, ROPE, 2, dtype=np.float32) / np.float32(ROPE))).astype(np.float32)
    pos = (T * p[:, None] + np.arange(T)[None, :]).astype(np.float32)
    ang = (pos[:, :, None] * inv[None, None, :]).astype(np.float32).astype(np.float64)
    c[:, C_COS:C_COS + P] = np.cos(ang).reshape(P, P)
    c[:, C_SIN:C_SIN + P] = np.sin(ang).reshape(P, P)
    c[:, C_E:C_E + N_EXPERTS] = np.arange(N_EXPERTS)[None, :]
    c[:, C_E128:C_E128 + N_EXPERTS] = P * np.arange(N_EXPERTS)[None, :]
    c[:, C_TOK:C_TOK + T] = p[:, None] + P * np.arange(T)[None, :]
    c[:, C_PART] = p
    c[:, C_SGN] = np.where(p < N, 1.0, -1.0)
    c[:, C_SGN + 2] = math.pi / 2
    c[:, C_SGN + 1] = np.float32(6.2831850) * c[:, C_SGN]
    return c


def persistent(nc, ctx, k):
    sb, _, _ = makers(nc, ctx, "all")
    const = sb("const", [P, C_END], f32)
    k.const = const
    k.ident = const[:, C_ID:C_ID + P]
    k.tri = const[:, C_TRI:C_TRI + P]
    k.ones = const[:, C_ONE:C_ONE + P]
    k.iota_e = const[:, C_E:C_E + N_EXPERTS]
    k.iota_e128 = const[:, C_E128:C_E128 + N_EXPERTS]
    k.tok = const[:, C_TOK:C_TOK + T]
    k.cos = const[:, C_COS:C_COS + P].rearrange("p (t f) -> p t f", t=T)
    k.sin = const[:, C_SIN:C_SIN + P].rearrange("p (t f) -> p t f", t=T)
    k.chunk = const[:, C_CHUNK:C_CHUNK + NC]
    k.chunkr = const[:, C_CHUNKR:C_CHUNKR + NC]
    k.sgn = const[:, C_SGN:C_SGN + 1]
    k.sgn2pi = const[:, C_SGN + 1:C_SGN + 2]
    k.half_pi = const[:, C_SGN + 2:C_SGN + 3]
    k.part = const[:, C_PART:C_PART + 1]
    k.x = sb("x_sb", [P, T, D], f32)
    k.rank = sb("rank", [P, T, N_EXPERTS], f32)
    k.counts = sb("counts", [P, N_EXPERTS], f32)
    k.picked = sb("picked", [P, T, TOP_K], f32)
    k.top_w = sb("top_w", [P, T, TOP_K], f32)
    k.dest = sb("dest_i", [P, T * TOP_K], i32)
    k.block_tok = sb("block_tok", [P, N_EXPERTS + OVER], i32)
    k.over_expert = sb("over_expert", [1, OVER], i32)
    k.n_over = sb("n_over", [1, 1], i32)
    k.x1_d = nc.dram_tensor("x1_d", (SEQ, D), f32).ap()
    k.y_d = nc.dram_tensor("y_d", (SLOTS, D), f32).ap()
    k.slot_tok_d = nc.dram_tensor("slot_tok_d", (SLOTS, 1), f32).ap()
    k.u_d = nc.dram_tensor("u_d", (D_SSM, SEQ), f32).ap()
    k.ys_d = nc.dram_tensor("ys_d", (D_SSM, SEQ), f32).ap()
    k.expert_d = nc.dram_tensor("expert_d", (P,), i32).ap()


def project(nc, k):
    DG = 2 * G
    C1, C2 = 6.28125, TWO_PI - 6.28125
    PI = 3.1415925
    NCV = Q_RANK + KV_RANK + ROPE
    with ExitStack() as ctx:
        sb, ps, sem = makers(nc, ctx, "proj", k.held)
        w = sb("w", [P, KD, D_SSM + NCV], f32)
        xT = sb("xT", [P, KD, SEQ], f32)
        uT = sb("uT", [P, 4, SEQ], f32)
        c = sb("c", [P, T, NCV], f32)
        sq = sb("sq", [P, Q_RANK], f32)
        ssq = sb("ssq", [P, 2, T], f32)
        ms = sb("ms", [P, 2, T], f32)
        rms = sb("rms", [P, 2, T], f32)
        gq = sb("gq", [P, 2], f32)
        gkv = sb("gkv", [P, 1], f32)
        p_x = ps("p_x", [P, 2, KD, P])
        p_c = ps("p_c", [P, 2, 512])
        p_u = ps("p_u", [P, 2, 512])
        const_in, w_in, wu_in, g_in, u_out = sem("const_in"), sem("w_in"), sem("wu_in"), sem("g_in"), sem("u_out")
        x_in = [sem(f"x_in{t}") for t in range(T)]
        x_turned, xT_dve, xT_act = sem("x_turned"), sem("xT_dve"), sem("xT_act")
        c_done, c_read, sq_done, ms_done, rms_done = sem("c_done"), sem("c_read"), sem("sq_done"), sem("ms_done"), sem("rms_done")
        u_done, u_read, scaled, c_turned, cT_read, own = sem("u_done"), sem("u_read"), sem("scaled"), sem("c_turned"), sem("cT_read"), sem("own")
        lr = sb("lr", [DG, P], f32)
        li = sb("li", [DG, P], f32)
        dt = sb("dt", [DG, 2], f32)
        mag = sb("mag", [DG, P], f32)
        th = sb("th", [DG, P], f32)
        turns = sb("turns", [DG, P], f32)
        tmp = sb("tmp", [DG, 2, P], f32)
        cs = sb("cs", [DG, 2, P], f32)
        par = sb("par", [DG, 6, P], f32)
        ar, ai, kr, ki, t8, m8 = [par[:, i, :] for i in range(6)]
        prm = sb("prm", [P, 6, DG], f32)
        b1 = sb("b1", [P, DG, CH], f32)
        b2 = sb("b2", [P, DG, CH], f32)
        c_rows = sb("c_rows", [P, 8, 3 * N], f32)
        ba, bb = k.e1, k.f2
        spare = k.pb[:, :, :, :].rearrange("p i g s -> p (i g s)")
        pt = spare[:, 0:4 * DG * 4].rearrange("p (i g m) -> p i g m", i=4, g=DG)
        rot = spare[:, 0:4 * T * (ROPE // 2)].rearrange("p (i t f) -> p i t f", i=4, t=T)
        p_p = p_x[:, 0, 0:4, :].rearrange("p k t -> p (k t)")
        lam_in, b_in, cm_in = sem("lam_in"), sem("b_in"), sem("cm_in")
        dt_done, lr_done, mag_done, ang_done, cs_done, par_done = sem("dt_done"), sem("lr_done"), sem("mag_done"), sem("ang_done"), sem("cs_done"), sem("par_done")
        par_turned, prm_kept, cm_turned = sem("par_turned"), sem("prm_kept"), sem("cm_turned")
        block = ctx.enter_context(nc.Block())

        @block.sync
        def _(sp):
            sp.dma_start(k.const[:, :], k.consts).then_inc(const_in, 16)
            xv = k.x_in[0].rearrange("(c j) d -> c j d", j=T)
            wv = k.w_in[0].rearrange("(p k) n -> p k n", k=KD)
            for t in range(T):
                sp.dma_start(k.x[:, t, :], xv[:, t, :]).then_inc(x_in[t], 16)
                if t == 0:
                    sp.dma_start(w[:, :, D_SSM:], wv[:, :, D_SSM:]).then_inc(w_in, 16)
            sp.dma_start(w[:, :, 0:D_SSM], wv[:, :, 0:D_SSM]).then_inc(wu_in, 16)
            for kk in range(2):
                sp.dma_start(gq[:, kk:kk + 1], k.q_norm_g[0, kk * P:(kk + 1) * P].rearrange("(p o) -> p o", o=1)).then_inc(g_in, 16)
            sp.dma_start(gkv[:, :], k.kv_norm_g[0].rearrange("(p o) -> p o", o=1)).then_inc(g_in, 16)
            for half in range(2):
                cols = slice(half * N, (half + 1) * N)
                sp.dma_start(lr[:, cols], k.lam_re[0].rearrange("d g n -> (d g) n")).then_inc(lam_in, 16)
                sp.dma_start(li[:, cols], k.lam_im[0].rearrange("d g n -> (d g) n")).then_inc(lam_in, 16)
            sp.dma_start(dt[:, 0:1], k.log_dt[0].rearrange("d (g o) -> (d g) o", o=1)).then_inc(lam_in, 16)
            for half in range(2):
                rows, other = slice(half * N, (half + 1) * N), slice((1 - half) * N, (2 - half) * N)
                src = (k.b_re, k.b_im)[half][0].rearrange("d g n p -> n (d g) p")
                sp.dma_start(b1[rows, :, :], src).then_inc(b_in, 16)
                sp.dma_start(b2[other, :, :], src).then_inc(b_in, 16)
            for i, src in enumerate((k.c_re, k.c_im, k.c_re)):
                sp.dma_start(c_rows[:, :, i * N:(i + 1) * N],
                             src[0].rearrange("d g p n -> (d g p) n").rearrange("(a r) n -> r a n", r=P)).then_inc(cm_in, 16)
            for m in range(4):
                sp.wait_ge(u_read, 2 * m + 2)
                sp.dma_start(k.u_d[m * P:(m + 1) * P, :], uT[:, m, :]).then_inc(u_out, 16)
            sp.wait_ge(u_out, 16 * 4)

        @block.tensor
        def _(pe):
            def turn_x(t):
                pe.wait_ge(x_in[t], 16)
                if t >= 2:
                    pe.wait_ge(xT_dve, t - 1)
                    pe.wait_ge(xT_act, t - 1)
                for half in range(2):
                    for q in range(4):
                        kk = half * 4 + q
                        last = nc.tensor.transpose(p_x[:, t % 2, kk, :], k.x[:, t, kk::KD], k.ident)
                    last.then_inc(x_turned, 1)

            def turn_c(t):
                pe.wait_ge(scaled, t + 1)
                if t >= 2:
                    pe.wait_ge(cT_read, t - 1)
                nc.tensor.transpose(p_c[:, t % 2, 0:P], c[:, t, 0:P], k.ident)
                nc.tensor.transpose(p_c[:, t % 2, P:2 * P], c[:, t, P:2 * P], k.ident)
                nc.tensor.transpose(p_c[:, t % 2, 2 * P:3 * P], c[:, t, 2 * P:3 * P], k.ident)
                nc.tensor.transpose(p_c[0:DQ, t % 2, 3 * P:4 * P], c[:, t, NCV - DQ:NCV], k.ident).then_inc(c_turned, 1)

            pe.wait_ge(const_in, 16)
            turn_x(0)
            for t in range(T):
                if t + 1 < T:
                    turn_x(t + 1)
                pe.wait_ge(xT_dve, t + 1)
                pe.wait_ge(xT_act, t + 1)
                if t == 0:
                    pe.wait_ge(w_in, 16)
                if t >= 2:
                    pe.wait_ge(c_read, t - 1)
                for kk in range(KD):
                    last = nc.tensor.matmul(p_c[:, t % 2, 0:NCV], xT[:, kk, t * P:(t + 1) * P], w[:, kk, D_SSM:],
                                            start=(kk == 0), stop=(kk == KD - 1))
                last.then_inc(c_done, 1)
            pe.wait_ge(wu_in, 16)
            for n in range(8):
                m, half = n // 2, n % 2
                if n == 3:
                    pe.wait_ge(par_done, 1)
                    for i in range(6):
                        last = nc.tensor.transpose(p_p[:, i * DG:(i + 1) * DG], par[:, i, :], k.ident[0:DG, 0:DG])
                    last.then_inc(par_turned, 1)
                if n == 4:
                    pe.wait_ge(cm_in, 48)
                    pe.wait_ge(prm_kept, 1)
                    for order in range(2):
                        for a in range(8):
                            last = nc.tensor.transpose(p_x[:, order, a, :], c_rows[:, a, order * N:order * N + P], k.ident)
                    last.then_inc(cm_turned, 1)
                if n >= 5:
                    for t in range(2 * (n - 5), 2 * (n - 4)):
                        turn_c(t)
                if n >= 2:
                    pe.wait_ge(u_read, n - 1)
                for kk in range(KD):
                    last = nc.tensor.matmul(p_u[:, n % 2, :], w[:, kk, m * P:(m + 1) * P], xT[:, kk, half * 512:(half + 1) * 512],
                                            start=(kk == 0), stop=(kk == KD - 1))
                last.then_inc(u_done, 1)
            for t in range(T - 2, T):
                turn_c(t)

        @block.scalar
        def _(act):
            for t in range(T):
                act.wait_ge(x_turned, 2 * t + 2)
                nc.scalar.activation(xT[:, 4:8, t * P:(t + 1) * P], p_x[:, t % 2, 4:8, :], ACT.Copy).then_inc(xT_act, 1)
            act.wait_ge(lam_in, 80)
            nc.scalar.activation(dt[:, 1:2], dt[:, 0:1], ACT.Exp).then_inc(dt_done, 1)
            for t in range(T):
                act.wait_ge(c_read, t + 1)
                if t:
                    act.wait_ge(sq_done, 2 * t)
                nc.scalar.activation(sq[:, :], c[:, t, 0:Q_RANK], ACT.Square, accum_out=ssq[:, 0, t:t + 1]).then_inc(sq_done, 1)
                act.wait_ge(sq_done, 2 * t + 1)
                nc.scalar.activation(sq[:, 0:KV_RANK], c[:, t, Q_RANK:Q_RANK + KV_RANK], ACT.Square,
                                     accum_out=ssq[:, 1, t:t + 1]).then_inc(sq_done, 1)
            act.wait_ge(lr_done, 1)
            act.wait_ge(dt_done, 1)
            nc.scalar.activation(mag[:, :], lr[:, :], ACT.Exp, scale=dt[:, 1:2]).then_inc(mag_done, 1)
            act.wait_ge(ang_done, 1)
            nc.scalar.activation(cs[:, :, :], tmp[:, :, :], ACT.Sin).then_inc(cs_done, 1)
            act.wait_ge(ms_done, 1)
            nc.scalar.activation(rms[:, :, :], ms[:, :, :], ACT.Sqrt).then_inc(rms_done, 1)
            for n in range(8):
                m, half = n // 2, n % 2
                act.wait_ge(u_done, n + 1)
                nc.scalar.activation(uT[:, m, half * 512:(half + 1) * 512], p_u[:, n % 2, :], ACT.Copy).then_inc(u_read, 1)

        @block.vector
        def _(dve):
            ch = Chain(dve, own)
            tt, ts_, stt = nc.vector.tensor_tensor, nc.vector.tensor_scalar, nc.vector.scalar_tensor_tensor

            def keep_c(t):
                dve.wait_ge(c_done, t + 1)
                nc.vector.tensor_copy(c[:, t, :], p_c[:, t % 2, 0:NCV]).then_inc(c_read, 1)

            for t in range(T):
                dve.wait_ge(x_turned, 2 * t + 1)
                nc.vector.tensor_copy(xT[:, 0:4, t * P:(t + 1) * P], p_x[:, t % 2, 0:4, :]).then_inc(xT_dve, 1)
                if t:
                    keep_c(t - 1)
            keep_c(T - 1)
            dve.wait_ge(lam_in, 80)
            ts_(lr[:, :], lr[:, :], -1e-4, None, ALU.min).then_inc(lr_done, 1)
            dve.wait_ge(dt_done, 1)
            dve.wait_ge(lr_done, 1)
            ch.link(ts_(th[:, :], li[:, :], dt[:, 1:2], None, ALU.mult))
            ch.link(ts_(turns[:, :], th[:, :], 1.0 / TWO_PI, ROUND, ALU.mult, ALU.add))
            ch.link(ts_(turns[:, :], turns[:, :], -ROUND, None, ALU.add))
            ch.link(stt(th[:, :], turns[:, :], -C1, th[:, :], ALU.mult, ALU.add))
            ch.link(stt(th[:, :], turns[:, :], -C2, th[:, :], ALU.mult, ALU.add))
            ch.link(ts_(th[:, :], th[:, :], PI, -PI, ALU.min, ALU.max))
            nc.vector.tensor_copy(tmp[:, 0, :], th[:, :])
            ch.link(stt(tmp[:, 1, :], th[:, :], -1.0, th[:, :], ALU.mult, ALU.max))
            ts_(tmp[:, 1, :], tmp[:, 1, :], -1.0, math.pi / 2, ALU.mult, ALU.add).then_inc(ang_done, 1)
            dve.wait_ge(sq_done, 2 * T)
            nc.vector.tensor_scalar(ms[:, 0, :], ssq[:, 0, :], 1.0 / Q_RANK, RMS_EPS, ALU.mult, ALU.add)
            nc.vector.tensor_scalar(ms[:, 1, :], ssq[:, 1, :], 1.0 / KV_RANK, RMS_EPS, ALU.mult, ALU.add).then_inc(ms_done, 1)
            c1, c2 = c[:, :, NCV - 32:NCV - 16], c[:, :, NCV - 16:NCV]
            dve.wait_ge(c_read, T)
            nc.vector.tensor_tensor(rot[:, 0], c1, k.cos, ALU.mult)
            nc.vector.tensor_tensor(rot[:, 1], c2, k.sin, ALU.mult)
            nc.vector.tensor_tensor(rot[:, 2], c1, k.sin, ALU.mult)
            ch.link(nc.vector.tensor_tensor(rot[:, 3], c2, k.cos, ALU.mult))
            nc.vector.tensor_tensor(c1, rot[:, 0], rot[:, 1], ALU.subtract)
            ch.link(nc.vector.tensor_tensor(c2, rot[:, 2], rot[:, 3], ALU.add))
            dve.wait_ge(rms_done, 1)
            ch.link(nc.vector.reciprocal(rms[:, :, :], rms[:, :, :]))
            for t in range(T):
                nc.vector.tensor_scalar(c[:, t, 0:Q_RANK], c[:, t, 0:Q_RANK], rms[:, 0, t:t + 1], None, ALU.mult)
                nc.vector.tensor_scalar(c[:, t, Q_RANK:Q_RANK + KV_RANK], c[:, t, Q_RANK:Q_RANK + KV_RANK],
                                        rms[:, 1, t:t + 1], None, ALU.mult).then_inc(scaled, 1)
            dve.wait_ge(mag_done, 1)
            dve.wait_ge(cs_done, 1)
            tt(ar, mag[:, :], cs[:, 1, :], ALU.mult)
            ch.link(tt(ai, mag[:, :], cs[:, 0, :], ALU.mult))
            tt(tmp[:, 0, :], lr[:, :], lr[:, :], ALU.mult)
            ch.link(tt(tmp[:, 1, :], li[:, :], li[:, :], ALU.mult))
            ch.link(tt(turns[:, :], tmp[:, 0, :], tmp[:, 1, :], ALU.add))
            nc.vector.reciprocal(turns[:, :], turns[:, :])
            ts_(cs[:, 0, :], ar, -1.0, None, ALU.add)
            ch.link(tt(tmp[:, 1, :], ai, li[:, :], ALU.mult))
            ch.link(tt(tmp[:, 0, :], cs[:, 0, :], lr[:, :], ALU.mult))
            ch.link(tt(kr, tmp[:, 0, :], tmp[:, 1, :], ALU.add))
            tt(tmp[:, 0, :], ai, lr[:, :], ALU.mult)
            ch.link(tt(tmp[:, 1, :], cs[:, 0, :], li[:, :], ALU.mult))
            ch.link(tt(ki, tmp[:, 0, :], tmp[:, 1, :], ALU.subtract))
            tt(kr, kr, turns[:, :], ALU.mult)
            tt(ki, ki, turns[:, :], ALU.mult)
            ch.link(ts_(th[:, :], th[:, :], T / TWO_PI, None, ALU.mult))
            ch.link(ts_(cs[:, 1, :], th[:, :], ROUND, -ROUND, ALU.add, ALU.add))
            tt(t8, th[:, :], cs[:, 1, :], ALU.subtract)
            ch.link(tt(m8, mag[:, :], mag[:, :], ALU.mult))
            ch.link(tt(m8, m8, m8, ALU.mult))
            tt(m8, m8, m8, ALU.mult).then_inc(par_done, 1)
            dve.wait_ge(par_turned, 1)
            ch.link(nc.vector.tensor_copy(prm[:, :, :], p_p[:, 0:6 * DG].rearrange("p (i g) -> p i g", i=6)))
            dve.sem_inc(prm_kept, 1)
            nc.vector.tensor_copy(k.t8[:, :], prm[:, 4, :])
            nc.vector.tensor_copy(k.m8[:, :], prm[:, 5, :])
            dve.wait_ge(b_in, 64)
            wide = [P, DG, CH]
            krb, kib = prm[:, 2, :].unsqueeze(2).to_broadcast(wide), prm[:, 3, :].unsqueeze(2).to_broadcast(wide)
            ch.link(ts_(b2[:, :, :], b2[:, :, :], k.sgn, -1.0, ALU.mult, ALU.mult))
            tt(ba[:, :, :], b1[:, :, :], krb, ALU.mult)
            ch.link(tt(bb[:, :, :], b2[:, :, :], kib, ALU.mult))
            ch.link(tt(k.b1[:, :, :], ba[:, :, :], bb[:, :, :], ALU.add))
            tt(ba[:, :, :], b2[:, :, :], krb, ALU.mult)
            ch.link(tt(bb[:, :, :], b1[:, :, :], kib, ALU.mult))
            ch.link(tt(k.b2[:, :, :], ba[:, :, :], bb[:, :, :], ALU.subtract))
            nc.vector.memset(k.pw[:, 0, :, 0:1], 1.0)
            nc.vector.memset(k.pw[:, 1, :, 0:1], 0.0)
            nc.vector.tensor_copy(k.pw[:, 0, :, 1], prm[:, 0, :])
            ch.link(nc.vector.tensor_copy(k.pw[:, 1, :, 1], prm[:, 1, :]))
            for m in (1, 2, 4):
                w = [P, DG, m]
                re, im = k.pw[:, 0, :, 1:1 + m], k.pw[:, 1, :, 1:1 + m]
                sr, si = k.pw[:, 0, :, m:m + 1].to_broadcast(w), k.pw[:, 1, :, m:m + 1].to_broadcast(w)
                tt(pt[:, 0, :, 0:m], re, sr, ALU.mult)
                tt(pt[:, 1, :, 0:m], im, si, ALU.mult)
                tt(pt[:, 2, :, 0:m], re, si, ALU.mult)
                ch.link(tt(pt[:, 3, :, 0:m], im, sr, ALU.mult))
                tt(k.pw[:, 0, :, 1 + m:1 + 2 * m], pt[:, 0, :, 0:m], pt[:, 1, :, 0:m], ALU.subtract)
                ch.link(tt(k.pw[:, 1, :, 1 + m:1 + 2 * m], pt[:, 2, :, 0:m], pt[:, 3, :, 0:m], ALU.add))
            for i in range(2):
                ch.link(nc.vector.tensor_copy(k.pb[:, i, :, :], k.pw[:, i, :, ::-1]))
            dve.wait_ge(cm_turned, 1)
            cr = p_x[:, 0].rearrange("p a (g c) -> p (a g) c", c=CH)
            ci = p_x[:, 1].rearrange("p a (g c) -> p (a g) c", c=CH)
            nc.vector.tensor_copy(k.c1[:, :, :], cr)
            nc.vector.tensor_copy(k.c2[:, :, :], ci)
            ts_(k.e1[:, :, :], cr, k.sgn, None, ALU.mult)
            ts_(k.f2[:, :, :], ci, k.sgn, -1.0, ALU.mult, ALU.mult)
            dve.wait_ge(g_in, 48)
            for t in range(T):
                cols = slice(t * P, (t + 1) * P)
                dve.wait_ge(c_turned, t + 1)
                nc.vector.tensor_scalar(k.cqT[:, 0, cols], p_c[:, t % 2, 0:P], gq[:, 0:1], None, ALU.mult)
                nc.vector.tensor_scalar(k.cqT[:, 1, cols], p_c[:, t % 2, P:2 * P], gq[:, 1:2], None, ALU.mult)
                nc.vector.tensor_scalar(k.ckvT[:, cols], p_c[:, t % 2, 2 * P:3 * P], gkv[:, 0:1], None, ALU.mult)
                for u in range(2):
                    last = nc.vector.tensor_copy(k.kT[NOPE:DQ, u, cols], p_c[NOPE:DQ, t % 2, 3 * P:4 * P])
                last.then_inc(cT_read, 1)


def attention(nc, k):
    SCALE = DQ ** -0.5
    with ExitStack() as ctx:
        sb, ps, sem = makers(nc, ctx, "att", k.held)
        wq = sb("wq", [P, 2, 2, DQ], f32)
        wkv = sb("wkv", [P, 2, NOPE + DV], f32)
        q = sb("q", [P, T, DQ], f32)
        rot = sb("rot", [P, 4, T, ROPE // 2], f32)
        qT = sb("qT", [DQ, 2, SEQ], f32)
        v = sb("v", [P, 2, T, DV], f32)
        nmax = sb("nmax", [P, 2], f32)
        bias = sb("bias", [P, 2], f32)
        total = sb("total", [P, 4], f32)
        rtotal = sb("rtotal", [P, 2], f32)
        pr = sb("pr", [P, 2, SEQ], f32)
        prT = sb("prT", [P, 2, T, P], f32)
        p_s = ps("p_s", [P, 2, SEQ])
        p_t = ps("p_t", [P, T, P])
        p_o = ps("p_o", [P, 512])
        p_p = ps("p_p", [P, 512])
        kT = k.kT
        w_in = [sem(f"w_in{u}") for u in range(2)]
        part_done, part_kept, q_rotated = sem("part_done"), sem("part_kept"), sem("q_rotated")
        scored, biased, probs, p_turned, pT_dve, pT_act = sem("scored"), sem("biased"), sem("probs"), sem("p_turned"), sem("pT_dve"), sem("pT_act")
        o_done, o_read, own = sem("o_done"), sem("o_read"), sem("own")
        PARTS = ("q", "q", "k", "k", "qT", "qT", "v")
        ROTATE = 2
        LINKS = 2 * T + 1
        block = ctx.enter_context(nc.Block())

        @block.sync
        def _(sp):
            def load(h, u):
                sp.dma_start(wq[:, u], k.w_uq[0].rearrange("(k p) n -> p k n", p=P)[:, :, bass.ds(h * DQ, DQ)]).then_inc(w_in[u], 16)
                sp.dma_start(wkv[:, u, :], k.w_ukv[0][:, bass.ds(h * (NOPE + DV), NOPE + DV)]).then_inc(w_in[u], 16)
            load(0, 0)
            load(1, 1)
            with sp.Fori(1, HEADS // 2) as hh:
                for u in range(2):
                    h = hh * 2 + u
                    sp.wait_ge(part_done, (h - 1) * len(PARTS))
                    load(h, u)

        @block.tensor
        def _(pe):
            def scores(h, u, t):
                if t == 0:
                    pe.wait_ge(part_kept, h * len(PARTS) + 6)
                for half in range(2):
                    last = nc.tensor.matmul(p_s[:, t % 2, half * 512:(half + 1) * 512], qT[:, u, t * P:(t + 1) * P],
                                            kT[:, u, half * 512:(half + 1) * 512], start=True, stop=True)
                last.then_inc(scored, 1)

            def part(h, u, i, nth_weights=None, first=False):
                what, second = PARTS[i], PARTS[:i].count(PARTS[i])
                if nth_weights is not None:
                    pe.wait_ge(w_in[u], nth_weights)
                if not first:
                    pe.wait_ge(part_kept, h * len(PARTS) + i)
                if what == "q":
                    for r in range(4):
                        t = second * 4 + r
                        for kk in range(2):
                            last = nc.tensor.matmul(p_p[:, r * DQ:(r + 1) * DQ], k.cqT[:, kk, t * P:(t + 1) * P],
                                                    wq[:, u, kk, :], start=(kk == 0), stop=(kk == 1))
                elif what == "k":
                    last = nc.tensor.matmul(p_p[0:NOPE, :], wkv[:, u, 0:NOPE], k.ckvT[:, second * 512:(second + 1) * 512],
                                            start=True, stop=True)
                elif what == "v":
                    for t in range(T):
                        last = nc.tensor.matmul(p_p[:, t * DV:(t + 1) * DV], k.ckvT[:, t * P:(t + 1) * P], wkv[:, u, NOPE:],
                                                start=True, stop=True)
                else:
                    if second == 0:
                        pe.wait_ge(q_rotated, h + 1)
                    for r in range(4):
                        last = nc.tensor.transpose(p_p[0:DQ, r * P:(r + 1) * P], q[:, second * 4 + r, :], k.ident)
                last.then_inc(part_done, 1)

            def head(hh, u, following):
                h = hh * 2 + u
                for t in range(T):
                    n = h * T + t
                    pe.wait_ge(probs, n + 1)
                    for half in range(2):
                        for r in range(4):
                            j = half * 4 + r
                            last = nc.tensor.transpose(p_t[:, j, :], pr[:, t % 2, j * P:(j + 1) * P], k.ident)
                        last.then_inc(p_turned, 1)
                    if t + 2 < T:
                        scores(h, u, t + 2)
                    elif following:
                        scores(h + 1, 1 - u, t + 2 - T)
                    if following and t < len(PARTS):
                        part(h + 1, 1 - u, t, (hh + u) * 32 + 32 if t == 0 else None)
                    pe.wait_ge(pT_dve, n + 1)
                    pe.wait_ge(pT_act, n + 1)
                    if t == 0:
                        pe.wait_ge(part_kept, h * len(PARTS) + 7)
                    pe.wait_ge(o_read, n + 1)
                    for j in range(T):
                        last = nc.tensor.matmul(p_o[:, 0:DV], prT[:, t % 2, j, :], v[:, u, j, :], start=(j == 0), stop=(j == T - 1))
                    last.then_inc(o_done, 1)

            for i in range(len(PARTS)):
                part(0, 0, i, 32 if i == 0 else None, first=(i == 0))
            scores(0, 0, 0)
            scores(0, 0, 1)
            with pe.Fori(0, HEADS // 2 - 1) as hh:
                for u in range(2):
                    head(hh, u, True)
            head(HEADS // 2 - 1, 0, True)
            head(HEADS // 2 - 1, 1, False)

        @block.scalar
        def _(act):
            def keep_part(h, u, i):
                what, second = PARTS[i], PARTS[:i].count(PARTS[i])
                act.wait_ge(part_done, h * len(PARTS) + (i + 1))
                if what == "q":
                    last = nc.scalar.activation(q[:, 4 * second:4 * second + 4, :].rearrange("p t n -> p (t n)"), p_p[:, 0:4 * DQ], ACT.Copy)
                elif what == "k":
                    last = nc.scalar.activation(kT[0:NOPE, u, second * 512:(second + 1) * 512], p_p[0:NOPE, :], ACT.Copy)
                elif what == "v":
                    last = nc.scalar.activation(v[:, u].rearrange("p t n -> p (t n)"), p_p[:, :], ACT.Copy)
                else:
                    last = nc.scalar.activation(qT[:, u, second * 512:(second + 1) * 512], p_p[0:DQ, :], ACT.Copy)
                last.then_inc(part_kept, 1)

            def head(hh, u, following):
                h = hh * 2 + u
                for t in range(T):
                    n = h * T + t
                    act.wait_ge(biased, n + 1)
                    nc.scalar.activation(pr[:, t % 2, :], p_s[:, t % 2, :], ACT.Exp, bias=bias[:, t % 2:t % 2 + 1], scale=SCALE,
                                         accum_out=total[:, t % 4:t % 4 + 1]).then_inc(probs, 1)
                    if following and t:
                        keep_part(h + 1, 1 - u, t - 1)
                    act.wait_ge(p_turned, 2 * n + 2)
                    nc.scalar.activation(prT[:, t % 2, 4:8, :], p_t[:, 4:8, :], ACT.Copy).then_inc(pT_act, 1)

            for i in range(len(PARTS)):
                keep_part(0, 0, i)
            with act.Fori(0, HEADS // 2 - 1) as hh:
                for u in range(2):
                    head(hh, u, True)
            head(HEADS // 2 - 1, 0, True)
            head(HEADS // 2 - 1, 1, False)

        @block.vector
        def _(dve):
            def rotate(ch, h):
                dve.wait_ge(part_kept, h * len(PARTS) + 2)
                q1, q2 = q[:, :, NOPE:NOPE + 16], q[:, :, NOPE + 16:DQ]
                nc.vector.tensor_tensor(rot[:, 0], q1, k.cos, ALU.mult)
                nc.vector.tensor_tensor(rot[:, 1], q2, k.sin, ALU.mult)
                nc.vector.tensor_tensor(rot[:, 2], q1, k.sin, ALU.mult)
                ch.link(nc.vector.tensor_tensor(rot[:, 3], q2, k.cos, ALU.mult))
                nc.vector.tensor_tensor(q1, rot[:, 0], rot[:, 1], ALU.subtract)
                nc.vector.tensor_tensor(q2, rot[:, 2], rot[:, 3], ALU.add).then_inc(q_rotated, 1)

            def top(ch, h, t):
                dve.wait_ge(scored, h * T + (t + 1))
                ch.link(nc.vector.tensor_reduce(nmax[:, t % 2:t % 2 + 1], p_s[:, t % 2, :], AX.X, ALU.max, negate=True))
                nc.vector.tensor_scalar(bias[:, t % 2:t % 2 + 1], nmax[:, t % 2:t % 2 + 1], SCALE, None, ALU.mult).then_inc(biased, 1)

            def finish(ch, h, t):
                dve.wait_ge(o_done, h * T + (t + 1))
                ch.link(nc.vector.reciprocal(rtotal[:, t % 2:t % 2 + 1], total[:, t % 4:t % 4 + 1]))
                nc.vector.tensor_scalar(k.o[:, t, bass.ds(h * DV, DV)], p_o[:, 0:DV], rtotal[:, t % 2:t % 2 + 1], None,
                                        ALU.mult).then_inc(o_read, 1)

            def head(hh, u, following):
                h = hh * 2 + u
                ch = Chain(dve, own, h * LINKS + 3)
                for t in range(T):
                    dve.wait_ge(p_turned, (h * T + t) * 2 + 1)
                    nc.vector.tensor_copy(prT[:, t % 2, 0:4, :], p_t[:, 0:4, :]).then_inc(pT_dve, 1)
                    if t + 2 < T:
                        top(ch, h, t + 2)
                    elif following:
                        top(ch, h + 1, t + 2 - T)
                    finish(ch, h, t)
                    if following and t == ROTATE:
                        rotate(ch, h + 1)
                assert ch.n == LINKS or not following

            dve.sem_inc(o_read, 1)
            ch = Chain(dve, own)
            rotate(ch, 0)
            top(ch, 0, 0)
            top(ch, 0, 1)
            with dve.Fori(0, HEADS // 2 - 1) as hh:
                for u in range(2):
                    head(hh, u, True)
            head(HEADS // 2 - 1, 0, True)
            head(HEADS // 2 - 1, 1, False)


def s5_scan(nc, k):
    GB = 8
    NG = 2 * GB
    S = T + 1
    with ExitStack() as ctx:
        sb, ps, sem = makers(nc, ctx, "ssm", k.held)
        U = sb("U", [P, G, NC], f32)
        ta = sb("ta", [P, GB, S, CH], f32)
        tb = sb("tb", [P, GB, S, CH], f32)
        vs = sb("vs", [P, NG, T, CH], f32)
        bs = sb("bs", [P, NG, CH], f32)
        ed1 = sb("ed1", [P, NG, S, CH], f32)
        ed2 = sb("ed2", [P, NG, T, CH], f32)
        w_in = sb("w_in", [P, NG, 3 * N], f32)
        fr = sb("fr", [P, 2, GB, NC], f32)
        ysb = sb("ysb", [P, GB, NC], f32)
        cos_t = sb("tc", [P, NG, NC], f32)
        sin_t = sb("ts", [P, NG, NC], f32)
        ka = sb("ka", [CH, GB, 2 * T - 1, CH], f32)
        kt = sb("kt", [P, GB, T * CH], f32)
        flat = [x[:, :, :, :].rearrange("p g s c -> p (g s c)") for x in (ta, tb)]
        ra = flat[0][:, 0:4 * NC].rearrange("p (r n) -> p r n", r=4)
        rb = flat[1][:, 0:4 * NC].rearrange("p (r n) -> p r n", r=4)
        gr = flat[1][:, 4 * NC:8 * NC].rearrange("p (r n) -> p r n", r=4)
        rnd = flat[0][:, 0:GB * NC].rearrange("p (g n) -> p g n", g=GB)
        gc = sb("gc", [P, NG, NC + 1], f32)
        gsn = sb("gsn", [P, NG, NC + 1], f32)
        p_w = ps("p_w", [P, 4, P])
        p_k = ps("p_k", [P, 4, P])
        p_v = ps("p_v", [P, 2, 2, 4, NC])
        p_y = ps("p_y", [P, 2, 4, NC])
        u_in, y_out, kt_in = sem("u_in"), sem("y_out"), sem("kt_in")
        vs_done, vs_turned, win_done = sem("vs_done"), sem("vs_turned"), sem("win_done")
        abs_done = sem("abs_done")
        ph_done, tab_done, ed_done, k_done, k_kept, ka_done = sem("ph_done"), sem("tab_done"), sem("ed_done"), sem("k_done"), sem("k_kept"), sem("ka_done")
        v_done, g_done, y_done, y_kept, own, own_p = sem("v_done"), sem("g_done"), sem("y_done"), sem("y_kept"), sem("own"), sem("own_p")
        block = ctx.enter_context(nc.Block())
        NBATCH = G // GB

        @block.sync
        def _(sp):
            sp.sem_inc(y_out, 1)
            uv = k.u_d.rearrange("(g c) (j n) -> j c g n", c=CH, j=T)
            for j in range(T):
                sp.dma_start(U[j * CH:(j + 1) * CH, :, :], uv[j]).then_inc(u_in, 16)
            yv = k.ys_d.rearrange("(g c) (j n) -> j c g n", c=CH, j=T)
            with sp.Fori(0, NBATCH) as b:
                sp.wait_ge(ka_done, b + 1)
                for j in range(T):
                    sp.dma_start(kt[j * CH:(j + 1) * CH, :, :],
                                 ka[:, :, T - 1 - j:2 * T - 1 - j, :].rearrange("c g l d -> c g (l d)")).then_inc(kt_in, 16)
                sp.wait_ge(y_kept, b * 2 + 2)
                for j in range(T):
                    sp.dma_start(yv[j][:, bass.ds(b * GB, GB), :], ysb[j * CH:(j + 1) * CH, :, :]).then_inc(y_out, 16)
            sp.wait_ge(y_out, 16 * T * NBATCH + 1)

        @block.tensor
        def _(pe):
            def effects(b, x):
                d, half = x // 2, x % 2
                for part in range(2):
                    for r in range(4):
                        gd = d * GB + half * 4 + r
                        last = nc.tensor.matmul(p_v[:, x % 2, part, r, :], w_in[:, gd, part * N:part * N + P],
                                                U[:, bass.ds(b * GB + half * 4 + r, 1), :].rearrange("p a n -> p (a n)"),
                                                start=True, stop=True)
                last.then_inc(v_done, 1)

            with pe.Fori(0, NBATCH) as b:
                for d in range(2):
                    pe.wait_ge(vs_done, b * 2 + d + 1)
                    for half in range(2):
                        x = 2 * d + half
                        if x:
                            pe.wait_ge(win_done, b * 4 + x)
                        for r in range(4):
                            gd = d * GB + half * 4 + r
                            last = nc.tensor.transpose(p_w[:, r, :], vs[:, gd].rearrange("p j c -> p (j c)"), k.ident)
                        last.then_inc(vs_turned, 1)
                pe.wait_ge(win_done, b * 4 + 4)
                pe.wait_ge(u_in, 16 * T)
                effects(b, 0)
                effects(b, 1)
                for x, (d, half) in enumerate(((1, 0), (1, 1), (0, 0), (0, 1))):
                    if half == 0:
                        pe.wait_ge(ed_done, b * 2 + 2 - d)
                    if x >= 2:
                        pe.wait_ge(k_kept, b * 4 + x - 1)
                    for r in range(4):
                        gd = d * GB + half * 4 + r
                        last = nc.tensor.matmul((p_k, p_w)[x % 2][0:CH, r, :], bs[:, gd, :], ed1[:, gd, d:d + T, :].rearrange("p j c -> p (j c)"),
                                                start=True, stop=True)
                    last.then_inc(k_done, 1)
                for x in (2, 3):
                    pe.wait_ge(g_done, b * 4 + x - 1)
                    effects(b, x)
                pe.wait_ge(kt_in, b * 16 * T + 16 * T)
                pe.wait_ge(g_done, b * 4 + 4)
                for half in range(2):
                    for r in range(4):
                        g = half * 4 + r
                        out = p_y[:, half, r, :]
                        nc.tensor.matmul(out, kt[:, g, :], U[:, bass.ds(b * GB + g, 1), :].rearrange("p a n -> p (a n)"), start=True, stop=False)
                        for d in range(2):
                            gd = d * GB + g
                            nc.tensor.matmul(out, ed1[:, gd, 1 - d:1 - d + T, :].rearrange("p j c -> p (j c)"), gc[:, gd, d:d + NC],
                                             start=False, stop=False)
                            last = nc.tensor.matmul(out, ed2[:, gd].rearrange("p j c -> p (j c)"), gsn[:, gd, d:d + NC],
                                                    start=False, stop=(d == 1))
                    last.then_inc(y_done, 1)

        @block.scalar
        def _(act):
            with act.Fori(0, NBATCH) as b:
                for x in range(4):
                    act.wait_ge(vs_turned, b * 4 + x + 1)
                    nc.scalar.activation(w_in[:, 4 * x:4 * x + 4, 0:P], p_w[:, :, :], ACT.Copy)
                    nc.scalar.activation(w_in[:, 4 * x:4 * x + 4, P:3 * N], p_w[:, :, 0:N], ACT.Copy).then_inc(win_done, 1)
                for d in range(2):
                    act.wait_ge(ph_done, b * 2 + d + 1)
                    nc.scalar.activation(fr[:, 1], fr[:, 0], ACT.Abs).then_inc(abs_done, 1)
                    nc.scalar.activation(sin_t[:, d * GB:(d + 1) * GB, :], fr[:, 0], ACT.Sin, scale=k.sgn2pi)
                    act.wait_ge(abs_done, b * 2 + d + 1)
                    nc.scalar.activation(cos_t[:, d * GB:(d + 1) * GB, :], fr[:, 1], ACT.Sin, scale=-6.2831850, bias=k.half_pi).then_inc(tab_done, 1)
                for x in range(2):
                    act.wait_ge(k_done, b * 4 + x + 1)
                    nc.scalar.activation(ka[:, x * 4:x * 4 + 4, 0:T, :], (p_k, p_w)[x][0:CH, :, :].rearrange("c g (l d) -> c g l d", d=CH),
                                         ACT.Copy).then_inc(k_kept, 1)
                act.wait_ge(y_out, b * 16 * T + 1)
                for half in range(2):
                    act.wait_ge(y_done, b * 2 + half + 1)
                    nc.scalar.activation(ysb[:, half * 4:half * 4 + 4, :], p_y[:, half], ACT.Copy).then_inc(y_kept, 1)

        @block.vector
        def _(dve):
            tt = nc.vector.tensor_tensor
            for g in (gc, gsn):
                nc.vector.memset(g[:, 0:GB, 0:1], 0.0)
                last = nc.vector.memset(g[:, GB:NG, NC:NC + 1], 0.0)
            last.then_inc(own_p, 1)
            LINKS = 2 * (1 + 2 + 3) + 4 * (1 + 1 + 1)

            def add_kernels(b, half):
                gs = slice(half * 4, half * 4 + 4)
                src = (p_k, p_w)[half][0:CH, :, :].rearrange("c g (l d) -> c g l d", d=CH)
                dve.wait_ge(k_done, b * 4 + half + 3)
                if half == 0:
                    dve.wait_ge(k_kept, b * 4 + 2)
                nc.vector.tensor_tensor(ka[:, gs, T - 1, :], ka[:, gs, T - 1, :], src[:, :, 0, :], ALU.add)
                nc.vector.tensor_copy(ka[:, gs, T:, :], src[:, :, 1:, :]).then_inc(k_kept, 1)

            def run_states(ch, b, x):
                d, half = x // 2, x % 2
                q = slice(4 * x, 4 * x + 4)
                dve.wait_ge(v_done, b * 4 + x + 1)
                tt(ra[:, :, :], p_v[:, x % 2, 0], cos_t[:, q, :], ALU.mult)
                ch.link(tt(rb[:, :, :], p_v[:, x % 2, 1], sin_t[:, q, :], ALU.mult))
                ch.link(tt(ra[:, :, :], ra[:, :, :], rb[:, :, :], ALU.add))
                for r in range(4):
                    decay = k.m8[:, bass.ds(b * GB + d * G + half * 4 + r, 1)].to_broadcast([P, NC])
                    src, out = ra[:, r, :], gr[:, r, :]
                    if d:
                        src, out = src[:, ::-1], out[:, ::-1]
                    last = nc.vector.tensor_tensor_scan(out, decay, src, 0.0, ALU.mult, ALU.add)
                ch.link(last)
                off = 1 - d
                tt(gc[:, q, off:off + NC], gr[:, :, :], cos_t[:, q, :], ALU.mult)
                tt(gsn[:, q, off:off + NC], gr[:, :, :], sin_t[:, q, :], ALU.mult).then_inc(g_done, 1)
                dve.wait_ge(g_done, b * 4 + x + 1)

            with dve.Fori(0, NBATCH) as b:
                ch = Chain(dve, own, b * LINKS)

                def combine(out, pr, pi, x, y, op, n):
                    w = [P, GB, n, CH]
                    nc.vector.tensor_tensor(ta[:, :, 0:n, :], pr.unsqueeze(3).to_broadcast(w), x.unsqueeze(2).to_broadcast(w), ALU.mult)
                    ch.link(nc.vector.tensor_tensor(tb[:, :, 0:n, :], pi.unsqueeze(3).to_broadcast(w), y.unsqueeze(2).to_broadcast(w), ALU.mult))
                    return nc.vector.tensor_tensor(out, ta[:, :, 0:n, :], tb[:, :, 0:n, :], op)

                def tables(d):
                    dg = bass.ds(b * GB + d * G, GB)
                    w = [P, GB, NC]
                    if d:
                        dve.wait_ge(tab_done, b * 2 + 1)
                    ch.link(tt(fr[:, 0], k.t8[:, dg].unsqueeze(2).to_broadcast(w), (k.chunk, k.chunkr)[d].unsqueeze(1).to_broadcast(w), ALU.mult))
                    ch.link(nc.vector.tensor_scalar(rnd, fr[:, 0], ROUND, -ROUND, ALU.add, ALU.add))
                    tt(fr[:, 0], fr[:, 0], rnd, ALU.subtract).then_inc(own_p, 1)
                    dve.wait_ge(own_p, b * 2 + d + 2)
                    dve.sem_inc(ph_done, 1)

                def edges(d):
                    dg = bass.ds(b * GB + d * G, GB)
                    pw = (k.pw, k.pb)[d][:, :, dg, :]
                    nc.vector.tensor_scalar(bs[:, d * GB:(d + 1) * GB, :], k.b1[:, dg, :], 1.0, None, ALU.mult)
                    combine(ed1[:, d * GB:(d + 1) * GB], pw[:, 0], pw[:, 1], k.e1[:, dg, :], k.c2[:, dg, :], ALU.subtract, S).then_inc(ed_done, 1)
                    dve.wait_ge(ed_done, b * 2 + (2 - d))
                    pw = k.pw[:, :, dg, 1:S] if d == 0 else k.pb[:, :, dg, 0:T]
                    ch.link(combine(ed2[:, d * GB:(d + 1) * GB], pw[:, 0], pw[:, 1], k.f2[:, dg, :], k.c1[:, dg, :], ALU.subtract, T))

                for d in range(2):
                    dg = bass.ds(b * GB + d * G, GB)
                    pw = k.pb[:, :, dg, 1:S] if d == 0 else k.pw[:, :, dg, 0:T]
                    combine(vs[:, d * GB:(d + 1) * GB], pw[:, 0], pw[:, 1], k.b1[:, dg, :], k.b2[:, dg, :], ALU.add, T).then_inc(vs_done, 1)
                    dve.wait_ge(vs_done, b * 2 + d + 1)
                tables(0)
                dve.wait_ge(vs_turned, b * 4 + 1)
                edges(1)
                tables(1)
                edges(0)
                dve.wait_ge(tab_done, b * 2 + 2)
                run_states(ch, b, 0)
                add_kernels(b, 0)
                add_kernels(b, 1)
                dve.wait_ge(k_kept, b * 4 + 4)
                dve.sem_inc(ka_done, 1)
                for x in (1, 2, 3):
                    run_states(ch, b, x)
                assert ch.n == LINKS, ch.n


def s5_gate(nc, k):
    GELU = 2.0 * math.sqrt(2.0 / math.pi)
    with ExitStack() as ctx:
        sb, ps, sem = makers(nc, ctx, "glu", k.held)
        w = sb("w", [P, 4, D_SSM], f32)
        y = sb("y", [P, 4, SEQ], f32)
        u = sb("u", [P, 4, SEQ], f32)
        sg = u
        skip = sb("skip", [P, 4], f32)
        bg = sb("bg", [P, 4], f32)
        p_z = ps("p_z", [P, 4, SEQ])
        w_in, skip_in, bg_in = sem("w_in"), sem("skip_in"), sem("bg_in")
        yu_in = [sem(f"yu_in{m}") for m in range(4)]
        cub, sig, s_done, z_done, z_sig, own = sem("cub"), sem("sig"), sem("s_done"), sem("z_done"), sem("z_sig"), sem("own")
        block = ctx.enter_context(nc.Block())

        @block.sync
        def _(sp):
            for m in range(4):
                rows = slice(m * P, (m + 1) * P)
                sp.dma_start(y[:, m, :], k.ys_d[rows, :]).then_inc(yu_in[m], 16)
                sp.dma_start(u[:, m, :], k.u_d[rows, :]).then_inc(yu_in[m], 16)
            sp.dma_start(w[:, :, :], k.w_glu[0].rearrange("(k p) n -> p k n", p=P)).then_inc(w_in, 16)
            sp.dma_start(k.mix_w[:, :, :], k.w_o[0].rearrange("(k p) n -> p k n", p=P)).then_inc(k.mix_w_in, 16)
            sp.dma_start(k.ws_gu[:, :, 0:F], k.ws_gate[0].rearrange("(p k) n -> p k n", k=KD)).then_inc(k.ws_in, 16)
            sp.dma_start(k.ws_gu[:, :, F:2 * F], k.ws_up[0].rearrange("(p k) n -> p k n", k=KD)).then_inc(k.ws_in, 16)
            sp.dma_start(k.ws_dn[:, :, :], k.ws_down[0].rearrange("(k p) n -> p k n", p=P)).then_inc(k.ws_in, 16)

        @block.scalar
        def _(act):
            for m in range(4):
                rows = slice(m * P, (m + 1) * P)
                act.dma_start(skip[:, m:m + 1], k.d_skip[0, rows].rearrange("(p o) -> p o", o=1)).then_inc(skip_in, 16)
            for m in range(4):
                rows = slice(m * P, (m + 1) * P)
                act.dma_start(bg[:, m:m + 1], k.b_glu[0, rows].rearrange("(p o) -> p o", o=1)).then_inc(bg_in, 16)
            for m in range(4):
                act.wait_ge(cub, m + 1)
                nc.scalar.activation(sg[:, m, :], k.sT[:, m, :], ACT.Sigmoid, scale=GELU).then_inc(sig, 1)
            act.wait_ge(bg_in, 64)
            for m in range(4):
                act.wait_ge(z_done, 2 * m + 2)
                act.wait_ge(s_done, 4)
                nc.scalar.activation(sg[:, m, :], p_z[:, m, :], ACT.Sigmoid, bias=bg[:, m:m + 1]).then_inc(z_sig, 1)

        @block.tensor
        def _(pe):
            pe.wait_ge(w_in, 16)
            for kk in range(4):
                pe.wait_ge(s_done, kk + 1)
                for m in range(4):
                    for half in range(2):
                        last = nc.tensor.matmul(p_z[:, m, half * 512:(half + 1) * 512], w[:, kk, m * P:(m + 1) * P],
                                                k.sT[:, kk, half * 512:(half + 1) * 512], start=(kk == 0), stop=(kk == 3))
                        if kk == 3:
                            last.then_inc(z_done, 1)

        @block.vector
        def _(dve):
            ch = Chain(dve, own)
            dve.wait_ge(skip_in, 64)

            def keep_s(m):
                dve.wait_ge(sig, m + 1)
                nc.vector.tensor_tensor(k.sT[:, m, :], y[:, m, :], sg[:, m, :], ALU.mult).then_inc(s_done, 1)

            for m in range(4):
                a = k.sT[:, m, :]
                dve.wait_ge(yu_in[m], 32)
                ch.link(nc.vector.scalar_tensor_tensor(y[:, m, :], u[:, m, :], skip[:, m:m + 1], y[:, m, :], ALU.mult, ALU.add))
                ch.link(nc.vector.tensor_tensor(a, y[:, m, :], y[:, m, :], ALU.mult))
                ch.link(nc.vector.tensor_scalar(a, a, 0.044715, 1.0, ALU.mult, ALU.add))
                nc.vector.tensor_tensor(a, a, y[:, m, :], ALU.mult).then_inc(cub, 1)
                if m:
                    keep_s(m - 1)
            keep_s(3)
            dve.wait_ge(z_done, 8)
            for m in range(4):
                dve.wait_ge(z_sig, m + 1)
                ch.link(nc.vector.tensor_tensor(k.sT[:, m, :], k.sT[:, m, :], sg[:, m, :], ALU.mult))


def shared_gate_up(nc, k, n, sums):
    half, f = n // KF, n % KF
    for part in range(2):
        for kk in range(KD):
            last = nc.tensor.matmul(sums[:, part * 512:(part + 1) * 512], k.ws_gu[:, kk, part * F + f * P:part * F + (f + 1) * P],
                                    k.x1T[:, kk, half * 512:(half + 1) * 512], start=(kk == 0), stop=(kk == KD - 1))
    return last


def load_expert(eng, k, slot, expert):
    gate_up, down = k.moe_gu[slot], k.moe_dn[slot]
    one = bass.ds(expert, 1)
    eng.dma_start(gate_up[:, :, 0:F], k.we_gate[0].rearrange("e (p k) f -> e p k f", k=KD)[one].rearrange("e p k f -> (e p) k f")).then_inc(k.gu_in[slot], 16)
    eng.dma_start(gate_up[:, :, F:2 * F], k.we_up[0].rearrange("e (p k) f -> e p k f", k=KD)[one].rearrange("e p k f -> (e p) k f")).then_inc(k.gu_in[slot], 16)
    eng.dma_start(down[:, :, :], k.we_down[0].rearrange("e (p k) n -> e p k n", k=KF)[one].rearrange("e p k n -> (e p) k n")).then_inc(k.dn_in[slot], 16)


def mix_norm_route(nc, k):
    with ExitStack() as ctx:
        sb, ps, sem = makers(nc, ctx, "mix", k.held)
        w_o = k.mix_w
        w_r = sb("w_r", [P, KD, N_EXPERTS], f32)
        r_bias = sb("r_bias", [P, N_EXPERTS], f32)
        zeros = sb("zeros", [P, D], f32)
        g1 = sb("g1", [P, D], f32)
        b1 = sb("b1", [P, D], f32)
        oT = sb("oT", [P, 2, 4, P], f32)
        r = sb("r", [P, D], f32)
        stats = sb("stats", [P, 2, 6], f32)
        mv = sb("mv", [P, 2, 2], f32)
        std = sb("std", [P, 2], f32)
        rstd = sb("rstd", [P, 1], f32)
        score = sb("score", [P, 2, N_EXPERTS], f32)
        choice = sb("choice", [P, N_EXPERTS], f32)
        top2 = sb("top2", [P, EGROUPS, 8], f32)
        gscore = sb("gscore", [P, EGROUPS], f32)
        gtop = sb("gtop", [P, 8], f32)
        gidx = sb("gidx", [P, 8], u32)
        gidxf = sb("gidxf", [P, 8], f32)
        geq = sb("geq", [P, EGROUPS, TOP_GROUPS], f32)
        gmask = sb("gmask", [P, EGROUPS], f32)
        gneg = sb("gneg", [P, EGROUPS], f32)
        top8 = sb("top8", [P, 8], f32)
        idx8 = sb("idx8", [P, 8], u32)
        hot = sb("hot", [P, TOP_K, N_EXPERTS], f32)
        hots = sb("hots", [P, TOP_K, N_EXPERTS], f32)
        wsum = sb("wsum", [P, 1], f32)
        wrec = sb("wrec", [P, 1], f32)
        member = sb("member", [P, 2, N_EXPERTS], f32)
        seen = sb("seen", [P, 2, N_EXPERTS], f32)
        sig = sb("s_sig", [P, KF, 512], f32)
        p_m = ps("p_m", [P, 2, D])
        p_x = ps("p_x", [P, KD, P])
        p_o = ps("p_o", [P, 512])
        p_log = ps("p_log", [P, 512])
        p_rank, p_log = p_o[:, 0:N_EXPERTS], p_log[:, 0:N_EXPERTS]

        wr_in, ln_in = sem("wr_in"), sem("ln_in")
        zeroed, y_zeroed = sem("zeroed"), sem("y_zeroed")
        x1_out = [sem(f"x1_out{t}") for t in range(T)]
        o_turned, oT_done, mixed, mix_read = sem("o_turned"), sem("oT_done"), sem("mixed"), sem("mix_read")
        var_done, std_done, x1_done = sem("var_done"), sem("std_done"), sem("x1_done")
        x_turned, xT_dve, xT_act, logits = sem("x_turned"), sem("xT_dve"), sem("xT_act"), sem("logits")
        score_done, member_done, ranked, rank_read, own = sem("score_done"), sem("member_done"), sem("ranked"), sem("rank_read"), sem("own")
        gu_done, sig_done = sem("gu_done"), sem("sig_done")
        block = ctx.enter_context(nc.Block())

        @block.sync
        def _(sp):
            sp.dma_start(g1[:, :], k.ln1_g.to_broadcast([P, D])).then_inc(ln_in, 16)
            sp.dma_start(b1[:, :], k.ln1_b.to_broadcast([P, D])).then_inc(ln_in, 16)
            sp.dma_start(w_r[:, :, :], k.w_router[0].rearrange("(p k) n -> p k n", k=KD)).then_inc(wr_in, 16)
            sp.dma_start(r_bias[:, :], k.router_bias.to_broadcast([P, N_EXPERTS])).then_inc(wr_in, 16)
            sp.wait_ge(zeroed, 1)
            sp.dma_start(k.y_d[N_EXPERTS * P:SLOTS, :].rearrange("(b p) d -> p b d", p=P),
                         zeros[:, :].unsqueeze(1).to_broadcast([P, OVER, D])).then_inc(y_zeroed, 16)
            for t in range(T):
                sp.wait_ge(x1_done, t + 1)
                sp.dma_start(k.x1_d[t * P:(t + 1) * P, :], k.x[:, t, :]).then_inc(x1_out[t], 16)
            for t in range(T):
                sp.wait_ge(x1_out[t], 16)
            sp.wait_ge(y_zeroed, 16)

        @block.tensor
        def _(pe):
            def turn_o(t):
                if t >= 5:
                    pe.wait_ge(rank_read, t - 4)
                elif t:
                    pe.wait_ge(oT_done, t)
                for q in range(4):
                    last = nc.tensor.transpose(p_o[:, q * P:(q + 1) * P], k.o[:, t, q * P:(q + 1) * P], k.ident)
                last.then_inc(o_turned, 1)

            def mix(t):
                if t == 0:
                    pe.wait_ge(k.mix_w_in, 16)
                if t >= 2:
                    pe.wait_ge(mix_read, 2 * t - 2)
                for half in range(2):
                    cols = slice(half * 512, (half + 1) * 512)
                    for kk in range(4):
                        nc.tensor.matmul(p_m[:, t % 2, cols], k.sT[:, kk, t * P:(t + 1) * P], w_o[:, kk, cols],
                                         start=(kk == 0), stop=False)
                    if half == 0:
                        pe.wait_ge(oT_done, t + 1)
                    for kk in range(4):
                        last = nc.tensor.matmul(p_m[:, t % 2, cols], oT[:, t % 2, kk, :], w_o[:, 4 + kk, cols],
                                                start=False, stop=(kk == 3))
                    last.then_inc(mixed, 1)

            def turn_x(t):
                pe.wait_ge(x1_done, t + 1)
                for half in range(2):
                    for q in range(4):
                        kk = half * 4 + q
                        last = nc.tensor.transpose(p_x[:, kk, :], k.x[:, t, kk::KD], k.ident)
                    last.then_inc(x_turned, 1)

            def route(t):
                pe.wait_ge(xT_dve, t + 1)
                pe.wait_ge(xT_act, t + 1)
                if t == 0:
                    pe.wait_ge(wr_in, 32)
                else:
                    pe.wait_ge(score_done, t)
                for kk in range(KD):
                    last = nc.tensor.matmul(p_log, k.x1T[:, kk, t * P:(t + 1) * P], w_r[:, kk, :], start=(kk == 0), stop=(kk == KD - 1))
                last.then_inc(logits, 1)

            def rank(t):
                pe.wait_ge(member_done, t + 1)
                pe.wait_ge(oT_done, min(t + 5, T))
                last = nc.tensor.matmul(p_rank, k.tri, member[:, t % 2, :], start=True, stop=(t == 0))
                if t:
                    last = nc.tensor.matmul(p_rank, k.ones, seen[:, t % 2, :], start=False, stop=True)
                last.then_inc(ranked, 1)

            turn_o(0)
            turn_o(1)
            mix(0)
            turn_o(2)
            mix(1)
            for t in range(T):
                turn_x(t)
                if t + 3 < T:
                    turn_o(t + 3)
                if t + 2 < T:
                    mix(t + 2)
                if t:
                    rank(t - 1)
                route(t)
                if t + 2 >= T:
                    n = t + 2 - T
                    pe.wait_ge(mix_read, 2 * t + 2)
                    if n == 0:
                        pe.wait_ge(k.ws_in, 48)
                    shared_gate_up(nc, k, n, p_m[:, n, :]).then_inc(gu_done, 1)
            pe.wait_ge(rank_read, T - 1)
            rank(T - 1)
            pe.wait_ge(rank_read, T)
            pe.wait_ge(member_done, T + 1)
            nc.tensor.matmul(p_rank, k.ones, seen[:, T % 2, :], start=True, stop=True).then_inc(ranked, 1)

        @block.scalar
        def _(act):
            def keep_oT(t):
                act.wait_ge(o_turned, t + 1)
                nc.scalar.activation(oT[:, t % 2, :, :].rearrange("p k t -> p (k t)"), p_o[:, :], ACT.Copy).then_inc(oT_done, 1)

            def deviation(t):
                act.wait_ge(var_done, t + 1)
                nc.scalar.activation(std[:, t % 2:t % 2 + 1], mv[:, t % 2, 1:2], ACT.Sqrt).then_inc(std_done, 1)

            keep_oT(0)
            keep_oT(1)
            keep_oT(2)
            deviation(0)
            for t in range(T):
                act.wait_ge(x_turned, 2 * t + 2)
                nc.scalar.activation(k.x1T[:, 4:8, t * P:(t + 1) * P], p_x[:, 4:8, :], ACT.Copy).then_inc(xT_act, 1)
                if t + 3 < T:
                    keep_oT(t + 3)
                if t + 1 < T:
                    deviation(t + 1)
                act.wait_ge(logits, t + 1)
                nc.scalar.activation(score[:, t % 2, :], p_log, ACT.Sigmoid).then_inc(score_done, 1)
            for n in range(KF):
                act.wait_ge(gu_done, n + 1)
                nc.scalar.activation(sig[:, n, :], p_m[:, n, 0:512], ACT.Sigmoid).then_inc(sig_done, 1)

        @block.vector
        def _(dve):
            ch = Chain(dve, own)

            def norm(t):
                xt = k.x[:, t, :]
                for half in range(2):
                    cols = slice(half * 512, (half + 1) * 512)
                    dve.wait_ge(mixed, 2 * t + half + 1)
                    nc.vector.scalar_tensor_tensor(r[:, cols], k.x[:, t, cols], ALPHA, p_m[:, t % 2, cols], ALU.mult, ALU.add).then_inc(mix_read, 1)
                dve.wait_ge(mix_read, 2 * t + 2)
                nc.vector.bn_stats(stats[:, 0, :], r[:, 0:512])
                ch.link(nc.vector.bn_stats(stats[:, 1, :], r[:, 512:D]))
                ch.link(nc.vector.bn_aggr(mv[:, t % 2, :], stats[:, :, :].rearrange("p a b -> p (a b)")))
                ch.link(nc.vector.tensor_scalar(mv[:, t % 2, 1:2], mv[:, t % 2, 1:2], LN_EPS, None, ALU.add))
                nc.vector.tensor_copy(rstd[:, :], mv[:, t % 2, 1:2]).then_inc(var_done, 1)
                dve.wait_ge(std_done, t + 1)
                ch.link(nc.vector.reciprocal(rstd[:, :], std[:, t % 2:t % 2 + 1]))
                ch.link(nc.vector.tensor_scalar(r[:, :], r[:, :], mv[:, t % 2, 0:1], rstd[:, 0:1], ALU.subtract, ALU.mult))
                if t == 0:
                    dve.wait_ge(ln_in, 32)
                ch.link(nc.vector.tensor_tensor(r[:, :], r[:, :], g1[:, :], ALU.mult))
                nc.vector.tensor_tensor(xt, r[:, :], b1[:, :], ALU.add).then_inc(x1_done, 1)

            def route(t):
                sc = score[:, t % 2, :]
                dve.wait_ge(score_done, t + 1)
                ch.link(nc.vector.tensor_tensor(choice[:, :], sc, r_bias[:, :], ALU.add))
                for g in range(EGROUPS):
                    last = nc.vector.max(top2[:, g, :], choice[:, g * 8:(g + 1) * 8])
                ch.link(last)
                ch.link(nc.vector.tensor_tensor(gscore[:, :], top2[:, :, 0], top2[:, :, 1], ALU.add))
                ch.link(nc.vector.max(gtop[:, :], gscore[:, :]))
                ch.link(nc.vector.max_index(gidx[:, :], gtop[:, :], gscore[:, :]))
                ch.link(nc.vector.tensor_copy(gidxf[:, :], gidx[:, :]))
                ch.link(nc.vector.tensor_tensor(geq[:, :, :], k.iota_e[:, 0:EGROUPS].unsqueeze(2).to_broadcast([P, EGROUPS, TOP_GROUPS]),
                                                gidxf[:, 0:TOP_GROUPS].unsqueeze(1).to_broadcast([P, EGROUPS, TOP_GROUPS]), ALU.is_equal))
                ch.link(nc.vector.tensor_reduce(gmask[:, :], geq[:, :, :], AX.X, ALU.add))
                ch.link(nc.vector.tensor_scalar(gneg[:, :], gmask[:, :], BIG, -BIG, ALU.mult, ALU.add))
                v3 = choice[:, :].rearrange("p (g e) -> p g e", g=EGROUPS)
                ch.link(nc.vector.tensor_tensor(v3, v3, gmask[:, :].unsqueeze(2).to_broadcast([P, EGROUPS, 8]), ALU.mult))
                ch.link(nc.vector.tensor_tensor(v3, v3, gneg[:, :].unsqueeze(2).to_broadcast([P, EGROUPS, 8]), ALU.add))
                ch.link(nc.vector.max(top8[:, :], choice[:, :]))
                ch.link(nc.vector.max_index(idx8[:, :], top8[:, :], choice[:, :]))
                ch.link(nc.vector.tensor_copy(k.picked[:, t, :], idx8[:, 0:TOP_K]))
                ch.link(nc.vector.tensor_tensor(hot[:, :, :], k.iota_e.unsqueeze(1).to_broadcast([P, TOP_K, N_EXPERTS]),
                                                k.picked[:, t, :].unsqueeze(2).to_broadcast([P, TOP_K, N_EXPERTS]), ALU.is_equal))
                nc.vector.tensor_reduce(member[:, t % 2, :], hot[:, :, :].rearrange("p k e -> p e k"), AX.X, ALU.add).then_inc(member_done, 1)
                ch.link(nc.vector.tensor_tensor(hots[:, :, :], hot[:, :, :], sc.unsqueeze(1).to_broadcast([P, TOP_K, N_EXPERTS]), ALU.mult))
                ch.link(nc.vector.tensor_reduce(k.top_w[:, t, :], hots[:, :, :], AX.X, ALU.add))
                ch.link(nc.vector.tensor_reduce(wsum[:, :], k.top_w[:, t, :], AX.X, ALU.add))
                ch.link(nc.vector.tensor_scalar(wsum[:, :], wsum[:, :], 1e-20, None, ALU.add))
                ch.link(nc.vector.reciprocal(wrec[:, :], wsum[:, :]))
                ch.link(nc.vector.tensor_scalar(k.top_w[:, t, :], k.top_w[:, t, :], wrec[:, 0:1], ROUTED_SCALE, ALU.mult, ALU.mult))

            def keep_rank(t):
                dve.wait_ge(ranked, t + 1)
                nc.vector.tensor_copy(k.rank[:, t, :], p_rank).then_inc(rank_read, 1)

            nc.vector.memset(zeros[:, :], 0.0).then_inc(zeroed, 1)
            norm(0)
            for t in range(T):
                dve.wait_ge(x_turned, 2 * t + 1)
                nc.vector.tensor_copy(k.x1T[:, 0:4, t * P:(t + 1) * P], p_x[:, 0:4, :]).then_inc(xT_dve, 1)
                if t + 1 < T:
                    norm(t + 1)
                if t:
                    keep_rank(t - 1)
                route(t)
                if t == 0:
                    ch.link(nc.vector.tensor_copy(seen[:, 1, :], member[:, 0, :]))
                else:
                    ch.link(nc.vector.tensor_tensor(seen[:, (t + 1) % 2, :], seen[:, t % 2, :], member[:, t % 2, :], ALU.add))
            def hidden(n):
                out = k.s_hT[:, n, 0:512]
                dve.wait_ge(sig_done, n + 1)
                ch.link(nc.vector.tensor_tensor(out, sig[:, n, :], p_m[:, n, 0:512], ALU.mult))
                ch.link(nc.vector.tensor_tensor(out, out, p_m[:, n, 512:D], ALU.mult))

            dve.sem_inc(member_done, 1)
            hidden(0)
            keep_rank(T - 1)
            dve.wait_ge(ranked, T + 1)
            ch.link(nc.vector.tensor_copy(k.counts[:, :], p_rank))
            hidden(1)


def dispatch(nc, k):
    E = N_EXPERTS
    with ExitStack() as ctx:
        sb, ps, sem = makers(nc, ctx, "disp", k.held)
        over = sb("over", [P, E], f32)
        over_end = sb("over_end", [P, E], f32)
        base = sb("base", [P, E], f32)
        far = sb("far", [P, T, E], f32)
        slot = sb("slot", [P, T, E], f32)
        hot = sb("d_hot", [P, TOP_K, E], f32)
        dest = sb("dest", [P, T, TOP_K], f32)
        le = sb("le", [P, E], f32)
        expert_f = sb("expert_f", [P, 2], f32)
        expert_i = sb("expert_i", [P, 2], i32)
        zero = sb("zero", [E + OVER, P], f32)
        toks = sb("toks", [E + OVER, P], f32)
        p_t = ps("p_t", [P, P])
        own, dest_done, zeroed, zeroed_d = sem("d_own"), sem("dest_done"), sem("zeroed"), sem("zeroed_d")
        scattered, toks_in, toks_turned = sem("scattered"), sem("toks_in"), sem("toks_turned")
        expert_done, expert_d, expert_in = sem("expert_done"), sem("expert_d"), sem("expert_in")
        sig = sb("s_sig", [P, 2, 512], f32)
        hT = k.s_hT
        p_gu = ps("p_gu", [P, 2, 2 * 512])
        p_y = ps("p_y", [P, 2, 512])
        gu_done, sig_done, gs_done, h_done, y_done, y_read = sem("gu_done"), sem("sig_done"), sem("gs_done"), sem("h_done"), sem("y_done"), sem("y_read")
        block = ctx.enter_context(nc.Block())

        @block.scalar
        def _(act):
            for e in range(EARLY):
                load_expert(act, k, e, e)
            for f in range(KF):
                act.wait_ge(gu_done, f + 1)
                nc.scalar.activation(sig[:, f, :], p_gu[:, f, 0:512], ACT.Sigmoid).then_inc(sig_done, 1)

        @block.vector
        def _(dve):
            ch = Chain(dve, own)
            nc.vector.memset(zero[:, :], 0.0).then_inc(zeroed, 1)
            ch.link(nc.vector.tensor_scalar(over[:, :], k.counts[:, :], float(P), None, ALU.is_gt))
            for m in range(2, SEQ // P):
                ch.link(nc.vector.scalar_tensor_tensor(over[:, :], k.counts[:, :], float(P * m), over[:, :], ALU.is_gt, ALU.add))
            ch.link(nc.vector.tensor_tensor_scan(over_end[:, :], k.ones[:, 0:E], over[:, :], 0.0, ALU.mult, ALU.add))
            ch.link(nc.vector.tensor_scalar(le[:, :], over_end[:, :], k.part, None, ALU.is_le))
            ch.link(nc.vector.tensor_reduce(expert_f[:, 0:1], le[:, :], AX.X, ALU.add))
            ch.link(nc.vector.tensor_scalar(expert_f[:, 0:1], expert_f[:, 0:1], float(E - 1), None, ALU.min))
            ch.link(nc.vector.tensor_copy(expert_f[:, 1:2], over_end[:, E - 1:E]))
            ch.link(nc.vector.tensor_copy(k.n_over[0:1, 0:1], expert_f[0:1, 1:2]))
            nc.vector.tensor_copy(expert_i[:, :], expert_f[:, :]).then_inc(expert_done, 1)
            ch.link(nc.vector.tensor_tensor(base[:, :], over_end[:, :], over[:, :], ALU.subtract))
            ch.link(nc.vector.tensor_scalar(base[:, :], base[:, :], float(P), float(P * E - P), ALU.mult, ALU.add))
            ch.link(nc.vector.tensor_tensor(base[:, :], base[:, :], k.iota_e128, ALU.subtract))
            wide = [P, T, E]
            ch.link(nc.vector.tensor_scalar(far[:, :, :], k.rank[:, :, :], float(P), None, ALU.is_ge))
            ch.link(nc.vector.tensor_tensor(far[:, :, :], far[:, :, :], base[:, :].unsqueeze(1).to_broadcast(wide), ALU.mult))
            ch.link(nc.vector.tensor_tensor(slot[:, :, :], k.rank[:, :, :], k.iota_e128.unsqueeze(1).to_broadcast(wide), ALU.add))
            ch.link(nc.vector.tensor_tensor(slot[:, :, :], slot[:, :, :], far[:, :, :], ALU.add))
            many = [P, TOP_K, E]
            for t in range(T):
                ch.link(nc.vector.tensor_tensor(hot[:, :, :], k.iota_e.unsqueeze(1).to_broadcast(many),
                                                k.picked[:, t, :].unsqueeze(2).to_broadcast(many), ALU.is_equal))
                ch.link(nc.vector.tensor_tensor(hot[:, :, :], hot[:, :, :], slot[:, t, :].unsqueeze(1).to_broadcast(many), ALU.mult))
                ch.link(nc.vector.tensor_reduce(dest[:, t, :], hot[:, :, :], AX.X, ALU.add))
                nc.vector.tensor_copy(k.dest[:, t * TOP_K:(t + 1) * TOP_K], dest[:, t, :]).then_inc(dest_done, 1)
            for f in range(KF):
                out = hT[:, f, 512:SEQ]
                dve.wait_ge(sig_done, f + 1)
                nc.vector.tensor_tensor(out, sig[:, f, :], p_gu[:, f, 0:512], ALU.mult).then_inc(gs_done, 1)
                dve.wait_ge(gs_done, f + 1)
                nc.vector.tensor_tensor(out, out, p_gu[:, f, 512:2 * 512], ALU.mult).then_inc(h_done, 1)
            for n in range(2 * T):
                t, cols = n // 2, slice(n % 2 * 512, (n % 2 + 1) * 512)
                dve.wait_ge(y_done, n + 1)
                nc.vector.scalar_tensor_tensor(k.x[:, t, cols], k.x[:, t, cols], ALPHA, p_y[:, n % 2, :], ALU.mult, ALU.add).then_inc(y_read, 1)
            dve.wait_ge(toks_turned, 1)
            nc.vector.tensor_copy(k.block_tok[:, :], p_t[:, 0:E + OVER])

        @block.gpsimd
        def _(pool):
            pool.wait_ge(zeroed_d, 16)
            for t in range(T):
                pool.wait_ge(dest_done, t + 1)
                for q in range(TOP_K):
                    nc.gpsimd.indirect_dma_start(k.slot_tok_d[:, :],
                                                 bass.IndirectOffsetOnAxis(ap=k.dest[:, t * TOP_K + q:t * TOP_K + q + 1], axis=0),
                                                 k.tok[:, t:t + 1], None).then_inc(scattered, 16)

        @block.sync
        def _(sp):
            sp.wait_ge(zeroed, 1)
            sp.dma_start(k.slot_tok_d.rearrange("(b s) o -> b (s o)", s=P), zero[:, :]).then_inc(zeroed_d, 16)
            sp.wait_ge(expert_done, 1)
            sp.dma_start(k.expert_d.rearrange("(p o) -> p o", o=1), expert_i[:, 0:1]).then_inc(expert_d, 16)
            sp.wait_ge(expert_d, 16)
            sp.dma_start(k.over_expert[0:1, :], k.expert_d[0:OVER].rearrange("(o p) -> o p", o=1)).then_inc(expert_in, 16)
            sp.wait_ge(scattered, 16 * T * TOP_K)
            sp.dma_start(toks[:, :], k.slot_tok_d.rearrange("(b s) o -> b (s o)", s=P)).then_inc(toks_in, 16)
            sp.wait_ge(expert_in, 16)

        @block.tensor
        def _(pe):
            for u in range(KF):
                shared_gate_up(nc, k, KF + u, p_gu[:, u, :]).then_inc(gu_done, 1)
            for n in range(2 * T):
                t, cols = n // 2, slice(n % 2 * 512, (n % 2 + 1) * 512)
                if n == T:
                    pe.wait_ge(h_done, KF)
                if n >= 2:
                    pe.wait_ge(y_read, n - 1)
                for f in range(KF):
                    last = nc.tensor.matmul(p_y[:, n % 2, :], hT[:, f, t * P:(t + 1) * P], k.ws_dn[:, f, cols],
                                            start=(f == 0), stop=(f == KF - 1))
                last.then_inc(y_done, 1)
            pe.wait_ge(toks_in, 16)
            nc.tensor.transpose(p_t[:, 0:E + OVER], toks[:, :], k.ident[0:E + OVER, 0:E + OVER]).then_inc(toks_turned, 1)



def moe_experts(nc, k):
    E = N_EXPERTS
    with ExitStack() as ctx:
        sb, ps, sem = makers(nc, ctx, "moe", k.held)
        for e in range(EARLY, RING):
            k.moe_gu.append(sb(f"gu{e}", [P, KD, 2 * F], f32))
            k.moe_dn.append(sb(f"dn{e}", [P, KF, D], f32))
        xg = sb("xg", [P, 2, D], f32)
        xgT = sb("xgT", [P, 2, KD, P], f32)
        sig = sb("sig", [P, 2, F], f32)
        gs = sb("gs", [P, 2, F], f32)
        h = sb("h", [P, 2, F], f32)
        hT = sb("hT", [P, 2, KF, P], f32)
        y = sb("y", [P, 2, D], f32)
        idx = sb("idx", [P, 2], i32)
        p_x = ps("p_x", [P, KD, P])
        p_gu = ps("p_gu", [P, 2, 2 * F])
        p_h = ps("p_h", [P, 512])
        p_y = ps("p_y", [P, D])

        xg_in = [sem(f"xg_in{u}") for u in range(2)]
        y_out = [sem(f"y_out{u}") for u in range(2)]
        x_turned = sem("x_turned")
        gu_done = sem("gu_done")
        h_turned = sem("h_turned")
        y_done = sem("y_done")
        xT_dve = sem("xT_dve")
        xT_act = sem("xT_act")
        sig_done = sem("sig_done")
        gs_done = sem("gs_done")
        h_done = sem("h_done")
        hT_done = sem("hT_done")
        y_dve = sem("y_dve")
        y_act = sem("y_act")
        idx_done = sem("idx_done")
        idx_seen = sem("idx_seen")
        all_out = sem("all_out")
        block = ctx.enter_context(nc.Block())

        @block.sync
        def _(sp):
            for e in range(EARLY, RING):
                load_expert(sp, k, e, e)
            with sp.Fori(1, E // RING) as ee:
                for v in range(RING):
                    e = ee * RING + v
                    sp.wait_ge(gu_done, e - (RING - 1))
                    sp.wait_ge(y_done, e * 2 - (2 * RING - 2))
                    load_expert(sp, k, v, e)
            n_over = sp.value_load(k.n_over[0:1, 0:1], min_val=0, max_val=OVER)
            with sp.Fori(0, OVER // SPAN) as span, sp.If(n_over > span * SPAN), sp.Fori(0, SPAN // RING) as round_:
                jj = span * (SPAN // RING) + round_
                for v in range(RING):
                    j = jj * RING + v
                    with sp.If(n_over > j):
                        expert = sp.value_load(k.over_expert[0:1, bass.ds(j, 1)], min_val=0, max_val=E - 1)
                        sp.wait_ge(gu_done, j + (E - (RING - 1)))
                        sp.wait_ge(y_done, j * 2 + (2 * E - (2 * RING - 2)))
                        load_expert(sp, k, v, expert)

        @block.gpsimd
        def _(pool):
            def gather(e, u):
                nc.gpsimd.tensor_copy(idx[:, u:u + 1], k.block_tok[:, bass.ds(e, 1)]).then_inc(idx_done, 1)
                pool.wait_ge(idx_done, e + 1)
                pool.sem_inc(idx_seen, 1)
                nc.gpsimd.indirect_dma_start(xg[:, u, :], None, k.x1_d[:, :],
                                             bass.IndirectOffsetOnAxis(ap=idx[:, u:u + 1], axis=0)).then_inc(xg_in[u], 16)

            for e in range(2):
                gather(e, e)
            with pool.Fori(1, E // 2) as ee:
                for u in range(2):
                    e = ee * 2 + u
                    pool.wait_ge(x_turned, e * 2 - 2)
                    gather(e, u)
            n_over = pool.value_load(k.n_over[0:1, 0:1], min_val=0, max_val=OVER)
            with pool.Fori(0, OVER // SPAN) as span, pool.If(n_over > span * SPAN), pool.Fori(0, SPAN // 2) as pair:
                jj = span * (SPAN // 2) + pair
                for u in range(2):
                    j = jj * 2 + u
                    with pool.If(n_over > j):
                        pool.wait_ge(x_turned, j * 2 + (2 * E - 2))
                        gather(j + E, u)

        @block.tensor
        def _(pe):
            def turn_x(n, c):
                u = c % 2
                pe.wait_ge(xg_in[u], n * (16 * RING // 2) + (c // 2 + 1) * 16)
                for half in range(2):
                    for q in range(4):
                        kk = half * 4 + q
                        last = nc.tensor.transpose(p_x[:, kk, :], xg[:, u, kk::KD], k.ident)
                    last.then_inc(x_turned, 1)

            def gate_up(n, c):
                e, u, v = n * RING + c, c % 2, c % RING
                pe.wait_ge(xT_dve, e + 1)
                pe.wait_ge(xT_act, e + 1)
                pe.wait_ge(k.gu_in[v], n * 32 + (c // RING + 1) * 32)
                for kk in range(KD):
                    last = nc.tensor.matmul(p_gu[:, u, :], xgT[:, u, kk, :], k.moe_gu[v][:, kk, :],
                                            start=(kk == 0), stop=(kk == KD - 1))
                last.then_inc(gu_done, 1)

            def turn_h(n, c):
                e, u = n * RING + c, c % 2
                pe.wait_ge(h_done, e + 1)
                for kk in range(KF):
                    last = nc.tensor.transpose(p_h[:, kk * P:(kk + 1) * P], h[:, u, kk::KF], k.ident)
                last.then_inc(h_turned, 1)

            def down(n, c, first=False):
                e, u, v = n * RING + c, c % 2, c % RING
                pe.wait_ge(hT_done, e + 1)
                pe.wait_ge(k.dn_in[v], n * 16 + (c // RING + 1) * 16)
                if not first:
                    pe.wait_ge(y_dve, e)
                    pe.wait_ge(y_act, e)
                for half in range(2):
                    for kk in range(KF):
                        last = nc.tensor.matmul(p_y[:, half * 512:(half + 1) * 512], hT[:, u, kk, :],
                                                k.moe_dn[v][:, kk, half * 512:(half + 1) * 512],
                                                start=(kk == 0), stop=(kk == KF - 1))
                    last.then_inc(y_done, 1)

            def step(n, c, first=False):
                gate_up(n, c + 1)
                turn_x(n, c + 2)
                down(n, c, first)
                turn_h(n, c + 1)

            turn_x(0, 0)
            gate_up(0, 0)
            turn_x(0, 1)
            turn_h(0, 0)
            step(0, 0, first=True)
            step(0, 1)
            with pe.Fori(0, E // RING - 1) as n:
                for v in range(RING):
                    step(n, v + 2)
            last = E // RING - 1
            gate_up(last, RING - 1)
            down(last, RING - 2)
            turn_h(last, RING - 1)
            down(last, RING - 1)
            n_over = pe.value_load(k.n_over[0:1, 0:1], min_val=0, max_val=OVER)
            with pe.Fori(0, OVER // SPAN) as span, pe.If(n_over > span * SPAN), pe.Fori(0, SPAN // RING) as round_:
                jj = span * (SPAN // RING) + round_
                for v in range(RING):
                    with pe.If(n_over > jj * RING + v):
                        turn_x(jj, v + E)
                        gate_up(jj, v + E)
                        turn_h(jj, v + E)
                        down(jj, v + E)

        @block.scalar
        def _(act):
            def keep_xT(e, u):
                act.wait_ge(x_turned, e * 2 + 2)
                nc.scalar.activation(xgT[:, u, 4:8, :], p_x[:, 4:8, :], ACT.Copy).then_inc(xT_act, 1)

            def gate(e, u):
                act.wait_ge(gu_done, e + 1)
                nc.scalar.activation(sig[:, u, :], p_gu[:, u, 0:F], ACT.Sigmoid).then_inc(sig_done, 1)

            def keep_y(e, u, n):
                act.wait_ge(y_done, e * 2 + 1)
                if n is not None:
                    act.wait_ge(y_out[u], n)
                nc.scalar.activation(y[:, u, 0:512], p_y[:, 0:512], ACT.Copy).then_inc(y_act, 1)
                act.wait_ge(y_act, e + 1)
                act.wait_ge(y_dve, e + 1)
                act.dma_start(k.y_d[bass.ds(e * P, P), :], y[:, u, :]).then_inc(y_out[u], 16)

            keep_xT(0, 0)
            gate(0, 0)
            keep_xT(1, 1)
            gate(1, 1)
            keep_xT(2, 0)
            keep_y(0, 0, None)
            gate(2, 0)
            keep_xT(3, 1)
            keep_y(1, 1, None)
            with act.Fori(1, E // 2 - 1) as ii:
                for u in range(2):
                    i = ii * 2 + u
                    gate(i + 1, 1 - u)
                    keep_xT(i + 2, u)
                    keep_y(i, u, ii * 16)
            gate(E - 1, 1)
            keep_y(E - 2, 0, 16 * (E // 2 - 1))
            keep_y(E - 1, 1, 16 * (E // 2 - 1))
            n_over = act.value_load(k.n_over[0:1, 0:1], min_val=0, max_val=OVER)
            with act.Fori(0, OVER // SPAN) as span, act.If(n_over > span * SPAN), act.Fori(0, SPAN // 2) as pair:
                jj = span * (SPAN // 2) + pair
                for u in range(2):
                    j = jj * 2 + u
                    with act.If(n_over > j):
                        keep_xT(j + E, u)
                        gate(j + E, u)
                        keep_y(j + E, u, jj * 16 + 16 * (E // 2))
            for u in range(2):
                act.wait_ge(y_out[u], (n_over + (1 - u)) // 2 * 16 + 16 * (E // 2))
                act.sem_inc(all_out, 1)

        @block.vector
        def _(dve):
            def keep_xT(e, u):
                dve.wait_ge(x_turned, e * 2 + 1)
                nc.vector.tensor_copy(xgT[:, u, 0:4, :], p_x[:, 0:4, :]).then_inc(xT_dve, 1)

            def hidden(e, u):
                dve.wait_ge(sig_done, e + 1)
                nc.vector.tensor_tensor(gs[:, u, :], sig[:, u, :], p_gu[:, u, 0:F], ALU.mult).then_inc(gs_done, 1)
                dve.wait_ge(gs_done, e + 1)
                nc.vector.tensor_tensor(h[:, u, :], gs[:, u, :], p_gu[:, u, F:2 * F], ALU.mult).then_inc(h_done, 1)

            def keep_hT(e, u):
                dve.wait_ge(h_turned, e + 1)
                nc.vector.tensor_copy(hT[:, u, :, :].rearrange("p k t -> p (k t)"), p_h[:, 0:KF * P]).then_inc(hT_done, 1)

            def keep_y(e, u, n):
                dve.wait_ge(y_done, e * 2 + 2)
                if n is not None:
                    dve.wait_ge(y_out[u], n)
                nc.vector.tensor_copy(y[:, u, 512:D], p_y[:, 512:D]).then_inc(y_dve, 1)

            keep_xT(0, 0)
            hidden(0, 0)
            keep_xT(1, 1)
            keep_hT(0, 0)
            keep_xT(2, 0)
            hidden(1, 1)
            keep_y(0, 0, None)
            keep_hT(1, 1)
            keep_xT(3, 1)
            hidden(2, 0)
            keep_y(1, 1, None)
            keep_hT(2, 0)
            with dve.Fori(1, E // 2 - 1) as ii:
                for u in range(2):
                    i = ii * 2 + u
                    keep_xT(i + 2, u)
                    hidden(i + 1, 1 - u)
                    keep_y(i, u, ii * 16)
                    keep_hT(i + 1, 1 - u)
            hidden(E - 1, 1)
            keep_y(E - 2, 0, 16 * (E // 2 - 1))
            keep_hT(E - 1, 1)
            keep_y(E - 1, 1, 16 * (E // 2 - 1))
            n_over = dve.value_load(k.n_over[0:1, 0:1], min_val=0, max_val=OVER)
            with dve.Fori(0, OVER // SPAN) as span, dve.If(n_over > span * SPAN), dve.Fori(0, SPAN // 2) as pair:
                jj = span * (SPAN // 2) + pair
                for u in range(2):
                    j = jj * 2 + u
                    with dve.If(n_over > j):
                        keep_xT(j + E, u)
                        hidden(j + E, u)
                        keep_hT(j + E, u)
                        keep_y(j + E, u, jj * 16 + 16 * (E // 2))


def combine(nc, k):
    with ExitStack() as ctx:
        sb, ps, sem = makers(nc, ctx, "comb", k.held)
        g2 = sb("g2", [P, D], f32)
        b2 = sb("b2", [P, D], f32)
        NB = 12
        yb = sb("yb", [P, NB, D], f32)
        stats = sb("stats2", [P, 2, 6], f32)
        mv = sb("mv2", [P, 2, 2], f32)
        std = sb("std2", [P, 2], f32)
        rstd = sb("rstd2", [P, 1], f32)
        ln_in, own, var_done, std_done, out_done, out_sent = sem("ln2_in"), sem("c_own"), sem("var2"), sem("std2s"), sem("out_done"), sem("out_sent")
        y_in = [sem(f"y_in{b}") for b in range(NB)]
        y_used, y_pe, diag_done, summed = sem("y_used"), sem("y_pe"), sem("diag_done"), sem("summed")
        PE_K = 4
        diag = sb("diag", [P, 2, PE_K, P], f32)
        p_sum = ps("p_sum", [P, 2, D])
        block = ctx.enter_context(nc.Block())

        @block.sync
        def _(sp):
            sp.dma_start(g2[:, :], k.ln2_g.to_broadcast([P, D])).then_inc(ln_in, 16)
            sp.dma_start(b2[:, :], k.ln2_b.to_broadcast([P, D])).then_inc(ln_in, 16)
            out = k.out[0].rearrange("(c j) d -> j c d", j=T)
            for t in range(T):
                sp.wait_ge(out_done, t + 1)
                sp.dma_start(out[t], k.x[:, t, :]).then_inc(out_sent, 16)
            sp.wait_ge(out_sent, 16 * T)

        @block.gpsimd
        def _(pool):
            for n in range(T * TOP_K):
                if n >= NB:
                    t, q = (n - NB) // TOP_K, (n - NB) % TOP_K
                    if q < PE_K:
                        pool.wait_ge(y_pe, t * PE_K + q + 1)
                    else:
                        pool.wait_ge(y_used, t * (TOP_K - PE_K) + q - PE_K + 1)
                nc.gpsimd.indirect_dma_start(yb[:, n % NB, :], None, k.y_d[:, :],
                                             bass.IndirectOffsetOnAxis(ap=k.dest[:, n:n + 1], axis=0)).then_inc(y_in[n % NB], 16)

        @block.tensor
        def _(pe):
            for t in range(T):
                pe.wait_ge(diag_done, t + 1)
                if t >= 2:
                    pe.wait_ge(summed, t - 1)
                for q in range(PE_K):
                    n = t * TOP_K + q
                    pe.wait_ge(y_in[n % NB], 16 * (n // NB + 1))
                    for half in range(2):
                        cols = slice(half * 512, (half + 1) * 512)
                        last = nc.tensor.matmul(p_sum[:, t % 2, cols], diag[:, t % 2, q, :], yb[:, n % NB, cols],
                                                start=(q == 0), stop=(q == PE_K - 1))
                    last.then_inc(y_pe, 1)

        @block.scalar
        def _(act):
            def weigh(t):
                if t >= 2:
                    act.wait_ge(y_pe, (t - 1) * PE_K)
                for q in range(PE_K):
                    last = nc.scalar.activation(diag[:, t % 2, q, :], k.ident, ACT.Copy, scale=k.top_w[:, t, q:q + 1])
                last.then_inc(diag_done, 1)

            weigh(0)
            for t in range(T):
                if t + 1 < T:
                    weigh(t + 1)
                act.wait_ge(var_done, t + 1)
                nc.scalar.activation(std[:, t % 2:t % 2 + 1], mv[:, t % 2, 1:2], ACT.Sqrt).then_inc(std_done, 1)

        @block.vector
        def _(dve):
            ch = Chain(dve, own)
            for t in range(T):
                xt = k.x[:, t, :]
                for q in range(PE_K, TOP_K):
                    n = t * TOP_K + q
                    dve.wait_ge(y_in[n % NB], 16 * (n // NB + 1))
                    if t or q > PE_K:
                        dve.wait_ge(y_used, t * (TOP_K - PE_K) + q - PE_K)
                    nc.vector.scalar_tensor_tensor(xt, yb[:, n % NB, :], k.top_w[:, t, q:q + 1], xt, ALU.mult, ALU.add).then_inc(y_used, 1)
                dve.wait_ge(y_used, (t + 1) * (TOP_K - PE_K))
                dve.wait_ge(y_pe, (t + 1) * PE_K)
                nc.vector.tensor_tensor(xt, xt, p_sum[:, t % 2, :], ALU.add).then_inc(summed, 1)
                dve.wait_ge(summed, t + 1)
                nc.vector.bn_stats(stats[:, 0, :], k.x[:, t, 0:512])
                ch.link(nc.vector.bn_stats(stats[:, 1, :], k.x[:, t, 512:D]))
                ch.link(nc.vector.bn_aggr(mv[:, t % 2, :], stats[:, :, :].rearrange("p a b -> p (a b)")))
                nc.vector.tensor_scalar(mv[:, t % 2, 1:2], mv[:, t % 2, 1:2], LN_EPS, None, ALU.add).then_inc(var_done, 1)
                dve.wait_ge(std_done, t + 1)
                ch.link(nc.vector.reciprocal(rstd[:, :], std[:, t % 2:t % 2 + 1]))
                ch.link(nc.vector.tensor_scalar(xt, xt, mv[:, t % 2, 0:1], rstd[:, 0:1], ALU.subtract, ALU.mult))
                if t == 0:
                    dve.wait_ge(ln_in, 32)
                ch.link(nc.vector.tensor_tensor(xt, xt, g2[:, :], ALU.mult))
                nc.vector.tensor_tensor(xt, xt, b2[:, :], ALU.add).then_inc(out_done, 1)


def build(nc, k):
    with ExitStack() as ctx:
        k.held, k.late = [], []
        persistent(nc, ctx, k)
        shared = ctx.enter_context(ExitStack())
        with ExitStack() as mixers:
            with ExitStack() as states:
                sb, _, _ = makers(nc, states, "states", side="right")
                k.b1, k.b2, k.c1, k.c2, k.e1, k.f2 = [sb(n, [P, 2 * G, CH], f32) for n in ("b1", "b2", "c1", "c2", "e1", "f2")]
                k.pw = sb("pw", [P, 2, 2 * G, T + 1], f32)
                k.pb = sb("pb", [P, 2, 2 * G, T + 1], f32)
                k.t8 = sb("t8", [P, 2 * G], f32)
                k.m8 = sb("m8", [P, 2 * G], f32)
                with ExitStack() as latents:
                    sb, _, _ = makers(nc, latents, "latents", side="right")
                    k.cqT = sb("cqT", [P, 2, SEQ], f32)
                    k.ckvT = sb("ckvT", [P, SEQ], f32)
                    k.kT = sb("kT", [DQ, 2, SEQ], f32)
                    project(nc, k)
                    mixer_tile, _, _ = makers(nc, mixers, "mixers")
                    k.o = mixer_tile("o", [P, T, 512], f32)
                    attention(nc, k)
                s5_scan(nc, k)
            k.sT = mixer_tile("sT", [P, 4, SEQ], f32)
            sb, _, sem = makers(nc, shared, "shared", k.late, side="right")
            k.x1T = sb("x1T", [P, KD, SEQ], f32)
            k.ws_gu = sb("gu", [P, KD, 2 * F], f32)
            k.ws_dn = sb("dn", [P, KF, D], f32)
            k.s_hT = sb("hT", [P, KF, SEQ], f32)
            k.ws_in = sem("ws_in")
            with ExitStack() as mix_weights:
                sb, _, sem = makers(nc, mix_weights, "mix", k.late, side="right")
                k.mix_w = sb("w_o", [P, KD, D], f32)
                k.mix_w_in = sem("w_o_in")
                s5_gate(nc, k)
                hand_back(nc, k.held)
                mix_norm_route(nc, k)
        with ExitStack() as experts:
            sb, _, sem = makers(nc, experts, "ring", k.held)
            k.moe_gu = [sb(f"gu{e}", [P, KD, 2 * F], f32) for e in range(EARLY)]
            k.moe_dn = [sb(f"dn{e}", [P, KF, D], f32) for e in range(EARLY)]
            k.gu_in = [sem(f"gu_in{e}") for e in range(RING)]
            k.dn_in = [sem(f"dn_in{e}") for e in range(RING)]
            dispatch(nc, k)
            shared.close()
            moe_experts(nc, k)
        combine(nc, k)


_INS = ['x', 'w_in', 'lam_re', 'lam_im', 'log_dt', 'b_re', 'b_im', 'c_re', 'c_im', 'd_skip', 'w_glu', 'b_glu',
        'q_norm_g', 'w_uq', 'kv_norm_g', 'w_ukv', 'w_o', 'ln1_g', 'ln1_b', 'w_router', 'router_bias',
        'we_gate', 'we_up', 'we_down', 'ws_gate', 'ws_up', 'ws_down', 'ln2_g', 'ln2_b']


def kernel(**inputs):
    import numpy as _np
    import concourse.bacc as _bacc
    from concourse.bass_utils import run_bass_kernel_spmd as _run

    nc = _bacc.Bacc("TRN2", target_bir_lowering=False, num_devices=1)
    arrays, aps = {}, {}
    for name in _INS:
        a = _np.ascontiguousarray(inputs[name])
        arrays[f"in_{name}_dram"] = a
        aps[name] = nc.dram_tensor(f"in_{name}_dram", a.shape, mybir.dt.from_np(a.dtype), kind="ExternalInput").ap()
    c = constants()
    arrays["in_consts_dram"] = c
    aps["consts"] = nc.dram_tensor("in_consts_dram", c.shape, f32, kind="ExternalInput").ap()
    aps["out"] = nc.dram_tensor("out_0_dram", (1, SEQ, D), f32, kind="ExternalOutput").ap()
    build(nc, Kit(aps))
    r = _run(nc, [arrays], core_ids=[0])
    return r.results[0]["out_0_dram"]
```
